# Optimizing a Trainium2 kernel written in Bass

```python
import math
import jax, jax.numpy as jnp
from jax import lax
import numpy as np

D_MODEL = 1024
BATCH = 1
SEQ = 256
DEPTH = 2

N_A = DEPTH // 2
N_B = DEPTH - N_A
Q_BLOCK = 128
RMS_EPS = 1e-6

FOX_HEADS = 16
FOX_HEAD_DIM = D_MODEL // FOX_HEADS
FOX_WIDTH = FOX_HEADS * FOX_HEAD_DIM

MLA_HEADS = 16
MLA_NOPE = 64
MLA_ROPE = 32
MLA_V = 64
KV_RANK = 4 * MLA_V
Q_RANK = 12 * MLA_V
ROPE_THETA = 10000.0

D_FF = ((8 * D_MODEL // 3 + 255) // 256) * 256


def rmsnorm(x, g):
    xf = x.astype(jnp.float32)
    inv = lax.rsqrt(jnp.mean(xf * xf, axis=-1, keepdims=True) + RMS_EPS)
    return (xf * inv).astype(x.dtype) * g

def rope(x, positions):
    d = x.shape[-1]
    inv_freq = ROPE_THETA ** (-jnp.arange(0, d // 2, dtype=jnp.float32) * 2.0 / d)
    ang = positions.astype(jnp.float32)[..., None] * inv_freq
    cos = jnp.cos(ang)[:, :, None, :]
    sin = jnp.sin(ang)[:, :, None, :]
    xf = x.astype(jnp.float32)
    x1, x2 = xf[..., : d // 2], xf[..., d // 2:]
    out = jnp.concatenate([x1 * cos - x2 * sin, x1 * sin + x2 * cos], axis=-1)
    return out.astype(x.dtype)

def causal_block_attention(q, k, v, scale, log_f_cum=None):
    B, S, H, dq = q.shape
    nb = S // Q_BLOCK
    qb = q.reshape(B, nb, Q_BLOCK, H, dq).transpose(1, 0, 2, 3, 4)
    k_pos = jnp.arange(S)
    if log_f_cum is not None:
        cq_blocks = log_f_cum.reshape(B, nb, Q_BLOCK, H).transpose(1, 0, 2, 3)
        ck = log_f_cum.transpose(0, 2, 1)
    else:
        cq_blocks, ck = None, None

    def one_block(args):
        i, q_blk, cq = args
        s = jnp.einsum('bqhd,bkhd->bhqk', q_blk, k,
                       preferred_element_type=jnp.float32) * scale
        if cq is not None:
            s = s + (cq.transpose(0, 2, 1)[..., None] - ck[:, :, None, :])
        q_pos = i * Q_BLOCK + jnp.arange(Q_BLOCK)
        mask = k_pos[None, :] <= q_pos[:, None]
        s = jnp.where(mask[None, None], s, -jnp.inf)
        p = jax.nn.softmax(s, axis=-1)
        return jnp.einsum('bhqk,bkhd->bqhd', p.astype(v.dtype), v)

    out = lax.map(one_block, (jnp.arange(nb), qb, cq_blocks))
    return out.transpose(1, 0, 2, 3, 4).reshape(B, S, H, v.shape[-1])

def fox_attention(xn, w_in, b_f, w_o):
    B, S, _ = xn.shape
    proj = xn @ w_in
    q = proj[..., :FOX_WIDTH].reshape(B, S, FOX_HEADS, FOX_HEAD_DIM)
    k = proj[..., FOX_WIDTH:2 * FOX_WIDTH].reshape(B, S, FOX_HEADS, FOX_HEAD_DIM)
    v = proj[..., 2 * FOX_WIDTH:3 * FOX_WIDTH].reshape(B, S, FOX_HEADS, FOX_HEAD_DIM)
    f_logit = proj[..., 3 * FOX_WIDTH:] + b_f
    log_f = jax.nn.log_sigmoid(f_logit.astype(jnp.float32))
    cum = jnp.cumsum(log_f, axis=1)
    o = causal_block_attention(q, k, v, 1.0 / math.sqrt(FOX_HEAD_DIM), cum)
    return o.reshape(B, S, FOX_WIDTH) @ w_o

def mla_shared_kv(h, positions, kv_norm, w_kv_a, ckv_norm, w_uk, w_uv):
    B, S, _ = h.shape
    hn = rmsnorm(h, kv_norm)
    a = hn @ w_kv_a
    c_kv = rmsnorm(a[..., :KV_RANK], ckv_norm)
    k_rope = rope(a[..., KV_RANK:][:, :, None, :], positions)
    k_nope = jnp.einsum('bsr,rhd->bshd', c_kv, w_uk)
    v = jnp.einsum('bsr,rhd->bshd', c_kv, w_uv)
    k = jnp.concatenate(
        [k_nope, jnp.broadcast_to(k_rope, (B, S, MLA_HEADS, MLA_ROPE))], axis=-1)
    return k, v

def mla_attention(xn, positions, k, v, w_dq, cq_norm, w_uq, w_o):
    B, S, _ = xn.shape
    c_q = rmsnorm(xn @ w_dq, cq_norm)
    q = (c_q @ w_uq).reshape(B, S, MLA_HEADS, MLA_NOPE + MLA_ROPE)
    q = jnp.concatenate([q[..., :MLA_NOPE], rope(q[..., MLA_NOPE:], positions)], axis=-1)
    o = causal_block_attention(q, k, v, 1.0 / math.sqrt(MLA_NOPE + MLA_ROPE))
    return o.reshape(B, S, MLA_HEADS * MLA_V) @ w_o

def swiglu(xn, w_gate, w_up, w_down):
    return (jax.nn.silu(xn @ w_gate) * (xn @ w_up)) @ w_down

def first_inputs(seed: int = 0) -> dict:
    key = jax.random.key(seed)
    ks = jax.random.split(key, 24)

    def nrm(k, shape, fan_in):
        return jax.random.normal(k, shape, jnp.float32) * (fan_in ** -0.5)

    def gain(k, shape):
        return 1.0 + 0.02 * jax.random.normal(k, shape, jnp.float32)

    x = jax.random.normal(ks[0], (BATCH, SEQ, D_MODEL), jnp.float32)
    positions = jnp.broadcast_to(jnp.arange(SEQ, dtype=jnp.int32), (BATCH, SEQ))
    return {
        "x": x,
        "positions": positions,
        "attn_norm": gain(ks[1], (DEPTH, D_MODEL)),
        "ffn_norm": gain(ks[2], (DEPTH, D_MODEL)),
        "w_gate": nrm(ks[3], (DEPTH, D_MODEL, D_FF), D_MODEL),
        "w_up": nrm(ks[4], (DEPTH, D_MODEL, D_FF), D_MODEL),
        "w_down": nrm(ks[5], (DEPTH, D_FF, D_MODEL), D_FF),
        "fox_w_in": nrm(ks[6], (N_A, D_MODEL, 3 * FOX_WIDTH + FOX_HEADS), D_MODEL),
        "fox_b_f": 3.0 + 0.5 * jax.random.normal(ks[7], (N_A, FOX_HEADS), jnp.float32),
        "fox_w_o": nrm(ks[8], (N_A, FOX_WIDTH, D_MODEL), FOX_WIDTH),
        "kv_norm": gain(ks[9], (D_MODEL,)),
        "w_kv_a": nrm(ks[10], (D_MODEL, KV_RANK + MLA_ROPE), D_MODEL),
        "ckv_norm": gain(ks[11], (KV_RANK,)),
        "w_uk": nrm(ks[12], (KV_RANK, MLA_HEADS, MLA_NOPE), KV_RANK),
        "w_uv": nrm(ks[13], (KV_RANK, MLA_HEADS, MLA_V), KV_RANK),
        "mla_w_dq": nrm(ks[14], (N_B, D_MODEL, Q_RANK), D_MODEL),
        "cq_norm": gain(ks[15], (N_B, Q_RANK)),
        "mla_w_uq": nrm(ks[16], (N_B, Q_RANK, MLA_HEADS * (MLA_NOPE + MLA_ROPE)), Q_RANK),
        "mla_w_o": nrm(ks[17], (N_B, MLA_HEADS * MLA_V, D_MODEL), MLA_HEADS * MLA_V),
        "final_norm": gain(ks[18], (D_MODEL,)),
    }

def first_block(x, positions, attn_norm, ffn_norm, w_gate, w_up, w_down,
              fox_w_in, fox_b_f, fox_w_o, kv_norm, w_kv_a, ckv_norm, w_uk, w_uv,
              mla_w_dq, cq_norm, mla_w_uq, mla_w_o, final_norm):
    h = x
    k_shared, v_shared = None, None
    for l in range(DEPTH):
        if l == N_A:
            k_shared, v_shared = mla_shared_kv(h, positions, kv_norm, w_kv_a,
                                               ckv_norm, w_uk, w_uv)
        xn = rmsnorm(h, attn_norm[l])
        if l < N_A:
            h = h + fox_attention(xn, fox_w_in[l], fox_b_f[l], fox_w_o[l])
        else:
            j = l - N_A
            h = h + mla_attention(xn, positions, k_shared, v_shared,
                                  mla_w_dq[j], cq_norm[j], mla_w_uq[j], mla_w_o[j])
        h = h + swiglu(rmsnorm(h, ffn_norm[l]), w_gate[l], w_up[l], w_down[l])
    return rmsnorm(h, final_norm)


DEPTH_2 = 1

CHUNK = 64
N_MEM = 256
EPS = 1e-6
SB_HEADS = 8
SB_HEAD_DIM = 64
SB_WIDTH = SB_HEADS * SB_HEAD_DIM
SB_Q_BLOCK = 128
GDN_HEADS = 4
GDN_HEAD_DIM = 128
GDN_WIDTH = GDN_HEADS * GDN_HEAD_DIM
CONV_WIDTH = 4
X_HEADS = 4
X_HEAD_DIM = D_MODEL // X_HEADS
PEER_HEADS = 8
PEER_KEYS = 128
PEER_EXPERTS = PEER_KEYS * PEER_KEYS
PEER_TOPK = 16
PEER_QDIM = 256
PEER_TOKEN_BLOCK = 128
IN_SPLIT_SIZES = (SB_WIDTH, SB_WIDTH, SB_WIDTH, GDN_WIDTH, GDN_WIDTH, GDN_WIDTH, GDN_WIDTH,
                  GDN_HEADS, GDN_HEADS, D_MODEL, D_MODEL)
IN_COLS = 3 * SB_WIDTH + 4 * GDN_WIDTH + 2 * GDN_HEADS + 2 * D_MODEL


def rmsnorm_2(x, g):
    xf = x.astype(jnp.float32)
    y = xf * lax.rsqrt(jnp.mean(xf * xf, axis=-1, keepdims=True) + EPS)
    return (y * g.astype(jnp.float32)).astype(x.dtype)

def l2norm(x):
    xf = x.astype(jnp.float32)
    return xf * lax.rsqrt(jnp.sum(xf * xf, axis=-1, keepdims=True) + EPS)

def causal_dwconv(x, w):
    K = w.shape[0]
    S = x.shape[1]
    xp = jnp.pad(x, ((0, 0), (K - 1, 0), (0, 0)))
    return sum(xp[:, j:j + S] * w[j] for j in range(K))

def stick_breaking_attention(q, k, v):
    S, d = q.shape[2], q.shape[3]
    scale = d ** -0.5
    outs = []
    for i in range(S // SB_Q_BLOCK):
        q0 = i * SB_Q_BLOCK
        kv_len = q0 + SB_Q_BLOCK
        qb = q[:, :, q0:kv_len]
        kb = k[:, :, :kv_len]
        vb = v[:, :, :kv_len]
        z = jnp.einsum('bhqd,bhkd->bhqk', qb, kb).astype(jnp.float32) * scale
        qpos = q0 + jnp.arange(SB_Q_BLOCK)[:, None]
        kpos = jnp.arange(kv_len)[None, :]
        mask = kpos < qpos
        log_keep = jnp.where(mask, jax.nn.log_sigmoid(-z), 0.0)
        after = lax.cumsum(log_keep, axis=3, reverse=True) - log_keep
        a = jnp.where(mask, jnp.exp(jax.nn.log_sigmoid(z) + after), 0.0)
        outs.append(jnp.einsum('bhqk,bhkd->bhqd', a.astype(v.dtype), vb))
    return jnp.concatenate(outs, axis=2)

def gated_delta_rule(q, k, v, beta, g):
    B, S, H, dk = q.shape
    dv = v.shape[-1]
    N, C = S // CHUNK, CHUNK
    f32 = jnp.float32

    def chunk4(t):
        return jnp.moveaxis(t.astype(f32).reshape(B, N, C, H, t.shape[-1]), 3, 1)

    def chunk3(t):
        return jnp.moveaxis(t.astype(f32).reshape(B, N, C, H), 3, 1)

    q = chunk4(q) * (dk ** -0.5)
    k = chunk4(k)
    v = chunk4(v)
    beta = chunk3(beta)
    gc = jnp.cumsum(chunk3(g), axis=-1)
    idx = jnp.arange(C)
    incl = idx[:, None] >= idx[None, :]
    strict = idx[:, None] > idx[None, :]
    decay = jnp.exp(jnp.where(incl, gc[..., :, None] - gc[..., None, :], -jnp.inf))
    kb = k * beta[..., None]
    vb = v * beta[..., None]
    a = jnp.where(strict, jnp.einsum('bhncd,bhnmd->bhncm', kb, k) * decay, 0.0)
    eye = jnp.eye(C, dtype=f32)
    rhs = jnp.concatenate([vb, kb * jnp.exp(gc)[..., None]], axis=-1)
    sol = lax.linalg.triangular_solve(a + eye, rhs, left_side=True, lower=True, unit_diagonal=True)
    u = sol[..., :dv]
    w = sol[..., dv:]
    qk = jnp.einsum('bhncd,bhnmd->bhncm', q, k) * decay
    q_dec = q * jnp.exp(gc)[..., None]
    k_dec = k * jnp.exp(gc[..., -1:] - gc)[..., None]
    chunk_decay = jnp.exp(gc[..., -1])
    xs = tuple(jnp.moveaxis(t, 2, 0) for t in (q_dec, k_dec, u, w, qk, chunk_decay))

    def step(state, inp):
        qd, kd, u_n, w_n, qk_n, cd = inp
        v_new = u_n - jnp.einsum('bhcd,bhde->bhce', w_n, state)
        o = jnp.einsum('bhcd,bhde->bhce', qd, state) + jnp.einsum('bhcm,bhme->bhce', qk_n, v_new)
        state = state * cd[..., None, None] + jnp.einsum('bhcd,bhce->bhde', kd, v_new)
        return state, o

    state0 = jnp.zeros((B, H, dk, dv), f32)
    _, o = lax.scan(step, state0, xs)
    return jnp.transpose(o, (1, 0, 3, 2, 4)).reshape(B, S, H, dv)

def token_mixer(xn, w_in, gdn_conv, gdn_a_log, gdn_dt_bias, gdn_norm_g, w_sb_up, w_gdn_up, w_mix_out):
    B, S, _ = xn.shape
    proj = xn @ w_in
    offs = [int(o) for o in np.cumsum(IN_SPLIT_SIZES)[:-1]]
    (sb_q, sb_k, sb_v, g_q, g_k, g_v, g_z, g_b, g_a, gate_sb, gate_gdn) = jnp.split(proj, offs, axis=-1)

    def heads_sb(t):
        return t.reshape(B, S, SB_HEADS, SB_HEAD_DIM).transpose(0, 2, 1, 3)
    o_sb = stick_breaking_attention(heads_sb(sb_q), heads_sb(sb_k), heads_sb(sb_v))
    o_sb = o_sb.transpose(0, 2, 1, 3).reshape(B, S, SB_WIDTH)

    qkv = jax.nn.silu(causal_dwconv(jnp.concatenate([g_q, g_k, g_v], axis=-1), gdn_conv))
    cq, ck, cv = jnp.split(qkv, 3, axis=-1)
    cq = l2norm(cq.reshape(B, S, GDN_HEADS, GDN_HEAD_DIM))
    ck = l2norm(ck.reshape(B, S, GDN_HEADS, GDN_HEAD_DIM))
    cv = cv.reshape(B, S, GDN_HEADS, GDN_HEAD_DIM)
    beta = jax.nn.sigmoid(g_b.astype(jnp.float32))
    g = -jnp.exp(gdn_a_log.astype(jnp.float32)) * jax.nn.softplus(g_a.astype(jnp.float32) + gdn_dt_bias.astype(jnp.float32))
    o_g = gated_delta_rule(cq, ck, cv, beta, g).astype(xn.dtype)
    o_g = rmsnorm_2(o_g, gdn_norm_g) * jax.nn.silu(g_z.reshape(B, S, GDN_HEADS, GDN_HEAD_DIM))
    o_g = o_g.reshape(B, S, GDN_WIDTH)

    merged = jax.nn.sigmoid(gate_sb) * (o_sb @ w_sb_up) + jax.nn.sigmoid(gate_gdn) * (o_g @ w_gdn_up)
    return merged @ w_mix_out

def memory_cross_attention(hn, mn, w_cq, w_ckv, w_co):
    B, S, _ = hn.shape
    M = mn.shape[1]
    q = (hn @ w_cq).reshape(B, S, X_HEADS, X_HEAD_DIM)
    k, v = jnp.split(mn @ w_ckv, 2, axis=-1)
    k = k.reshape(B, M, X_HEADS, X_HEAD_DIM)
    v = v.reshape(B, M, X_HEADS, X_HEAD_DIM)
    s = jnp.einsum('bshd,bmhd->bhsm', q, k).astype(jnp.float32) * (X_HEAD_DIM ** -0.5)
    p = jax.nn.softmax(s, axis=-1).astype(v.dtype)
    o = jnp.einsum('bhsm,bmhd->bshd', p, v).reshape(B, S, D_MODEL)
    return o @ w_co

def peer(xn, w_pq, subkeys, peer_u, peer_v):
    B, S, D = xn.shape
    T = B * S
    xt = xn.reshape(T, D)
    q = (xt @ w_pq).reshape(T, PEER_HEADS, 2, PEER_QDIM // 2)
    s = jnp.einsum('thpd,hpnd->thpn', q, subkeys).astype(jnp.float32)
    top_s, top_i = lax.top_k(s, PEER_TOPK)
    cand_s = top_s[:, :, 0, :, None] + top_s[:, :, 1, None, :]
    cand_i = top_i[:, :, 0, :, None] * PEER_KEYS + top_i[:, :, 1, None, :]
    kk = PEER_TOPK * PEER_TOPK
    best_s, best_pos = lax.top_k(cand_s.reshape(T, PEER_HEADS, kk), PEER_TOPK)
    expert = jnp.take_along_axis(cand_i.reshape(T, PEER_HEADS, kk), best_pos, axis=-1)
    gate = jax.nn.softmax(best_s, axis=-1).astype(xn.dtype)
    nb = T // PEER_TOKEN_BLOCK

    def block(args):
        xb, eb, gb = args
        act = jax.nn.gelu(jnp.einsum('thkd,td->thk', peer_u[eb], xb), approximate=False) * gb
        return jnp.einsum('thk,thkd->td', act, peer_v[eb])

    out = lax.map(block, (xt.reshape(nb, PEER_TOKEN_BLOCK, D),
                          expert.reshape(nb, PEER_TOKEN_BLOCK, PEER_HEADS, PEER_TOPK),
                          gate.reshape(nb, PEER_TOKEN_BLOCK, PEER_HEADS, PEER_TOPK)))
    return out.reshape(B, S, D)

def second_inputs(seed: int = 0) -> dict:
    key = jax.random.key(seed)
    ks = jax.random.split(key, 24)
    f32 = jnp.float32

    def nrm(k, shape, scale):
        return jax.random.normal(k, shape, f32) * scale

    def gain(k, shape):
        return 1.0 + 0.02 * jax.random.normal(k, shape, f32)

    L, D = DEPTH_2, D_MODEL
    a_log = jnp.log(jax.random.uniform(ks[5], (L, GDN_HEADS), f32, 1.0, 16.0))
    dt = jnp.exp(jax.random.uniform(ks[6], (L, GDN_HEADS), f32, math.log(1e-3), math.log(1e-1)))
    dt_bias = dt + jnp.log(-jnp.expm1(-dt))
    return {
        "x": nrm(ks[0], (BATCH, SEQ, D), 1.0),
        "mem": nrm(ks[1], (BATCH, N_MEM, D), 1.0),
        "g_mix": gain(ks[2], (L, D)),
        "w_in": nrm(ks[3], (L, D, IN_COLS), D ** -0.5),
        "gdn_conv": nrm(ks[4], (L, CONV_WIDTH, 3 * GDN_WIDTH), CONV_WIDTH ** -0.5),
        "gdn_a_log": a_log,
        "gdn_dt_bias": dt_bias,
        "gdn_norm_g": gain(ks[7], (L, GDN_HEAD_DIM)),
        "w_sb_up": nrm(ks[8], (L, SB_WIDTH, D), SB_WIDTH ** -0.5),
        "w_gdn_up": nrm(ks[9], (L, GDN_WIDTH, D), GDN_WIDTH ** -0.5),
        "w_mix_out": nrm(ks[10], (L, D, D), D ** -0.5),
        "g_cross": gain(ks[11], (L, D)),
        "g_mem": gain(ks[12], (L, D)),
        "w_cq": nrm(ks[13], (L, D, D), D ** -0.5),
        "w_ckv": nrm(ks[14], (L, D, 2 * D), D ** -0.5),
        "w_co": nrm(ks[15], (L, D, D), D ** -0.5),
        "g_peer": gain(ks[16], (L, D)),
        "w_pq": nrm(ks[17], (L, D, PEER_HEADS * PEER_QDIM), D ** -0.5),
        "peer_subkeys": nrm(ks[18], (L, PEER_HEADS, 2, PEER_KEYS, PEER_QDIM // 2), (PEER_QDIM // 2) ** -0.5),
        "peer_u": nrm(ks[19], (L, PEER_EXPERTS, D), D ** -0.5),
        "peer_v": nrm(ks[20], (L, PEER_EXPERTS, D), PEER_HEADS ** -0.5),
        "g_final": gain(ks[21], (D,)),
    }

def second_block(x, mem, g_mix, w_in, gdn_conv, gdn_a_log, gdn_dt_bias, gdn_norm_g, w_sb_up, w_gdn_up,
              w_mix_out, g_cross, g_mem, w_cq, w_ckv, w_co, g_peer, w_pq, peer_subkeys, peer_u, peer_v,
              g_final):
    for l in range(DEPTH_2):
        x = x + token_mixer(rmsnorm_2(x, g_mix[l]), w_in[l], gdn_conv[l], gdn_a_log[l], gdn_dt_bias[l],
                            gdn_norm_g[l], w_sb_up[l], w_gdn_up[l], w_mix_out[l])
        x = x + memory_cross_attention(rmsnorm_2(x, g_cross[l]), rmsnorm_2(mem, g_mem[l]),
                                       w_cq[l], w_ckv[l], w_co[l])
        x = x + peer(rmsnorm_2(x, g_peer[l]), w_pq[l], peer_subkeys[l], peer_u[l], peer_v[l])
    return rmsnorm_2(x, g_final)


def setup_inputs(seed=0):
    out = dict(first_inputs(seed))
    for name, value in second_inputs(seed + 1).items():
        if name != "x":
            out[name + "_2"] = value
    return out


def reference(
    x, positions, attn_norm, ffn_norm, w_gate, w_up, w_down, fox_w_in, fox_b_f, fox_w_o,
    kv_norm, w_kv_a, ckv_norm, w_uk, w_uv, mla_w_dq, cq_norm, mla_w_uq, mla_w_o, final_norm,
    mem_2, g_mix_2, w_in_2, gdn_conv_2, gdn_a_log_2, gdn_dt_bias_2, gdn_norm_g_2, w_sb_up_2,
    w_gdn_up_2, w_mix_out_2, g_cross_2, g_mem_2, w_cq_2, w_ckv_2, w_co_2, g_peer_2, w_pq_2,
    peer_subkeys_2, peer_u_2, peer_v_2, g_final_2,
):
    x = first_block(
        x, positions, attn_norm, ffn_norm, w_gate, w_up, w_down, fox_w_in, fox_b_f, fox_w_o,
        kv_norm, w_kv_a, ckv_norm, w_uk, w_uv, mla_w_dq, cq_norm, mla_w_uq, mla_w_o, final_norm,
    )
    return second_block(
        x, mem_2, g_mix_2, w_in_2, gdn_conv_2, gdn_a_log_2, gdn_dt_bias_2, gdn_norm_g_2,
        w_sb_up_2, w_gdn_up_2, w_mix_out_2, g_cross_2, g_mem_2, w_cq_2, w_ckv_2, w_co_2,
        g_peer_2, w_pq_2, peer_subkeys_2, peer_u_2, peer_v_2, g_final_2,
    )


_drawn_inputs = setup_inputs


def setup_inputs(seed=0):
    import zlib

    import numpy as np

    out = dict(_drawn_inputs(seed))
    spreads = {}
    factors = {'kv_norm': 4.293,
     'ckv_norm': 3.917,
     'cq_norm': 5.163,
     'gdn_norm_g_2': 4.373,
     'g_cross_2': 6.994,
     'g_mem_2': 6.084,
     'g_final_2': 8.03,
     'g_peer_2': 8.0}
    for name, (base, spread) in spreads.items():
        noise = np.random.default_rng([zlib.crc32(name.encode()), seed]).standard_normal(out[name].shape)
        drawn = base * np.exp(spread * noise) if base else spread * noise
        out[name] = __import__('jax').numpy.asarray(drawn.astype(out[name].dtype))
    for name, factor in factors.items():
        out[name] = (out[name] * factor).astype(out[name].dtype)
    return out
```

```python
from contextlib import ExitStack, contextmanager

import numpy as np
import concourse.bass as bass
from concourse import mybir

F32, F32R, U32, I32 = mybir.dt.float32, mybir.dt.float32r, mybir.dt.uint32, mybir.dt.int32
ALU, ACT = mybir.AluOpType, mybir.ActivationFunctionType
AX = mybir.AxisListType.X
ds = bass.ds

P = 128
NT = 2
S = NT * P
D = 1024
KC = D // P
DFF = 2816
FB = DFF // P
EPS = 1e-6
NEG = -1e30
TWO_PI = 6.283185307179586
PAIRS = 8
KVR, QR, ROPE, NOPE = 256, 768, 32, 64
SBW, GH, XD = 512, 4, 256
TOPK, PH = 16, 8
PICKS = TOPK * PH
RING = 16
CONV = 4

MLA_SCALE = (NOPE + ROPE) ** -0.5
_C1 = 6.28125
_C2 = float((np.array([TWO_PI - _C1], np.float32).view(np.uint32) & np.uint32(0xFFFFF000)).view(np.float32)[0])
PI_PARTS = (_C1, _C2, TWO_PI - _C1 - _C2)

_COLS = {}
_at = 0
for _n, _w in [("ident", 128), ("ones", 128), ("upto", 128), ("from_", 128), ("blk_upto", 128), ("blk", 128),
               ("half0", 128), ("half1", 128), ("dmask", 128), ("causal", 256), ("sb_neg", 384), ("sb_keep", 384),
               ("lev", 6 * 128), ("levT", 6 * 128), ("rot", 96), ("inv_freq", 1), ("iota16", 16), ("zero", 128)]:
    _COLS[_n] = (_at, _w)
    _at += _w
NCONST = _at


def constant_table():
    c = np.zeros((P, NCONST), np.float32)

    def put(name, a):
        o, w = _COLS[name]
        c[:a.shape[0], o:o + w] = a.reshape(a.shape[0], -1)

    i, j = np.arange(P)[:, None], np.arange(P)[None, :]
    same = i // 64 == j // 64
    put("ident", np.eye(P))
    put("ones", np.ones((P, P)))
    put("upto", (i <= j) * 1.0)
    put("from_", (i >= j) * 1.0)
    put("blk_upto", ((i <= j) & same) * 1.0)
    put("blk", same * 1.0)
    put("half0", np.repeat((i < 64) * 1.0, P, 1))
    put("half1", np.repeat((i >= 64) * 1.0, P, 1))
    put("dmask", np.where((i >= j) & same, 0.0, NEG))
    put("causal", np.concatenate([np.zeros((P, P)), np.where(j <= i, 0.0, NEG)], 1))
    put("sb_neg", np.concatenate([np.where(i < j, 0.0, NEG), np.zeros((P, P)), np.where(i < j, 0.0, NEG)], 1))
    put("sb_keep", -np.concatenate([(i < j) * 1.0, np.ones((P, P)), (i < j) * 1.0], 1))
    lev = [((i // (2 * s) == j // (2 * s)) & (i // s > j // s)) * 1.0 for s in (1, 2, 4, 8, 16, 32)]
    put("lev", np.concatenate(lev, 1))
    put("levT", np.concatenate([a.T for a in lev], 1))
    rot = np.zeros((96, 96))
    for r in range(ROPE // 2):
        rot[NOPE + 16 + r, NOPE + r] = -1.0
        rot[NOPE + r, NOPE + 16 + r] = 1.0
    put("rot", rot)
    inv = np.float32(10000.0) ** (-np.arange(ROPE // 2, dtype=np.float32) * np.float32(2.0) / np.float32(ROPE))
    put("inv_freq", np.concatenate([np.zeros(NOPE), inv, inv])[:, None])
    put("iota16", np.repeat(np.arange(16)[None], P, 0))
    return c


class Tally:

    def __init__(self, eng, name, per_iter):
        self.eng, self.name, self.per_iter = eng, name, per_iter
        self.base, self.local, self.i, self.per = {}, {}, None, {}

    def add(self, sem, n=1):
        if self.i is None:
            self.base[sem] = self.base.get(sem, 0) + n
        else:
            self.local[sem] = self.local.get(sem, 0) + n

    def due(self, sem):
        fixed = self.base.get(sem, 0) + self.local.get(sem, 0)
        per = self.per.get(sem.name, 0) if self.i is not None else 0
        return self.i * per + fixed if per else fixed

    def next(self, sem, n=1):
        self.add(sem, n)
        return self.due(sem)

    @contextmanager
    def loop(self, label, n):
        key = f"{self.name}:{label}"
        self.per = self.per_iter.get(key, {})
        with self.eng.Fori(0, n) as i:
            self.i = i
            yield i
        found = {s.name: k for s, k in self.local.items()}
        self.per_iter[key] = found
        for s, k in self.local.items():
            self.base[s] = self.base.get(s, 0) + n * k
        self.local, self.i, self.per = {}, None, {}


def program(nc, a, out, per_iter):
    with ExitStack() as ctx:
        def sb(name, shape, dt=F32):
            return ctx.enter_context(nc.sbuf_tensor(name, shape, dt))

        sems = {}

        def sem(name):
            if name not in sems:
                sems[name] = ctx.enter_context(nc.semaphore(name))
            return sems[name]

        ctx.enter_context(nc.allow_non_contiguous_dma(reason="small columns and weight blocks"))
        arena_at = -(-nc.sbuf_base // 32) * 32
        AR = sb("AR", [P, 18200])
        ARH = nc.alloc_sbuf_tensor_at("ARH", [P, 17408], F32R, offset=arena_at)
        ps = ctx.enter_context(nc.psum_tensor("ps", [P, 8, 512], F32))
        CT = sb("CT", [P, NCONST])
        SLOT = [sb(f"SLOT{s}", [P, 4096]) for s in range(4)]
        H = sb("H", [P, NT, D])
        XS = sb("XS", [P, NT, D])
        XT = sb("XT", [P, KC, S])
        XT2 = sb("XT2", [P, KC, S])
        V = sb("V", [P, NT, D])
        OT = sb("OT", [P, KC, S])
        ROWG = sb("ROWG", [P, D])
        GCOL = sb("GCOL", [P, P])
        WF = sb("WF", [P, KC, 16])
        SS = sb("SS", [P, 16])
        RS = sb("RS", [P, 16])
        BF = sb("BF", [P, 16])
        SM = sb("SM", [P, 64])

        def const(name, rows=P):
            o, w = _COLS[name]
            return CT[0:rows, o:o + w]

        IDENT = const("ident")

        def arena(off, *shape, parts=P):
            n = int(np.prod(shape))
            v = AR[0:parts, off:off + n]
            assert off + n <= 18200, (off, n)
            if len(shape) == 1:
                return v
            names = "abcde"[:len(shape)]
            return v.rearrange(f"p ({' '.join(names)}) -> p {' '.join(names)}", **{m: k for m, k in zip(names, shape)})

        def halves(off, *shape):
            return view(ARH[:, off:off + int(np.prod(shape))], *shape)

        def view(x, *shape):
            names = "abcde"[:len(shape)]
            return x.rearrange(f"p ({' '.join(names)}) -> p {' '.join(names)}", **{m: k for m, k in zip(names, shape)})

        QT = arena(0, 2, S)
        KT = arena(512, 2, S)
        LG = arena(1024, 2, 512)
        PR = arena(2048, 2, 512)
        PT = arena(3072, 2, 512)
        ON = arena(4096, 2, 128)
        NEGCUM = arena(4608, 4096, parts=1)
        LF = arena(8704, NT, 16)
        LF2 = arena(8736, NT, 16)
        CQ = arena(8768, NT, 16)
        CUMT = arena(8800, S, parts=16)
        QRAW = arena(9056, 2, S)
        COS = arena(9568, 2, S)
        SIN = arena(10080, 2, S)
        WPAD = arena(10592, KC, 96)
        KVA = arena(11360, NT, 768)
        CKT = arena(12896, 2, S)
        CQT = arena(13408, 6, S)
        KRT = arena(14944, S)
        ANG = arena(15200, 4, S)
        SG = arena(17408, 2, S)
        WGU = halves(0, 2, 2, 2, KC, P)
        WDN = halves(8192, 2, 2, D)
        XH = halves(12288, 2, KC, S)
        HT = halves(16384, 2, 2, S)
        PRE = arena(0, 12, S + CONV - 1)
        G = arena(3108, 12, S)
        SQ = arena(6180, 8, S)
        KBG, VB = arena(0, NT, 512), arena(1024, NT, 512)
        KD = arena(6180, NT, 512)
        DEC = arena(8228, NT, 512)
        AA, AT = arena(9252, NT, 512), arena(10276, NT, 512)
        TI_, UI = arena(11300, NT, 512), arena(12324, NT, 512)
        LT, PP = arena(13348, NT, 512), arena(14372, NT, 512)
        ER, QK = LT, PP
        QKT = arena(2048, NT, 512)
        QD = arena(15396, NT, 512)
        WT = arena(16420, NT, 512)
        UU = arena(7204, NT, 512)
        ST = arena(17444, 512)
        VN, OI = XT2[:, 0:4, :].rearrange("p a b -> p (a b)").rearrange("p (t n) -> p t n", t=NT), XS[:, :, 0:512]
        GT, MG = arena(0, NT, 2 * D), arena(4096, NT, D)
        MEM = arena(8192, NT, D)
        ONX = arena(4096, NT, XD)
        QP, SKT = arena(0, 2, S), arena(512, 2, P)
        SC, SCR = arena(768, NT, 2, P), arena(1280, NT, 2, P)
        TV, TIF = arena(1792, NT, 2, 16), arena(1920, NT, 2, 16)
        CAND, CANDR = arena(1984, NT, 256), arena(2496, NT, 256)
        BV, PAF, PBF = arena(3008, NT, 16), arena(3104, NT, 16), arena(3136, NT, 16)
        OH = arena(3300, NT, 256)
        DOT, AV = arena(5024, NT, TOPK), arena(5280, NT, PICKS)
        GS = arena(5536, NT * PH)
        GX, AX_, BSX = arena(4000, NT, TOPK), arena(4032, NT, TOPK), arena(4064, NT, TOPK)
        SUBK = arena(10000, 2, P)
        PW = view(XT2[:].rearrange("p a b -> p (a b)"), 2, KC, P)
        DIAG = arena(7700, RING, P)
        TIX, BP, PA, PB = (sb(n_, s_, U32) for n_, s_ in (("TIX", [P, NT, 2, 16]), ("BP", [P, NT, 16]), ("PA", [P, NT, 16]), ("PB", [P, NT, 16])))
        EXU, IX = sb("EXU", [P, NT, PICKS], U32), sb("IX", [P, RING], U32)
        BA, BT, BE = sb("BA", [P, NT, 8]), sb("BT", [P, NT, 4]), sb("BE", [P, NT, 4])
        SMALL = sb("SMALL", [P, 128])
        GSM, AEXP, GDNG = SMALL[:, 0:8], SMALL[:, 8:12], SMALL[:, 12:13]
        GZ, GL, GG = (view(SMALL[:, 16 + 8 * n_:24 + 8 * n_], NT, 4) for n_ in range(3))
        RAW, EX = SMALL[:, 40:72], SMALL[:, 72:104]
        PSCR = sb("PSCR", [P, 16])
        ASCR = sb("ASCR", [P, 64])
        POSI = sb("POSI", [P, S], I32)

        full = {r: [sem(f"full_{r}{b}") for b in range(8)] for r in "va"}
        free = {r: [sem(f"free_{r}{b}") for b in range(8)] for r in "va"}
        here = [sem(f"slot_here{s}") for s in range(4)]
        used = [sem(f"slot_used{s}") for s in range(4)]

        raw_here = [sem(f"raw_here{s}") for s in range(4)]
        ring_used = [sem(f"ring_used{j}") for j in range(RING)]
        gathered = [sem(f"gathered{j}") for j in range(RING)]

        def inner(x, n):
            shape = list(x.shape)
            names = "abc"[:len(shape) - 1]
            lhs = " ".join(names[:-1]) + f" ({names[-1]} o)"
            return x.rearrange(f"p {lhs} -> p {' '.join(names)} o", o=1).to_broadcast(shape + [n])

        def outer(x, n):
            return x.rearrange("p (o m) -> p o m", o=1).to_broadcast([x.shape[0], n, x.shape[1]])

        def hd(X, t, h):
            return X[:, t, h * P:(h + 1) * P]

        def ring(j):
            return SLOT[j // 4][:, (j % 4) * D:(j % 4 + 1) * D]

        g_at = dict(attn0=0, attn1=8, ffn0=16, ffn1=24, kv=32, ckv=40, cq=42, mix=48, cross=56, mem=64, peer=72, conv=80)

        def gcol(name, k, n):
            o = g_at[name] + k
            return GCOL[:, o:o + n]

        def rows(w, c0, c1):
            return w[:, c0:c1].rearrange("(k p) n -> p k n", p=P)

        x_in, mem_in = a["x"][0].rearrange("(t p) d -> p t d", p=P), a["mem_2"][0].rearrange("(t p) d -> p t d", p=P)
        fw = a["fox_w_in"][0]
        w_in = a["w_in_2"][0]
        w_uk = a["w_uk"].rearrange("(k p) h d -> p k (h d)", p=P)
        w_uv = a["w_uv"].rearrange("(k p) h d -> p k (h d)", p=P)
        w_uq = a["mla_w_uq"][0]
        w_dq = a["mla_w_dq"][0].rearrange("(k p) n -> p k n", p=P)
        subkeys = a["peer_subkeys_2"][0].rearrange("h q n d -> n (h q) d")

        def flat_rows(x):
            while len(x.shape) > 1:
                x = x.rearrange("a b -> (a b)") if len(x.shape) == 2 else x.rearrange("a b c -> (a b c)")
            return x.rearrange("(r c) -> r c", c=P)

        GAINS = [(n_, flat_rows(a[src])) for n_, src in (
            ("attn0", "attn_norm"), ("ffn0", "ffn_norm"), ("kv", "kv_norm"), ("ckv", "ckv_norm"), ("cq", "cq_norm"), ("mix", "g_mix_2"),
            ("cross", "g_cross_2"), ("mem", "g_mem_2"), ("peer", "g_peer_2"), ("conv", "gdn_conv_2"))]

        block = ctx.enter_context(nc.Block())

        @block.sync
        def _(sp):
            T = Tally(sp, "sp", per_iter)

            def fill(s, *pairs, arrival=here):
                sp.wait_ge(used[s], T.due(used[s]))
                for dst, src in pairs:
                    sp.dma_start(dst, src).then_inc(arrival[s], 16)
                T.add(used[s])

            def slot(s, *shape):
                return view(SLOT[s][:, 0:int(np.prod(shape))], *shape)

            def row_gain(src):
                sp.wait_ge(sem("rowg_used"), T.due(sem("rowg_used")))
                sp.dma_start(ROWG[:], src.to_broadcast([P, D])).then_inc(sem("rowg_here"), 16)
                T.add(sem("rowg_used"))

            def qk(q_src, k_src):
                fill(0, (slot(0, q_src.shape[1], q_src.shape[2]), q_src))
                fill(1, (slot(1, k_src.shape[1], k_src.shape[2]), k_src))

            def dyn(w, off, n=P):
                return w[:, ds(off, n)].rearrange("(k p) n -> p k n", p=P)

            def two_tiles(w, c0=0):
                for c in range(2):
                    fill(2 + c, (slot(2 + c, KC, 512), rows(w, c0 + 512 * c, c0 + 512 * c + 512)))

            def ffn(l):
                wg, wu, wd = a["w_gate"][l], a["w_up"][l], a["w_down"][l]
                with T.loop(f"ffn{l}", FB // 2) as i:
                    for b in range(2):
                        w = slot(b, 2, KC, P)
                        fill(b, (w[:, 0], dyn(wg, i * 256 + b * P)), (w[:, 1], dyn(wu, i * 256 + b * P)), arrival=raw_here)
                    for b in range(2):
                        fill(2 + b, (SLOT[2 + b][:, 0:D], wd[ds(i * 256 + b * P, P), :]), arrival=raw_here)

            sp.dma_start(H[:], x_in).then_inc(sem("x_here"), 16)
            sp.dma_start(CT[:], a["consts"]).then_inc(sem("const_here"), 16)
            for name, src in GAINS:
                r0 = g_at[name]
                sp.dma_start(SLOT[0][r0:r0 + src.shape[0], 0:P], src).then_inc(here[0], 16)
            T.add(used[0])
            sp.dma_start(WF[:], rows(fw, 3072, 3088)).then_inc(sem("wf_here"), 16)
            sp.dma_start(BF[:], a["fox_b_f"].to_broadcast([P, 16])).then_inc(sem("wf_here"), 16)
            two_tiles(fw, 2048)
            sp.wait_ge(sem("cumt_ready"), 1)
            sp.dma_start(NEGCUM[0:1, :], CUMT).then_inc(sem("negcum_here"), 16)
            qk(rows(fw, 0, P), rows(fw, D, D + P))
            with T.loop("fox", PAIRS - 1) as i:
                qk(dyn(fw, i * P + P), dyn(fw, i * P + (D + P)))
            two_tiles(a["fox_w_o"][0])
            ffn(0)
            fill(0, (slot(0, KC, 288), rows(a["w_kv_a"], 0, 288)))
            sp.dma_start(POSI[0:96, :], a["positions"].to_broadcast([96, S])).then_inc(sem("pos_here"), 16)
            fill(1, (slot(1, 4, QR), w_dq[:, 0:4, :]))
            fill(2, (slot(2, 4, QR), w_dq[:, 4:8, :]))
            fill(3, (slot(3, 2, D), w_uv))
            qk(rows(w_uq, 0, 192), w_uk[:, :, 0:P])
            with T.loop("mla", PAIRS - 1) as i:
                qk(dyn(w_uq, i * 192 + 192, 192), w_uk[:, :, ds(i * P + P, P)])
            two_tiles(a["mla_w_o"][0])
            ffn(1)
            row_gain(a["final_norm"].rearrange("(o d) -> o d", o=1))
            fill(2, (slot(2, KC, 512), rows(w_in, 1024, 1536)))
            qk(rows(w_in, 0, P), rows(w_in, SBW, SBW + P))
            with T.loop("sb", 3) as i:
                qk(dyn(w_in, i * P + P), dyn(w_in, i * P + (SBW + P)))
            for n_, s_ in enumerate((3, 2, 3)):
                fill(s_, (slot(s_, KC, 512), rows(w_in, 1536 + 512 * n_, 2048 + 512 * n_)))
            fill(2, (slot(2, KC, 512), rows(w_in, 3072, 3584)))
            sp.wait_ge(used[0], T.due(used[0]))
            fill(0, (slot(0, KC, 8), rows(w_in, 3584, 3592)))
            for k_, name in enumerate(("gdn_a_log_2", "gdn_dt_bias_2")):
                sp.dma_start(GSM[:, 4 * k_:4 * k_ + 4], a[name].to_broadcast([P, 4])).then_inc(sem("gsm_here"), 16)
            sp.dma_start(GDNG, a["gdn_norm_g_2"].rearrange("o d -> d o")).then_inc(sem("gsm_here"), 16)
            for n_, s_ in enumerate((3, 2, 3, 2)):
                fill(s_, (slot(s_, KC, 512), rows(w_in, 3592 + 512 * n_, 4104 + 512 * n_)))
            fill(0, (slot(0, 4, D), a["w_sb_up_2"][0].rearrange("(k p) n -> p k n", p=P)))
            fill(1, (slot(1, 4, D), a["w_gdn_up_2"][0].rearrange("(k p) n -> p k n", p=P)))
            two_tiles(a["w_mix_out_2"][0])
            wckv, wcq = a["w_ckv_2"][0], a["w_cq_2"][0]
            sp.wait_ge(sem("mix_done"), 1)
            sp.dma_start(MEM, mem_in).then_inc(sem("mem_here"), 16)
            two_tiles(wckv, D)
            qk(rows(wcq, 0, XD), rows(wckv, 0, XD))
            with T.loop("cross", 3) as i:
                qk(dyn(wcq, i * XD + XD, XD), dyn(wckv, i * XD + XD, XD))
            two_tiles(a["w_co_2"][0])
            row_gain(a["g_peer_2"])
            def head_weights(h):
                wq = a["w_pq_2"][0]
                fill(0, *((PW[:, q], dyn(wq, h * 256 + q * P)) for q in range(2)))
                fill(1, (SUBK[:], subkeys[:, ds(h * 2, 2), :]))

            sp.wait_ge(used[1], T.due(used[1]))
            head_weights(0)
            with T.loop("route", PH - 1) as i:
                head_weights(i + 1)
            row_gain(a["g_final_2"].rearrange("(o d) -> o d", o=1))
            sp.wait_ge(sem("result"), 1)
            sp.dma_start(out[0].rearrange("(t p) d -> p t d", p=P), XS[:]).then_inc(sem("out_done"), 16)
            sp.wait_ge(sem("out_done"), 16)

        @block.tensor
        def _(pe):
            T = Tally(pe, "pe", per_iter)
            pending = []

            def first(ins):
                if pending:
                    ins.then_inc(pending.pop(0), 1)

            def take(*banks):
                for b in banks:
                    pe.wait_ge(free["v"][b], T.due(free["v"][b]))
                    pe.wait_ge(free["a"][b], T.due(free["a"][b]))

            evacuated = take

            def release(s):
                pending.append(used[s])

            def flush():
                for _ in range(len(pending)):
                    take(7)
                    first(pe.matmul(ps[:, 7, 0:1], const("zero"), CT[:, 0:1], start=True, stop=True))

            def group(outp, pairs):
                pairs = list(pairs)
                for n_, (l, r) in enumerate(pairs):
                    m = pe.matmul(outp, l, r, start=(n_ == 0), stop=(n_ == len(pairs) - 1))
                    if n_ < len(pairs) - 1:
                        first(m)
                return m

            def tr(outp, src):
                return pe.transpose(outp, src, IDENT)

            def slot(s, *shape):
                return view(SLOT[s][:, 0:int(np.prod(shape))], *shape)

            def transposes(src, n_chunks, banks=(0, 1, 2, 3)):
                for g in range(n_chunks // 2):
                    b = banks[g % len(banks)]
                    take(b)
                    for n_ in range(4):
                        m = tr(ps[:, b, n_ * P:(n_ + 1) * P], src(n_ % 2, 2 * g + n_ // 2))
                        if n_ < 3:
                            first(m)
                    m.then_inc(full["v"][b], 1)
                    T.add(free["v"][b])

            def norm_t():
                pe.wait_ge(sem("xs_ready"), T.next(sem("xs_ready")))
                transposes(lambda t, k: XS[:, t, k * P:(k + 1) * P], KC)
                evacuated(0, 1, 2, 3)

            def cols(X, t, k):
                return X[:, k, t * P:(t + 1) * P]

            def row_tile(s, banks, X, n=512, reader="v"):
                pe.wait_ge(here[s], T.next(here[s], 16))
                w = slot(s, KC, n)
                for t in range(NT):
                    take(banks[t])
                    group(ps[:, banks[t], 0:n], ((cols(X, t, k), w[:, k, :]) for k in range(KC))).then_inc(full[reader][banks[t]], 1)
                    T.add(free[reader][banks[t]])
                release(s)

            def out_proj(X, bank):
                evacuated(bank)
                for c in range(2):
                    row_tile(2 + c, (2 * c, 2 * c + 1), X)

            def qk_proj():
                take(0)
                for s_ in range(2):
                    pe.wait_ge(here[s_], T.next(here[s_], 16))
                    m = group(ps[:, 0, s_ * S:(s_ + 1) * S], ((slot(s_, KC, P)[:, k, :], XT[:, k, :]) for k in range(KC)))
                    release(s_)
                m.then_inc(full["a"][0], 1)
                T.add(free["a"][0])

            def attend_tail(i):
                for hh in range(2):
                    pe.wait_ge(sem("probs_ready"), T.next(sem("probs_ready")))
                    take(3)
                    for n_ in range(3):
                        m = tr(ps[:, 3, n_ * P:(n_ + 1) * P], PR[:, hh, n_ * P:(n_ + 1) * P])
                        if n_ < 2:
                            first(m)
                    m.then_inc(full["a"][3], 1)
                    T.add(free["a"][3])
                evacuated(3)
                take(4)
                for hh in range(2):
                    v0, v1 = (V[:, kt, ds((i * 2 + hh) * 64, 64)] for kt in range(2))
                    group(ps[:, 4, hh * 64:hh * 64 + 64], [(PT[:, hh, 0:P], v0)])
                    m = group(ps[:, 4, P + hh * 64:P + hh * 64 + 64], [(PT[:, hh, P:2 * P], v0), (PT[:, hh, 2 * P:3 * P], v1)])
                m.then_inc(full["v"][4], 1)
                T.add(free["v"][4])
                evacuated(4)
                take(5)
                for t in range(NT):
                    m = tr(ps[:, 5, t * P:(t + 1) * P], ON[:, t, :])
                m.then_inc(full["a"][5], 1)
                T.add(free["a"][5])

            def thirds(l, r):
                return [(l(0), r(0)), (l(0), r(1)), (l(1), r(0))]

            def ffn(l):
                norm_t()
                pe.wait_ge(sem("xh_ready"), T.next(sem("xh_ready")))
                for b in range(4):
                    take(b)
                    first(pe.matmul(ps[:, b, :], const("zero"), XT[:, 0:2, :], start=True, stop=False))
                assert not pending
                with T.loop(f"ffn{l}", FB // 2) as i:
                    for b in range(2):
                        pe.wait_ge(sem(f"gu_split{b}"), T.next(sem(f"gu_split{b}")))
                        take(4 + b)
                        for g in range(2):
                            m = group(ps[:, 4 + b, g * S:(g + 1) * S],
                                      sum((thirds(lambda h: WGU[:, b, h, g, k, :], lambda h: XH[:, h, k, :]) for k in range(KC)), []))
                        m.then_inc(full["a"][4 + b], 1)
                        T.add(free["v"][4 + b])
                    for b in range(2):
                        pe.wait_ge(sem(f"dn_split{b}"), T.next(sem(f"dn_split{b}")))
                        evacuated(4 + b)
                        for t in range(NT):
                            for c in range(2):
                                for l_, r_ in thirds(lambda h: HT[:, b, h, t * P:(t + 1) * P], lambda h: WDN[:, b, h, c * 512:(c + 1) * 512]):
                                    m = pe.matmul(ps[:, 2 * t + c, :], l_, r_, start=False, stop=False)
                        m.then_inc(sem(f"dn_used{b}"), 1)
                for b in range(4):
                    pe.matmul(ps[:, b, :], const("zero"), XT[:, 0:2, :], start=False, stop=True).then_inc(full["v"][b], 1)
                    T.add(free["v"][b])

            pe.wait_ge(sem("const_here"), T.next(sem("const_here"), 16))
            T.add(free["a"][3])
            T.add(free["a"][5])
            pe.wait_ge(here[0], T.next(here[0], 16 * len(GAINS)))
            take(0)
            tr(ps[:, 0, 0:P], SLOT[0][:, 0:P]).then_inc(full["v"][0], 1)
            T.add(free["v"][0])
            release(0)
            norm_t()
            pe.wait_ge(sem("wf_here"), T.next(sem("wf_here"), 32))
            take(4)
            for t in range(NT):
                m = group(ps[:, 4, 16 * t:16 * t + 16], ((cols(XT, t, k), WF[:, k, :]) for k in range(KC)))
            m.then_inc(full["v"][4], 1)
            T.add(free["v"][4])
            for c in range(2):
                row_tile(2 + c, (2 * c, 2 * c + 1), XT)
            pe.wait_ge(sem("logf_ready"), T.next(sem("logf_ready")))
            take(4)
            group(ps[:, 4, 0:16], [(const("upto"), LF[:, 0, :])])
            m = group(ps[:, 4, 16:32], [(const("upto"), LF[:, 1, :]), (const("ones"), LF[:, 0, :])])
            m.then_inc(full["v"][4], 1)
            T.add(free["v"][4])
            evacuated(4)
            take(5)
            for t in range(NT):
                m = tr(ps[0:16, 5, t * P:(t + 1) * P], CQ[:, t, :])
            m.then_inc(full["v"][5], 1)
            T.add(free["v"][5])
            evacuated(2, 3)

            def fox_scores(i):
                evacuated(0)
                one = const("ones")[0:1, :]
                for hh in range(2):
                    take(1 + hh)
                    r = slice(64 * hh, 64 * hh + 64)
                    for c0, q, n in ((0, 0, P), (P, P, S)):
                        first(pe.matmul(ps[:, 1 + hh, c0:c0 + n], one, NEGCUM[0:1, ds((i * 2 + hh) * S, n)], start=True, stop=False))
                        m = pe.matmul(ps[:, 1 + hh, c0:c0 + n], QT[r, 0, q:q + P], KT[r, 0, 0:n], start=False, stop=True)
                    m.then_inc(full["v"][1 + hh], 1)
                    T.add(free["v"][1 + hh])

            qk_proj()
            pe.wait_ge(sem("negcum_here"), T.next(sem("negcum_here"), 16))
            flush()
            assert not pending
            with T.loop("fox", PAIRS - 1) as i:
                fox_scores(i)
                qk_proj()
                attend_tail(i)
                assert not pending
            fox_scores(PAIRS - 1)
            attend_tail(PAIRS - 1)
            out_proj(OT, 5)
            ffn(0)
            norm_t()
            pe.wait_ge(sem("wpad_here"), T.next(sem("wpad_here"), 17))
            take(4)
            group(ps[0:96, 4, 0:S], ((WPAD[:, k, :], XT2[:, k, :]) for k in range(KC))).then_inc(full["a"][4], 1)
            T.add(free["a"][4])
            pe.wait_ge(here[0], T.next(here[0], 16))
            for t in range(NT):
                take(t)
                group(ps[:, t, 0:KVR], ((cols(XT2, t, k), slot(0, KC, 288)[:, k, 0:KVR]) for k in range(KC))).then_inc(full["a"][t], 1)
                T.add(free["a"][t])
            release(0)
            pe.wait_ge(here[1], T.next(here[1], 16))
            pe.wait_ge(here[2], T.next(here[2], 16))
            for t in range(NT):
                for c in range(2):
                    b = (2, 3, 6, 7)[2 * t + c]
                    take(b)
                    group(ps[:, b, 0:384], ((cols(XT, t, k), slot(1 + k // 4, 4, QR)[:, k % 4, 384 * c:384 * c + 384])
                                                 for k in range(KC))).then_inc(full["a"][b], 1)
                    T.add(free["a"][b])
            release(1)
            release(2)
            evacuated(4)
            take(5)
            pe.matmul(ps[0:96, 5, 0:S], const("rot", 96), KRT[0:96, :], start=True, stop=True).then_inc(full["v"][5], 1)
            T.add(free["v"][5])
            pe.wait_ge(sem("xs_ready"), T.next(sem("xs_ready")))
            transposes(lambda t, k: XS[:, t, k * P:(k + 1) * P], 2)
            evacuated(0)
            pe.wait_ge(here[3], T.next(here[3], 16))
            for c in range(2):
                for t in range(NT):
                    b = (4, 5)[t]
                    take(b)
                    group(ps[:, b, :], ((cols(CKT, t, k), slot(3, 2, D)[:, k, 512 * c:512 * c + 512]) for k in range(2))).then_inc(full["v"][b], 1)
                    T.add(free["v"][b])
            release(3)
            pe.wait_ge(sem("xs_ready"), T.next(sem("xs_ready")))
            transposes(lambda t, k: XS[:, t, k * P:(k + 1) * P], 6, (0, 1, 2))
            evacuated(0, 1, 2, 4, 5)

            def mla_proj():
                pe.wait_ge(here[0], T.next(here[0], 16))
                take(0)
                for hh in range(2):
                    m = group(ps[0:96, 0, hh * S:(hh + 1) * S], ((slot(0, 6, 192)[:, k, 96 * hh:96 * hh + 96], CQT[:, k, :]) for k in range(6)))
                release(0)
                m.then_inc(full["a"][0], 1)
                T.add(free["a"][0])
                pe.wait_ge(here[1], T.next(here[1], 16))
                take(6)
                for hh in range(2):
                    m = group(ps[0:64, 6, hh * S:(hh + 1) * S], ((slot(1, 2, P)[:, k, 64 * hh:64 * hh + 64], CKT[:, k, :]) for k in range(2)))
                release(1)
                m.then_inc(full["a"][6], 1)
                T.add(free["a"][6])
                take(7)
                evacuated(0)
                first(pe.matmul(ps[0:96, 7, 0:S], const("rot", 96), QRAW[0:96, 0, :], start=True, stop=True))
                pe.matmul(ps[0:96, 7, S:2 * S], const("rot", 96), QRAW[0:96, 1, :], start=True, stop=True).then_inc(full["v"][7], 1)
                T.add(free["v"][7])

            def mla_scores(i):
                evacuated(6, 7)
                for hh in range(2):
                    take(1 + hh)
                    pe.matmul(ps[:, 1 + hh, 0:P], QT[0:96, hh, 0:P], KT[0:96, hh, 0:P], start=True, stop=True)
                    pe.matmul(ps[:, 1 + hh, P:3 * P], QT[0:96, hh, P:S], KT[0:96, hh, :], start=True, stop=True).then_inc(full["v"][1 + hh], 1)
                    T.add(free["v"][1 + hh])

            pe.wait_ge(sem("krope_ready"), T.next(sem("krope_ready")))
            mla_proj()
            assert not pending
            with T.loop("mla", PAIRS - 1) as i:
                mla_scores(i)
                mla_proj()
                attend_tail(i)
                assert not pending
            mla_scores(PAIRS - 1)
            attend_tail(PAIRS - 1)
            out_proj(OT, 5)
            ffn(1)
            norm_t()
            row_tile(2, (6, 7), XT)

            def sb_scores(i):
                evacuated(0)
                for hh in range(2):
                    take(1 + hh)
                    r = slice(64 * hh, 64 * hh + 64)
                    first(pe.matmul(ps[:, 1 + hh, 0:S], KT[r, 0, 0:P], QT[r, 0, :], start=True, stop=True))
                    pe.matmul(ps[:, 1 + hh, S:3 * P], KT[r, 0, P:S], QT[r, 0, P:S], start=True, stop=True).then_inc(full["v"][1 + hh], 1)
                    T.add(free["v"][1 + hh])

            def sb_tail(i):
                for hh in range(2):
                    pe.wait_ge(sem("keep_ready"), T.next(sem("keep_ready")))
                    take(3 + hh)
                    k_ = PT[:, hh, :]
                    o_ = ps[:, 3 + hh, :]
                    group(o_[:, 0:P], [(const("from_"), k_[:, 0:P])])
                    group(o_[:, P:S], [(const("from_"), k_[:, P:S]), (const("ones"), k_[:, S:3 * P])])
                    group(o_[:, S:3 * P], [(const("from_"), k_[:, S:3 * P])]).then_inc(full["v"][3 + hh], 1)
                    T.add(free["v"][3 + hh])
                take(5)
                for hh in range(2):
                    pe.wait_ge(sem("probs_ready"), T.next(sem("probs_ready")))
                    v0, v1 = (V[:, kt, ds((i * 2 + hh) * 64, 64)] for kt in range(2))
                    group(ps[:, 5, hh * 64:hh * 64 + 64], [(PR[:, hh, 0:P], v0)])
                    m = group(ps[:, 5, P + hh * 64:P + hh * 64 + 64], [(PR[:, hh, P:S], v0), (PR[:, hh, S:3 * P], v1)])
                m.then_inc(full["v"][5], 1)
                T.add(free["v"][5])
                evacuated(5)
                take(6)
                for t in range(NT):
                    m = tr(ps[:, 6, t * P:(t + 1) * P], ON[:, t, :])
                m.then_inc(full["a"][6], 1)
                T.add(free["a"][6])

            qk_proj()
            evacuated(6, 7)
            flush()
            assert not pending
            with T.loop("sb", 3) as i:
                sb_scores(i)
                qk_proj()
                sb_tail(i)
                assert not pending
            sb_scores(3)
            sb_tail(3)
            for n_, s_ in enumerate((3, 2, 3)):
                pe.wait_ge(here[s_], T.next(here[s_], 16))
                for g in range(2):
                    b = 2 * n_ + g
                    take(b)
                    for c in range(2):
                        m = group(ps[:, b, c * S:(c + 1) * S], ((slot(s_, KC, 512)[:, k, (2 * g + c) * P:(2 * g + c + 1) * P], XT[:, k, :])
                                                                 for k in range(KC)))
                    m.then_inc(full["a"][b], 1)
                    T.add(free["a"][b])
                release(s_)
            row_tile(2, (6, 7), XT, reader="a")
            pe.wait_ge(here[0], T.next(here[0], 16))
            take(0)
            for t in range(NT):
                m = group(ps[:, 0, 8 * t:8 * t + 8], ((cols(XT, t, k), slot(0, KC, 8)[:, k, :]) for k in range(KC)))
            m.then_inc(full["v"][0], 1)
            T.add(free["v"][0])
            release(0)

            def heads(b, l, r, reader="v", freer=None, base=None):
                take(b)
                for h in range(GH):
                    m = pe.matmul(ps[:, b, h * P:(h + 1) * P], l(h), r(h), start=True, stop=True)
                    if h < GH - 1:
                        first(m)
                m.then_inc(full[reader][b], 1)
                T.add(free[freer or reader][b])

            def heads_t(b, src, reader="v"):
                take(b)
                for h in range(GH):
                    m = tr(ps[:, b, h * P:(h + 1) * P], src(h))
                m.then_inc(full[reader][b], 1)
                T.add(free[reader][b])

            pe.wait_ge(sem("g_ready"), T.next(sem("g_ready")))
            take(1)
            for t in range(NT):
                g_ = GG[:, t, :]
                for o_, c_ in ((4 * t, "blk_upto"), (8 + 4 * t, "blk"), (16 + 8 * t, "half0"), (20 + 8 * t, "half1")):
                    m = pe.matmul(ps[:, 1, o_:o_ + 4], const(c_), g_, start=True, stop=True)
                    if c_ != "half1":
                        first(m)
            m.then_inc(full["v"][1], 1)
            T.add(free["v"][1])
            for t in range(NT):
                heads(2 + t, lambda h: GG[:, t, h:h + 1].to_broadcast([P, P]), lambda h: const("blk_upto"), "v", "a")
            pe.wait_ge(sem("sq_ready"), T.next(sem("sq_ready")))
            for n_ in range(4):
                b = 4 + n_
                take(b)
                pe.matmul(ps[:, b, :], const("ones"), SQ[:, 2 * n_:2 * n_ + 2, :], start=True, stop=True).then_inc(full["v"][b], 1)
                T.add(free["v"][b])
            pe.wait_ge(sem("unit_ready"), T.next(sem("unit_ready")))
            for t in range(NT):
                heads_t(t, lambda h: cols(G, t, 4 + h))
            for t in range(NT):
                heads_t(2 + t, lambda h: cols(G, t, 8 + h))
            for t in range(NT):
                heads(4 + t, lambda h: cols(G, t, 4 + h), lambda h: cols(G, t, 4 + h))
            for t in range(NT):
                heads(6 + t, lambda h: cols(G, t, h), lambda h: cols(G, t, 4 + h))
            evacuated(4, 5)
            for t in range(NT):
                heads_t(4 + t, lambda h: hd(AA, t, h))
            evacuated(6, 7)
            for t in range(NT):
                heads_t(6 + t, lambda h: hd(QK, t, h))
            for lev in range(1, 6):
                for t in range(NT):
                    pe.wait_ge(sem("lt_ready"), T.next(sem("lt_ready")))
                    heads(t, lambda h: hd(LT, t, h), lambda h: hd(TI_, t, h), "a")
                for t in range(NT):
                    evacuated(t)
                    heads(2 + t, lambda h: hd(UI, t, h), lambda h: hd(PP, t, h))
                    heads(4 + t, lambda h: hd(PP, t, h), lambda h: hd(UI, t, h))
            evacuated(2, 3, 4, 5, 6, 7)
            pe.wait_ge(sem("kb_ready"), T.next(sem("kb_ready")))
            for t in range(NT):
                heads(t, lambda h: hd(UI, t, h), lambda h: hd(VB, t, h))
                heads(2 + t, lambda h: hd(KBG, t, h), lambda h: hd(UI, t, h), "a")
            evacuated(0, 1, 2, 3)
            pe.wait_ge(sem("state_ready"), T.next(sem("state_ready")))
            for c in range(4):
                t, r = c // 2, slice(64 * (c % 2), 64 * (c % 2) + 64)
                heads(4, lambda h: hd(WT, t, h), lambda h: ST[:, h * P:(h + 1) * P])
                heads(5, lambda h: hd(QD, t, h), lambda h: ST[:, h * P:(h + 1) * P])
                evacuated(4)
                heads(6, lambda h: hd(KD, t, h)[r, :], lambda h: hd(VN, t, h)[r, :])
                if c % 2:
                    heads(7, lambda h: hd(QKT, t, h), lambda h: hd(VN, t, h))
                evacuated(6)
            pe.wait_ge(sem("og_ready"), T.next(sem("og_ready")))
            transposes(lambda t, k: hd(OI, t, k), 4)
            evacuated(0, 1)
            for n_, s_ in enumerate((3, 2, 3, 2)):
                row_tile(s_, (2 * (n_ % 2), 2 * (n_ % 2) + 1), XT, reader="a")
            for s_ in range(2):
                pe.wait_ge(here[s_], T.next(here[s_], 16))
                for c in range(2):
                    for t in range(NT):
                        b = 4 * (1 - s_) + 2 * c + t
                        take(b)
                        group(ps[:, b, :], ((cols(OT, t, 4 * s_ + k), slot(s_, 4, D)[:, k, c * 512:(c + 1) * 512]) for k in range(4))).then_inc(full["v"][b], 1)
                        T.add(free["v"][b])
                release(s_)
            pe.wait_ge(sem("merged_ready"), T.next(sem("merged_ready")))
            transposes(lambda t, k: MG[:, t, k * P:(k + 1) * P], KC)
            evacuated(0, 1, 2, 3)
            out_proj(XT2, 3)
            pe.wait_ge(sem("xs_ready"), T.next(sem("xs_ready")))
            transposes(lambda t, k: XS[:, t, k * P:(k + 1) * P], KC)
            norm_t()
            for c in range(2):
                row_tile(2 + c, (2 * c, 2 * c + 1), XT2)

            def cross_proj():
                for s_, X in ((0, XT), (1, XT2)):
                    pe.wait_ge(here[s_], T.next(here[s_], 16))
                    b = (0, 6)[s_]
                    take(b)
                    for c in range(2):
                        m = group(ps[:, b, c * S:(c + 1) * S], ((slot(s_, KC, XD)[:, k, c * P:(c + 1) * P], X[:, k, :]) for k in range(KC)))
                    release(s_)
                    m.then_inc(full["a"][b], 1)
                    T.add(free["a"][b])

            def cross_scores():
                evacuated(0, 6)
                take(1)
                for t in range(NT):
                    m = group(ps[:, 1, t * S:(t + 1) * S], ((cols(QT, t, c), KT[:, c, :]) for c in range(2)))
                m.then_inc(full["v"][1], 1)
                T.add(free["v"][1])

            def cross_tail(i):
                pe.wait_ge(sem("probs_ready"), T.next(sem("probs_ready")))
                take(3)
                for n_ in range(4):
                    t, k = n_ // 2, n_ % 2
                    m = tr(ps[:, 3, n_ * P:(n_ + 1) * P], PR[:, 0, t * S + k * P:t * S + (k + 1) * P])
                    if n_ < 3:
                        first(m)
                m.then_inc(full["a"][3], 1)
                T.add(free["a"][3])
                evacuated(3)
                take(4)
                for t in range(NT):
                    m = group(ps[:, 4, t * XD:(t + 1) * XD], ((PT[:, 0, (2 * t + k) * P:(2 * t + k + 1) * P], V[:, k, ds(i * XD, XD)]) for k in range(2)))
                m.then_inc(full["v"][4], 1)
                T.add(free["v"][4])
                evacuated(4)
                take(5)
                for n_ in range(4):
                    c, t = n_ // 2, n_ % 2
                    m = tr(ps[:, 5, n_ * P:(n_ + 1) * P], ONX[:, t, c * P:(c + 1) * P])
                m.then_inc(full["a"][5], 1)
                T.add(free["a"][5])

            cross_proj()
            evacuated(2, 3)
            flush()
            assert not pending
            with T.loop("cross", 3) as i:
                cross_scores()
                cross_proj()
                cross_tail(i)
                assert not pending
            cross_scores()
            cross_tail(3)
            out_proj(OT, 5)
            norm_t()
            def route():
                pe.wait_ge(here[0], T.next(here[0], 32))
                for q in range(2):
                    take(4 + q)
                    group(ps[:, 4 + q, 0:S], ((PW[:, q, k, :], XT[:, k, :]) for k in range(KC))).then_inc(full["a"][4 + q], 1)
                    T.add(free["a"][4 + q])
                release(0)
                pe.wait_ge(here[1], T.next(here[1], 16))
                take(6)
                first(tr(ps[:, 6, 0:P], SUBK[:, 0, :]))
                tr(ps[:, 6, P:2 * P], SUBK[:, 1, :]).then_inc(full["v"][6], 1)
                T.add(free["v"][6])
                release(1)
                evacuated(4, 5, 6)
                take(7)
                for n_ in range(4):
                    t, q = n_ // 2, n_ % 2
                    m = pe.matmul(ps[:, 7, n_ * P:(n_ + 1) * P], QP[:, q, t * P:(t + 1) * P], SKT[:, q, :], start=True, stop=True)
                    if n_ < 3:
                        first(m)
                m.then_inc(full["v"][7], 1)
                T.add(free["v"][7])
                assert not pending

            def skip_u():
                for j in range(RING):
                    T.add(gathered[j], 16 * NT)

            def mix_v():
                for t in range(NT):
                    for j in range(RING):
                        pe.wait_ge(sem("diag_ready"), T.next(sem("diag_ready")))
                        pe.wait_ge(gathered[j], T.next(gathered[j], 16))
                        for c in range(2):
                            m = pe.matmul(ps[:, 2 * t + c, :], DIAG[:, j, :], ring(j)[:, c * 512:(c + 1) * 512], start=False, stop=False)
                        m.then_inc(ring_used[j], 1)

            take(0, 1, 2, 3)
            for b in range(4):
                pe.matmul(ps[:, b, :], const("zero"), XT[:, 0:2, :], start=True, stop=False)
            route()
            route()
            skip_u()
            with T.loop("peer", PH - 2) as i:
                route()
                skip_u()
                mix_v()
            skip_u()
            mix_v()
            mix_v()
            for b in range(4):
                pe.matmul(ps[:, b, :], const("zero"), XT[:, 0:2, :], start=False, stop=True).then_inc(full["v"][b], 1)
                T.add(free["v"][b])

        @block.scalar
        def _(act):
            T = Tally(act, "act", per_iter)
            chain = sem("act_chain")

            spare = []

            def signal(name):
                spare.append(len(spare) % 64)
                act.copy(ASCR[:, spare[-1]:spare[-1] + 1], CT[:, 0:1]).then_inc(sem(name) if isinstance(name, str) else name, 1)

            act.wait_ge(sem("const_here"), T.next(sem("const_here"), 16))
            for credit in (free["a"][3], free["a"][5], *ring_used):
                signal(credit)

            def root(n=NT):
                act.wait_ge(sem("rms_ready"), T.next(sem("rms_ready")))
                act.activation(RS[:, 0:n], RS[:, 0:n], ACT.Sqrt).then_inc(sem("rstd_ready"), 1)

            def softplus_part(x):
                act.activation(x, x, ACT.Exp, scale=-1.0).then_inc(chain, 1)
                act.wait_ge(chain, T.next(chain))
                return act.activation(x, x, ACT.Ln, bias=1.0)

            def probs(blocks):
                act.wait_ge(sem("max_ready"), T.next(sem("max_ready")))
                for n_, (dst, src) in blocks:
                    m = act.activation(dst, src, ACT.Exp, bias=SM[:, n_:n_ + 1], accum_out=SM[:, 8 + n_:9 + n_])
                m.then_inc(sem("probs_ready"), 1)

            def two_probs():
                for hh in range(2):
                    probs([(4 * hh + t, (PR[:, hh, c], LG[:, hh, c])) for t, c in enumerate((slice(0, P), slice(P, 3 * P)))])

            def tail(i, b=5):
                for hh in range(2):
                    act.wait_ge(full["a"][3], T.next(full["a"][3]))
                    act.copy(PT[:, hh, 0:384], ps[:, 3, 0:384]).then_inc(free["a"][3], 1)
                ot_copy(i, b)

            def ot_copy(i, b):
                act.wait_ge(full["a"][b], T.next(full["a"][b]))
                act.copy(OT[:, ds(i, 1), :].rearrange("p o s -> p (o s)"), ps[:, b, 0:S]).then_inc(free["a"][b], 1)

            def qk_copy(scale):
                act.wait_ge(full["a"][0], T.next(full["a"][0]))
                act.mul(QT[:, 0, :], ps[:, 0, 0:S], scale)
                act.copy(KT[:, 0, :], ps[:, 0, S:2 * S]).then_inc(free["a"][0], 1)

            def high_gu(b):
                act.wait_ge(raw_here[b], T.next(raw_here[b], 32))
                act.copy(WGU[:, b, 0].rearrange("p g k n -> p (g k n)"), SLOT[b][:, 0:2 * KC * P]).then_inc(sem("high_ready"), 1)

            def high_dn(b):
                act.wait_ge(raw_here[2 + b], T.next(raw_here[2 + b], 16))
                act.wait_ge(sem(f"dn_used{b}"), T.due(sem(f"dn_used{b}")))
                act.copy(WDN[:, b, 0, :], SLOT[2 + b][:, 0:D]).then_inc(sem("high_ready"), 1)
                T.add(sem(f"dn_used{b}"))

            def gated(b):
                act.wait_ge(full["a"][4 + b], T.next(full["a"][4 + b]))
                act.activation(SG[:, b, :], ps[:, 4 + b, 0:S], ACT.Silu).then_inc(sem("silu_ready"), 1)

            def ffn(l):
                for b in range(2):
                    high_gu(b)
                root()
                for g in range(4):
                    act.wait_ge(sem("xt_ready"), T.next(sem("xt_ready")))
                    act.copy(XH[:, 0, 2 * g:2 * g + 2, :], XT[:, 2 * g:2 * g + 2, :]).then_inc(sem("high_ready"), 1)
                for b in range(2):
                    high_dn(b)
                with T.loop(f"ffn{l}", FB // 2 - 1) as i:
                    for b in range(2):
                        gated(b)
                        high_gu(b)
                    for b in range(2):
                        high_dn(b)
                for b in range(2):
                    gated(b)

            root()
            act.wait_ge(sem("absz_ready"), T.next(sem("absz_ready")))
            softplus_part(LF2[:]).then_inc(sem("ln_ready"), 1)
            qk_copy(0.125)
            with T.loop("fox", PAIRS - 1) as i:
                two_probs()
                qk_copy(0.125)
                tail(i)
            two_probs()
            tail(PAIRS - 1)
            ffn(0)
            root()
            act.wait_ge(sem("wpad_here"), 1)
            act.dma_start(WPAD[:, :, 64:96], rows(a["w_kv_a"], 256, 288)).then_inc(sem("wpad_here"), 16)
            act.wait_ge(sem("angle_ready"), T.next(sem("angle_ready")))
            act.activation(COS[0:96, 0, :], ANG[0:96, 0, :], ACT.Sin)
            act.activation(SIN[0:96, 0, :], ANG[0:96, 1, :], ACT.Sin).then_inc(sem("sin_ready"), 1)
            act.wait_ge(full["a"][4], T.next(full["a"][4]))
            act.copy(KRT[0:96, :], ps[0:96, 4, 0:S]).then_inc(free["a"][4], 1)
            for t in range(NT):
                act.wait_ge(full["a"][t], T.next(full["a"][t]))
                act.copy(KVA[:, t, 0:KVR], ps[:, t, 0:KVR]).then_inc(free["a"][t], 1)
            signal("kva_ready")
            root()
            act.wait_ge(sem("kva_used"), T.next(sem("kva_used")))
            for t in range(NT):
                for c in range(2):
                    b = (2, 3, 6, 7)[2 * t + c]
                    act.wait_ge(full["a"][b], T.next(full["a"][b]))
                    act.copy(KVA[:, t, 384 * c:384 * c + 384], ps[:, b, 0:384]).then_inc(free["a"][b], 1)
            signal("kva_ready")
            root()

            def mla_copy():
                act.wait_ge(full["a"][0], T.next(full["a"][0]))
                act.copy(QRAW[0:96, :, :], view(ps[0:96, 0, :], 2, S)).then_inc(free["a"][0], 1)
                act.wait_ge(full["a"][6], T.next(full["a"][6]))
                act.copy(KT[0:64, :, :], view(ps[0:64, 6, :], 2, S)).then_inc(free["a"][6], 1)

            mla_copy()
            with T.loop("mla", PAIRS - 1) as i:
                two_probs()
                mla_copy()
                tail(i)
            two_probs()
            tail(PAIRS - 1)
            ffn(1)
            root()
            root()
            def sb_soft():
                for hh in range(2):
                    act.wait_ge(sem("absz_ready"), T.next(sem("absz_ready")))
                    softplus_part(PR[:, hh, 0:384]).then_inc(sem("ln_ready"), 1)

            def sb_tail(i):
                for hh in range(2):
                    act.wait_ge(sem("expo_ready"), T.next(sem("expo_ready")))
                    act.activation(PR[:, hh, 0:384], LG[:, hh, 0:384], ACT.Exp).then_inc(sem("probs_ready"), 1)
                ot_copy(i, 6)

            qk_copy(0.125)
            with T.loop("sb", 3) as i:
                sb_soft()
                qk_copy(0.125)
                sb_tail(i)
            sb_soft()
            sb_tail(3)
            act.wait_ge(sem("pad_ready"), T.next(sem("pad_ready")))
            for b in range(6):
                act.wait_ge(full["a"][b], T.next(full["a"][b]))
                act.copy(PRE[:, 2 * b:2 * b + 2, CONV - 1:], view(ps[:, b, :], 2, S)).then_inc(free["a"][b], 1)
            signal("pre_ready")
            for t in range(NT):
                act.wait_ge(full["a"][6 + t], T.next(full["a"][6 + t]))
                act.activation(V[:, t, 512:], ps[:, 6 + t, :], ACT.Silu).then_inc(free["a"][6 + t], 1)
            act.wait_ge(sem("gates_ready"), T.next(sem("gates_ready")))
            act.activation(BT[:], BA[:, :, 0:4], ACT.Sigmoid)
            act.activation(AEXP, GSM[:, 0:4], ACT.Exp)
            softplus_part(GL).then_inc(sem("ln_ready"), 1)
            act.wait_ge(sem("sums_ready"), T.next(sem("sums_ready")))
            act.activation(EX, RAW, ACT.Exp).then_inc(sem("ex_ready"), 1)
            for t in range(NT):
                act.wait_ge(sem("dec_ready"), T.next(sem("dec_ready")))
                for h in range(GH):
                    m = act.activation(hd(DEC, t, h), hd(DEC, t, h), ACT.Exp, bias=RAW[:, 4 * t + h:4 * t + h + 1])
                act.activation(ER[:, t, :], ps[:, 2 + t, :], ACT.Exp).then_inc(free["a"][2 + t], 1)
            signal("er_ready")
            act.wait_ge(sem("conv_ready"), T.next(sem("conv_ready")))
            act.activation(G[:], G[:], ACT.Silu).then_inc(sem("silu_ready"), 1)
            act.wait_ge(sem("rnorm_ready"), T.next(sem("rnorm_ready")))
            act.activation(SQ[:], SQ[:], ACT.Sqrt).then_inc(sem("sqrt_ready"), 1)
            for lev in range(1, 6):
                for t in range(NT):
                    act.wait_ge(full["a"][t], T.next(full["a"][t]))
                    act.copy(PP[:, t, :], ps[:, t, :]).then_inc(free["a"][t], 1)
            for t in range(NT):
                act.wait_ge(full["a"][2 + t], T.next(full["a"][2 + t]))
                act.copy(WT[:, t, :], ps[:, 2 + t, :]).then_inc(free["a"][2 + t], 1)
            root(8)
            act.wait_ge(sem("og_ready"), T.next(sem("og_ready")))
            for n_ in range(4):
                for t in range(NT):
                    b = 2 * (n_ % 2) + t
                    act.wait_ge(full["a"][b], T.next(full["a"][b]))
                    act.activation(GT[:, t, n_ * 512:(n_ + 1) * 512], ps[:, b, :], ACT.Sigmoid).then_inc(free["a"][b], 1)
            signal("gt_ready")
            root()
            root()
            def cross_copy():
                act.wait_ge(full["a"][0], T.next(full["a"][0]))
                act.mul(QT[:], view(ps[:, 0, :], 2, S), 0.0625).then_inc(free["a"][0], 1)
                act.wait_ge(full["a"][6], T.next(full["a"][6]))
                act.copy(KT[:], view(ps[:, 6, :], 2, S)).then_inc(free["a"][6], 1)

            def cross_tail(i):
                act.wait_ge(full["a"][3], T.next(full["a"][3]))
                act.copy(PT[:, 0, :], ps[:, 3, :]).then_inc(free["a"][3], 1)
                act.wait_ge(full["a"][5], T.next(full["a"][5]))
                act.copy(OT[:, ds(i * 2, 2), :], view(ps[:, 5, :], 2, S)).then_inc(free["a"][5], 1)

            def cross_probs():
                probs([(t, (PR[:, 0, t * S:(t + 1) * S], LG[:, 0, t * S:(t + 1) * S])) for t in range(NT)])

            cross_copy()
            with T.loop("cross", 3) as i:
                cross_probs()
                cross_copy()
                cross_tail(i)
            cross_probs()
            cross_tail(3)
            root()
            def queries():
                for q in range(2):
                    act.wait_ge(full["a"][4 + q], T.next(full["a"][4 + q]))
                    act.copy(QP[:, q, :], ps[:, 4 + q, 0:S]).then_inc(free["a"][4 + q], 1)

            def gate_exp():
                act.wait_ge(sem("best_ready"), T.next(sem("best_ready")))
                act.activation(GX[:], BSX[:], ACT.Exp).then_inc(sem("gate_exp"), 1)

            def gelu():
                for j in range(RING):
                    T.add(ring_used[j], NT)
                act.wait_ge(ring_used[RING - 1], T.due(ring_used[RING - 1]))
                act.activation(AX_[:], DOT[:], ACT.Gelu).then_inc(sem("gelu_ready"), 1)

            def diagonals(h):
                for t in range(NT):
                    for j in range(RING):
                        act.wait_ge(ring_used[j], T.due(ring_used[j]))
                        act.activation(DIAG[:, j, :], IDENT, ACT.Copy, scale=AV[:, t, ds(h * TOPK + j, 1)]).then_inc(sem("diag_ready"), 1)
                        T.add(ring_used[j])

            for j in range(RING):
                T.add(ring_used[j])
            queries()
            gate_exp()
            queries()
            gelu()
            gate_exp()
            with T.loop("peer", PH - 2) as i:
                queries()
                gelu()
                act.wait_ge(sem("av_ready"), T.next(sem("av_ready")))
                diagonals(i)
                gate_exp()
            gelu()
            act.wait_ge(sem("av_ready"), T.next(sem("av_ready")))
            diagonals(PH - 2)
            act.wait_ge(sem("av_ready"), T.next(sem("av_ready")))
            diagonals(PH - 1)
            root()

        @block.gpsimd
        def _(pool):
            T = Tally(pool, "pool", per_iter)

            for j in range(RING):
                T.add(ring_used[j])
            pool.memset(PSCR[:], 0.0).then_inc(sem("pool_chain"), 1)
            pool.wait_ge(sem("pool_chain"), T.next(sem("pool_chain")))
            u_rows, v_rows = a["peer_u_2"][0], a["peer_v_2"][0]

            def gather(table, h):
                for t in range(NT):
                    for g in range(0, RING, 4):
                        for j in range(g, g + 4):
                            pool.wait_ge(ring_used[j], T.due(ring_used[j]))
                            T.add(ring_used[j])
                        pool.tensor_copy(IX[:, g:g + 4], EXU[:, t, ds(h * TOPK + g, 4)]).then_inc(sem("pool_chain"), 1)
                        pool.wait_ge(sem("pool_chain"), T.next(sem("pool_chain")))
                        pool.tensor_tensor(PSCR[:, g:g + 1], PSCR[:, 15:16], PSCR[:, 15:16], ALU.add)
                        for j in range(g, g + 4):
                            pool.indirect_dma_start(ring(j), None, table, bass.IndirectOffsetOnAxis(IX[:, j:j + 1], 0)).then_inc(gathered[j], 16)

            pool.wait_ge(sem("expert_ready"), T.next(sem("expert_ready")))
            gather(u_rows, 0)
            with T.loop("peer", PH - 2) as i:
                pool.wait_ge(sem("expert_ready"), T.next(sem("expert_ready")))
                gather(u_rows, i + 1)
                gather(v_rows, i)
            pool.wait_ge(sem("expert_ready"), T.next(sem("expert_ready")))
            gather(u_rows, PH - 1)
            gather(v_rows, PH - 2)
            gather(v_rows, PH - 1)

        @block.vector
        def _(dve):
            T = Tally(dve, "dve", per_iter)
            chain = sem("dve_chain")
            TT, TS, STT = dve.tensor_tensor, dve.tensor_scalar, dve.scalar_tensor_tensor

            def settled(*banks):
                for b in banks:
                    dve.wait_ge(free["v"][b], T.due(free["v"][b]))

            def rstd(width, n):
                TS(RS[:, 0:n], SS[:, 0:n], 1.0 / width, EPS, ALU.mult, ALU.add).then_inc(chain, 1)
                dve.wait_ge(chain, T.next(chain))
                dve.reciprocal(RS[:, 0:n], RS[:, 0:n]).then_inc(sem("rms_ready"), 1)
                dve.wait_ge(sem("rstd_ready"), T.next(sem("rstd_ready")))

            spare = []

            def signal(name):
                spare.append(34 + len(spare) % 24)
                dve.tensor_copy(SM[:, spare[-1]:spare[-1] + 1], SM[:, 33:34]).then_inc(sem(name), 1)

            def scaled(src, w):
                for t in range(NT):
                    m = STT(XS[:, t, 0:w], src[:, t, 0:w], 1.0, src[:, t, 0:w], ALU.mult, ALU.mult, accum_out=SS[:, t:t + 1])
                m.then_inc(chain, 1)
                dve.wait_ge(chain, T.next(chain))
                rstd(w, NT)
                for t in range(NT):
                    m = TS(XS[:, t, 0:w], src[:, t, 0:w], RS[:, t:t + 1], None, ALU.mult)
                return m

            def gained(X, name, n_chunks, banks=(0, 1, 2, 3), X2=None, name2=None):
                for g in range(n_chunks // 2):
                    b = banks[g % len(banks)]
                    dve.wait_ge(full["v"][b], T.next(full["v"][b]))
                    src = view(ps[:, b, :], 2, S)
                    if X2 is not None:
                        TT(X2[:, 2 * g:2 * g + 2, :], src, inner(gcol(name2, 2 * g, 2), S), ALU.mult)
                    TT(X[:, 2 * g:2 * g + 2, :], src, inner(gcol(name, 2 * g, 2), S), ALU.mult).then_inc(free["v"][b], 1)
                    T.add(free["v"][b])

            def norm(name, X=None, X2=None, name2=None, src=None):
                scaled(H if src is None else src, D).then_inc(sem("xs_ready"), 1)
                gained(XT if X is None else X, name, KC, X2=X2, name2=name2)

            def values(banks_of):
                for c in range(2):
                    for t in range(NT):
                        b = banks_of(c, t)
                        dve.wait_ge(full["v"][b], T.next(full["v"][b]))
                        dve.tensor_copy(V[:, t, c * 512:(c + 1) * 512], ps[:, b, :]).then_inc(free["v"][b], 1)
                        T.add(free["v"][b])

            def residual(banks_of=lambda c, t: 2 * c + t, order=None):
                for c in range(2):
                    for t in range(NT):
                        b = banks_of(c, t)
                        dve.wait_ge(full["v"][b], T.next(full["v"][b]))
                        TT(H[:, t, c * 512:(c + 1) * 512], H[:, t, c * 512:(c + 1) * 512], ps[:, b, :], ALU.add).then_inc(free["v"][b], 1)
                        T.add(free["v"][b])
                settled(0, 1, 2, 3)

            def neg_max(hh):
                link_before = [(0, slice(0, P)), (1, slice(P, 3 * P))]
                for t, c in link_before:
                    m = dve.tensor_reduce(SM[:, 4 * hh + t:4 * hh + t + 1], LG[:, hh, c], AX, ALU.max, negate=True)
                m.then_inc(sem("max_ready"), 1)

            CAUSAL = const("causal")

            def attend_tail(i):
                for hh in range(2):
                    dve.wait_ge(sem("probs_ready"), T.next(sem("probs_ready")))
                dve.reciprocal(SM[:, 16:24], SM[:, 8:16]).then_inc(chain, 1)
                dve.wait_ge(chain, T.next(chain))
                dve.wait_ge(full["v"][4], T.next(full["v"][4]))
                for hh in range(2):
                    for t in range(NT):
                        m = TS(ON[:, t, hh * 64:hh * 64 + 64], ps[:, 4, t * P + hh * 64:t * P + hh * 64 + 64],
                               SM[:, 16 + 4 * hh + t:17 + 4 * hh + t], None, ALU.mult)
                m.then_inc(free["v"][4], 1)
                T.add(free["v"][4])

            def low(out_, x, high):
                return TT(out_, x, high.bitcast(F32), ALU.subtract)

            def low_gu(b):
                dve.wait_ge(sem("high_ready"), T.next(sem("high_ready")))
                low(WGU[:, b, 1].rearrange("p g k n -> p (g k n)"), SLOT[b][:, 0:2 * KC * P],
                    WGU[:, b, 0].rearrange("p g k n -> p (g k n)")).then_inc(used[b], 1)
                signal(f"gu_split{b}")

            def low_dn(b):
                dve.wait_ge(sem("high_ready"), T.next(sem("high_ready")))
                low(WDN[:, b, 1, :], SLOT[2 + b][:, 0:D], WDN[:, b, 0, :]).then_inc(used[2 + b], 1)
                signal(f"dn_split{b}")

            def gated(b):
                dve.wait_ge(sem("silu_ready"), T.next(sem("silu_ready")))
                TT(SG[:, b, :], SG[:, b, :], ps[:, 4 + b, S:2 * S], ALU.mult).then_inc(chain, 1)
                dve.wait_ge(chain, T.next(chain))
                dve.tensor_copy(HT[:, b, 0, :], SG[:, b, :]).then_inc(chain, 1)
                dve.wait_ge(chain, T.next(chain))
                low(HT[:, b, 1, :], SG[:, b, :], HT[:, b, 0, :]).then_inc(free["v"][4 + b], 1)
                T.add(free["v"][4 + b])

            def ffn(l):
                settled(*range(4))
                for b in range(2):
                    low_gu(b)
                scaled(H, D).then_inc(sem("xs_ready"), 1)
                for g in range(4):
                    dve.wait_ge(full["v"][g], T.next(full["v"][g]))
                    TT(XT[:, 2 * g:2 * g + 2, :], view(ps[:, g, :], 2, S), inner(gcol(f"ffn{l}", 2 * g, 2), S), ALU.mult).then_inc(free["v"][g], 1)
                    T.add(free["v"][g])
                    settled(g)
                    signal("xt_ready")
                for g in range(4):
                    dve.wait_ge(sem("high_ready"), T.next(sem("high_ready")))
                    m = low(XH[:, 1, 2 * g:2 * g + 2, :], XT[:, 2 * g:2 * g + 2, :], XH[:, 0, 2 * g:2 * g + 2, :])
                m.then_inc(sem("xh_ready"), 1)
                for b in range(2):
                    low_dn(b)
                with T.loop(f"ffn{l}", FB // 2 - 1) as i:
                    for b in range(2):
                        gated(b)
                        low_gu(b)
                    for b in range(2):
                        low_dn(b)
                for b in range(2):
                    gated(b)
                residual(lambda c, t: 2 * t + c)

            def absolute(out_, x):
                return STT(out_, x, -1.0, x, ALU.mult, ALU.max)

            def softplus(out_, x, part):
                return STT(out_, x, 0.0, part, ALU.max, ALU.add)

            dve.memset(SM[:], 1.0)
            dve.wait_ge(sem("x_here"), T.next(sem("x_here"), 16))
            scaled(H, D).then_inc(sem("xs_ready"), 1)
            dve.wait_ge(full["v"][0], T.next(full["v"][0]))
            dve.tensor_copy(GCOL[:], ps[:, 0, 0:P]).then_inc(free["v"][0], 1)
            T.add(free["v"][0])
            settled(0)
            gained(XT, "attn0", KC)
            dve.wait_ge(sem("wf_here"), T.next(sem("wf_here"), 32))
            dve.wait_ge(full["v"][4], T.next(full["v"][4]))
            TT(LF[:], view(ps[:, 4, 0:32], NT, 16), outer(BF[:], NT), ALU.add).then_inc(free["v"][4], 1)
            T.add(free["v"][4])
            settled(4)
            absolute(LF2[:], LF[:]).then_inc(sem("absz_ready"), 1)
            dve.wait_ge(sem("ln_ready"), T.next(sem("ln_ready")))
            STT(LF[:], LF[:], 0.0, LF2[:], ALU.min, ALU.subtract).then_inc(chain, 1)
            dve.wait_ge(chain, T.next(chain))
            signal("logf_ready")
            values(lambda c, t: 2 * c + t)
            dve.wait_ge(full["v"][4], T.next(full["v"][4]))
            dve.tensor_copy(CQ[:], view(ps[:, 4, 0:32], NT, 16)).then_inc(free["v"][4], 1)
            T.add(free["v"][4])
            dve.wait_ge(full["v"][5], T.next(full["v"][5]))
            TS(CUMT[:], ps[0:16, 5, 0:S], -1.0, None, ALU.mult).then_inc(free["v"][5], 1)
            T.add(free["v"][5])
            settled(5)
            signal("cumt_ready")

            def fox_scores(i):
                for hh in range(2):
                    dve.wait_ge(full["v"][1 + hh], T.next(full["v"][1 + hh]))
                    STT(LG[:, hh, 0:P], ps[:, 1 + hh, 0:P], CQ[:, 0, ds(i * 2 + hh, 1)], CAUSAL[:, P:2 * P], ALU.add, ALU.add)
                    STT(LG[:, hh, P:3 * P], ps[:, 1 + hh, P:3 * P], CQ[:, 1, ds(i * 2 + hh, 1)], CAUSAL, ALU.add, ALU.add).then_inc(free["v"][1 + hh], 1)
                    T.add(free["v"][1 + hh])
                    settled(1 + hh)
                    neg_max(hh)

            with T.loop("fox", PAIRS - 1) as i:
                fox_scores(i)
                attend_tail(i)
            fox_scores(PAIRS - 1)
            attend_tail(PAIRS - 1)
            residual()
            ffn(0)
            dve.memset(WPAD[:], 0.0).then_inc(chain, 1)
            dve.wait_ge(chain, T.next(chain))
            signal("wpad_here")
            norm("attn1", X2=XT2, name2="kv")
            dve.wait_ge(sem("pos_here"), T.next(sem("pos_here"), 16))
            R96 = slice(0, 96)
            posf, ang = ANG[R96, 2, :], ANG[R96, 3, :]
            dve.tensor_copy(posf, POSI[R96, :]).then_inc(chain, 1)
            dve.wait_ge(chain, T.next(chain))
            TS(ang, posf, const("inv_freq", 96), None, ALU.mult).then_inc(chain, 1)
            dve.wait_ge(chain, T.next(chain))
            MAGIC = 12582912.0
            for n_, quarter in ((0, 0.25), (1, 0.0)):
                x, k = ANG[R96, n_, :], posf
                TS(k, ang, 1.0 / TWO_PI, quarter, ALU.mult, ALU.add).then_inc(chain, 1)
                dve.wait_ge(chain, T.next(chain))
                TS(k, k, MAGIC, None, ALU.add).then_inc(chain, 1)
                dve.wait_ge(chain, T.next(chain))
                TS(k, k, MAGIC, None, ALU.subtract).then_inc(chain, 1)
                dve.wait_ge(chain, T.next(chain))
                STT(x, k, -PI_PARTS[0], ang, ALU.mult, ALU.add).then_inc(chain, 1)
                dve.wait_ge(chain, T.next(chain))
                STT(x, k, -PI_PARTS[1], x, ALU.mult, ALU.add).then_inc(chain, 1)
                dve.wait_ge(chain, T.next(chain))
                STT(x, k, -PI_PARTS[2], x, ALU.mult, ALU.add).then_inc(chain, 1)
                dve.wait_ge(chain, T.next(chain))
                TS(x, x, quarter * TWO_PI, 3.1415925, ALU.add, ALU.min).then_inc(chain, 1)
                dve.wait_ge(chain, T.next(chain))
                TS(x, x, -3.1415925, None, ALU.max).then_inc(chain, 1)
                dve.wait_ge(chain, T.next(chain))
            signal("angle_ready")
            dve.wait_ge(sem("sin_ready"), T.next(sem("sin_ready")))
            dve.tensor_copy(COS[R96, 1, :], COS[R96, 0, :])
            dve.tensor_copy(SIN[R96, 1, :], SIN[R96, 0, :]).then_inc(chain, 1)
            dve.wait_ge(chain, T.next(chain))
            dve.wait_ge(sem("kva_ready"), T.next(sem("kva_ready")))
            scaled(KVA, KVR).then_inc(sem("xs_ready"), 1)
            dve.wait_ge(full["v"][5], T.next(full["v"][5]))
            TT(ANG[R96, 2, :], ps[R96, 5, 0:S], SIN[R96, 0, :], ALU.mult).then_inc(chain, 1)
            dve.wait_ge(chain, T.next(chain))
            TT(KRT[R96, :], KRT[R96, :], COS[R96, 0, :], ALU.mult).then_inc(chain, 1)
            dve.wait_ge(chain, T.next(chain))
            TT(KRT[R96, :], KRT[R96, :], ANG[R96, 2, :], ALU.add).then_inc(free["v"][5], 1)
            T.add(free["v"][5])
            settled(5)
            dve.tensor_copy(KT[64:96, 0, :], KRT[64:96, :])
            dve.tensor_copy(KT[64:96, 1, :], KRT[64:96, :]).then_inc(chain, 1)
            dve.wait_ge(chain, T.next(chain))
            signal("krope_ready")
            signal("kva_used")
            gained(CKT, "ckv", 2)
            values(lambda c, t: (4, 5)[t])
            dve.wait_ge(sem("kva_ready"), T.next(sem("kva_ready")))
            scaled(KVA, QR).then_inc(sem("xs_ready"), 1)
            gained(CQT, "cq", 6, (0, 1, 2))

            def rotate():
                dve.wait_ge(full["v"][7], T.next(full["v"][7]))
                TT(ANG[R96, 0:2, :], view(ps[R96, 7, :], 2, S), SIN[R96, :, :], ALU.mult)
                TT(ANG[R96, 2:4, :], QRAW[R96, :, :], COS[R96, :, :], ALU.mult).then_inc(chain, 1)
                dve.wait_ge(chain, T.next(chain))
                TT(QT[R96, :, :], ANG[R96, 0:2, :], ANG[R96, 2:4, :], ALU.add).then_inc(free["v"][7], 1)
                T.add(free["v"][7])

            def mla_scores():
                for hh in range(2):
                    dve.wait_ge(full["v"][1 + hh], T.next(full["v"][1 + hh]))
                    STT(LG[:, hh, 0:P], ps[:, 1 + hh, 0:P], MLA_SCALE, CAUSAL[:, P:2 * P], ALU.mult, ALU.add)
                    STT(LG[:, hh, P:3 * P], ps[:, 1 + hh, P:3 * P], MLA_SCALE, CAUSAL, ALU.mult, ALU.add).then_inc(free["v"][1 + hh], 1)
                    T.add(free["v"][1 + hh])
                    settled(1 + hh)
                    neg_max(hh)

            rotate()
            with T.loop("mla", PAIRS - 1) as i:
                mla_scores()
                rotate()
                attend_tail(i)
            mla_scores()
            attend_tail(PAIRS - 1)
            residual()
            ffn(1)
            scaled(H, D).then_inc(chain, 1)
            dve.wait_ge(chain, T.next(chain))
            dve.wait_ge(sem("rowg_here"), T.next(sem("rowg_here"), 16))
            TT(H[:], XS[:], outer(ROWG[:], NT), ALU.mult).then_inc(chain, 1)
            dve.wait_ge(chain, T.next(chain))
            signal("rowg_used")
            norm("mix")
            for t in range(NT):
                dve.wait_ge(full["v"][6 + t], T.next(full["v"][6 + t]))
                dve.tensor_copy(V[:, t, 0:512], ps[:, 6 + t, :]).then_inc(free["v"][6 + t], 1)
                T.add(free["v"][6 + t])

            def sb_scores():
                for hh in range(2):
                    dve.wait_ge(full["v"][1 + hh], T.next(full["v"][1 + hh]))
                    dve.tensor_copy(LG[:, hh, 0:384], ps[:, 1 + hh, 0:384]).then_inc(free["v"][1 + hh], 1)
                    T.add(free["v"][1 + hh])
                    settled(1 + hh)
                    absolute(PR[:, hh, 0:384], LG[:, hh, 0:384]).then_inc(sem("absz_ready"), 1)

            def sb_keep():
                for hh in range(2):
                    dve.wait_ge(sem("ln_ready"), T.next(sem("ln_ready")))
                    softplus(PT[:, hh, 0:384], LG[:, hh, 0:384], PR[:, hh, 0:384]).then_inc(chain, 1)
                    dve.wait_ge(chain, T.next(chain))
                    TT(LG[:, hh, 0:384], LG[:, hh, 0:384], const("sb_neg"), ALU.add)
                    TT(PT[:, hh, 0:384], PT[:, hh, 0:384], const("sb_keep"), ALU.mult).then_inc(sem("keep_ready"), 1)

            def sb_tail():
                for hh in range(2):
                    dve.wait_ge(full["v"][3 + hh], T.next(full["v"][3 + hh]))
                    TT(LG[:, hh, 0:384], LG[:, hh, 0:384], ps[:, 3 + hh, 0:384], ALU.add).then_inc(free["v"][3 + hh], 1)
                    T.add(free["v"][3 + hh])
                    settled(3 + hh)
                    signal("expo_ready")
                dve.wait_ge(full["v"][5], T.next(full["v"][5]))
                dve.tensor_copy(ON[:], view(ps[:, 5, 0:S], 2, P)).then_inc(free["v"][5], 1)
                T.add(free["v"][5])

            with T.loop("sb", 3) as i:
                sb_scores()
                sb_keep()
                sb_tail()
            sb_scores()
            sb_keep()
            sb_tail()
            T.add(sem("probs_ready"), 8)
            settled(5)
            dve.memset(PRE[:, :, 0:CONV - 1], 0.0).then_inc(chain, 1)
            dve.wait_ge(chain, T.next(chain))
            dve.memset(ST[:], 0.0).then_inc(sem("pad_ready"), 1)
            dve.wait_ge(sem("gsm_here"), T.next(sem("gsm_here"), 48))
            dve.wait_ge(full["v"][0], T.next(full["v"][0]))
            dve.tensor_copy(BA[:], view(ps[:, 0, 0:16], NT, 8)).then_inc(free["v"][0], 1)
            T.add(free["v"][0])
            settled(0)
            TT(GZ, BA[:, :, 4:8], outer(GSM[:, 4:8], NT), ALU.add).then_inc(chain, 1)
            dve.wait_ge(chain, T.next(chain))
            absolute(GL, GZ).then_inc(sem("gates_ready"), 1)
            dve.wait_ge(sem("ln_ready"), T.next(sem("ln_ready")))
            softplus(GZ, GZ, GL).then_inc(chain, 1)
            dve.wait_ge(chain, T.next(chain))
            STT(GG, GZ, -1.0, outer(AEXP, NT), ALU.mult, ALU.mult).then_inc(chain, 1)
            dve.wait_ge(chain, T.next(chain))
            signal("g_ready")
            dve.wait_ge(full["v"][1], T.next(full["v"][1]))
            dve.tensor_copy(RAW[:, 16:32], ps[:, 1, 16:32])
            dve.tensor_copy(RAW[:, 0:8], ps[:, 1, 0:8]).then_inc(chain, 1)
            dve.wait_ge(chain, T.next(chain))
            TT(RAW[:, 8:16], ps[:, 1, 8:16], RAW[:, 0:8], ALU.subtract).then_inc(free["v"][1], 1)
            T.add(free["v"][1])
            settled(1)
            signal("sums_ready")
            for t in range(NT):
                dve.wait_ge(full["v"][2 + t], T.next(full["v"][2 + t]))
                TT(view(DEC[:, t, :], GH, P), outer(const("dmask"), GH), view(ps[:, 2 + t, :], GH, P), ALU.subtract).then_inc(sem("dec_ready"), 1)
            dve.wait_ge(sem("pre_ready"), T.next(sem("pre_ready")))
            for j in range(CONV):
                for b in range(12):
                    tap, src = gcol("conv", j * 12 + b, 1), PRE[:, b, j:j + S]
                    m = TS(G[:, b, :], src, tap, None, ALU.mult) if j == 0 else STT(G[:, b, :], src, tap, G[:, b, :], ALU.mult, ALU.add)
                m.then_inc(chain, 1)
                dve.wait_ge(chain, T.next(chain))
            signal("conv_ready")
            dve.wait_ge(sem("silu_ready"), T.next(sem("silu_ready")))
            TT(SQ[:], G[:, 0:8, :], G[:, 0:8, :], ALU.mult).then_inc(sem("sq_ready"), 1)
            for n_ in range(4):
                dve.wait_ge(full["v"][4 + n_], T.next(full["v"][4 + n_]))
                TS(SQ[:, 2 * n_:2 * n_ + 2, :], view(ps[:, 4 + n_, :], 2, S), EPS, None, ALU.add).then_inc(free["v"][4 + n_], 1)
                T.add(free["v"][4 + n_])
            settled(4, 5, 6, 7)
            dve.reciprocal(SQ[:], SQ[:]).then_inc(sem("rnorm_ready"), 1)
            dve.wait_ge(sem("sqrt_ready"), T.next(sem("sqrt_ready")))
            STT(G[:, 0:4, :], G[:, 0:4, :], float(P) ** -0.5, SQ[:, 0:4, :], ALU.mult, ALU.mult)
            TT(G[:, 4:8, :], G[:, 4:8, :], SQ[:, 4:8, :], ALU.mult).then_inc(chain, 1)
            dve.wait_ge(chain, T.next(chain))
            signal("unit_ready")
            dve.wait_ge(sem("er_ready"), T.next(sem("er_ready")))
            dve.wait_ge(sem("ex_ready"), T.next(sem("ex_ready")))
            for t in range(NT):
                TT(view(QD[:, t, :], GH, P), G[:, 0:4, t * P:(t + 1) * P], view(ER[:, t, :], GH, P), ALU.mult)
            TT(BE[:], BT[:], view(EX[:, 0:8], NT, GH), ALU.mult).then_inc(chain, 1)
            dve.wait_ge(chain, T.next(chain))
            for t in range(NT):
                dve.wait_ge(full["v"][t], T.next(full["v"][t]))
                TT(view(KBG[:, t, :], GH, P), view(ps[:, t, :], GH, P), inner(BE[:, t, :], P), ALU.mult)
                TT(view(KD[:, t, :], GH, P), view(ps[:, t, :], GH, P), inner(EX[:, 8 + 4 * t:12 + 4 * t], P), ALU.mult).then_inc(free["v"][t], 1)
                T.add(free["v"][t])
            for t in range(NT):
                dve.wait_ge(full["v"][2 + t], T.next(full["v"][2 + t]))
                TT(view(VB[:, t, :], GH, P), view(ps[:, 2 + t, :], GH, P), inner(BT[:, t, :], P), ALU.mult).then_inc(free["v"][2 + t], 1)
                T.add(free["v"][2 + t])
            settled(2, 3)
            for t in range(NT):
                dve.wait_ge(full["v"][4 + t], T.next(full["v"][4 + t]))
                TT(view(AA[:, t, :], GH, P), view(ps[:, 4 + t, :], GH, P), inner(BT[:, t, :], P), ALU.mult).then_inc(chain, 1)
                dve.wait_ge(chain, T.next(chain))
                TT(AA[:, t, :], AA[:, t, :], DEC[:, t, :], ALU.mult).then_inc(free["v"][4 + t], 1)
                T.add(free["v"][4 + t])
            for t in range(NT):
                dve.wait_ge(full["v"][6 + t], T.next(full["v"][6 + t]))
                TT(QK[:, t, :], ps[:, 6 + t, :], DEC[:, t, :], ALU.mult).then_inc(free["v"][6 + t], 1)
                T.add(free["v"][6 + t])

            def level(name, l):
                return outer(const(name)[:, l * P:(l + 1) * P], GH)

            for t in range(NT):
                dve.wait_ge(full["v"][4 + t], T.next(full["v"][4 + t]))
                dve.tensor_copy(AT[:, t, :], ps[:, 4 + t, :]).then_inc(free["v"][4 + t], 1)
                T.add(free["v"][4 + t])
            for t in range(NT):
                dve.wait_ge(full["v"][6 + t], T.next(full["v"][6 + t]))
                dve.tensor_copy(QKT[:, t, :], ps[:, 6 + t, :]).then_inc(free["v"][6 + t], 1)
                T.add(free["v"][6 + t])
            settled(4, 5, 6, 7)
            for t in range(NT):
                TT(view(TI_[:, t, :], GH, P), view(AA[:, t, :], GH, P), level("lev", 0), ALU.mult)
                TT(view(UI[:, t, :], GH, P), view(AT[:, t, :], GH, P), level("levT", 0), ALU.mult).then_inc(chain, 1)
                dve.wait_ge(chain, T.next(chain))
                TT(view(TI_[:, t, :], GH, P), outer(IDENT, GH), view(TI_[:, t, :], GH, P), ALU.subtract)
                TT(view(UI[:, t, :], GH, P), outer(IDENT, GH), view(UI[:, t, :], GH, P), ALU.subtract).then_inc(chain, 1)
                dve.wait_ge(chain, T.next(chain))
            for lev in range(1, 6):
                for t in range(NT):
                    TT(view(LT[:, t, :], GH, P), view(AT[:, t, :], GH, P), level("levT", lev), ALU.mult).then_inc(sem("lt_ready"), 1)
                for t in range(NT):
                    dve.wait_ge(full["v"][2 + t], T.next(full["v"][2 + t]))
                    TT(TI_[:, t, :], TI_[:, t, :], ps[:, 2 + t, :], ALU.subtract).then_inc(free["v"][2 + t], 1)
                    T.add(free["v"][2 + t])
                    dve.wait_ge(full["v"][4 + t], T.next(full["v"][4 + t]))
                    TT(UI[:, t, :], UI[:, t, :], ps[:, 4 + t, :], ALU.subtract).then_inc(free["v"][4 + t], 1)
                    T.add(free["v"][4 + t])
                settled(2, 3, 4, 5)
            signal("kb_ready")
            for t in range(NT):
                dve.wait_ge(full["v"][t], T.next(full["v"][t]))
                dve.tensor_copy(UU[:, t, :], ps[:, t, :]).then_inc(free["v"][t], 1)
                T.add(free["v"][t])
            settled(0, 1)
            signal("state_ready")
            for c in range(4):
                t, r = c // 2, slice(64 * (c % 2), 64 * (c % 2) + 64)
                dve.wait_ge(full["v"][4], T.next(full["v"][4]))
                TT(VN[r, t, :], UU[r, t, :], ps[r, 4, :], ALU.subtract).then_inc(free["v"][4], 1)
                T.add(free["v"][4])
                dve.wait_ge(full["v"][5], T.next(full["v"][5]))
                dve.tensor_copy(OI[r, t, :], ps[r, 5, :]).then_inc(free["v"][5], 1)
                T.add(free["v"][5])
                TT(view(ST, GH, P), view(ST, GH, P), inner(EX[:, 16 + 4 * c:20 + 4 * c], P), ALU.mult).then_inc(chain, 1)
                dve.wait_ge(chain, T.next(chain))
                dve.wait_ge(full["v"][6], T.next(full["v"][6]))
                TT(ST, ST, ps[:, 6, :], ALU.add).then_inc(free["v"][6], 1)
                T.add(free["v"][6])
                settled(6)
                if c % 2:
                    dve.wait_ge(full["v"][7], T.next(full["v"][7]))
                    TT(OI[:, t, :], OI[:, t, :], ps[:, 7, :], ALU.add).then_inc(free["v"][7], 1)
                    T.add(free["v"][7])
            settled(7)
            TT(VN[:], OI[:], OI[:], ALU.mult).then_inc(chain, 1)
            dve.wait_ge(chain, T.next(chain))
            dve.tensor_reduce(SS[:, 0:8], VN[:].rearrange("p t (h d) -> p (t h) d", h=GH), AX, ALU.add).then_inc(chain, 1)
            dve.wait_ge(chain, T.next(chain))
            rstd(P, 8)
            for t in range(NT):
                m = TT(view(OI[:, t, :], GH, P), view(OI[:, t, :], GH, P), inner(RS[:, 4 * t:4 * t + 4], P), ALU.mult)
            m.then_inc(chain, 1)
            dve.wait_ge(chain, T.next(chain))
            TT(OI[:], OI[:], V[:, :, 512:], ALU.mult).then_inc(chain, 1)
            dve.wait_ge(chain, T.next(chain))
            signal("og_ready")
            for g in range(2):
                dve.wait_ge(full["v"][g], T.next(full["v"][g]))
                TS(OT[:, 4 + 2 * g:6 + 2 * g, :], view(ps[:, g, :], 2, S), GDNG, None, ALU.mult).then_inc(free["v"][g], 1)
                T.add(free["v"][g])
            dve.wait_ge(sem("gt_ready"), T.next(sem("gt_ready")))
            for s_ in range(2):
                for c in range(2):
                    for t in range(NT):
                        b = 4 * (1 - s_) + 2 * c + t
                        dve.wait_ge(full["v"][b], T.next(full["v"][b]))
                        gate = GT[:, t, s_ * D + c * 512:s_ * D + (c + 1) * 512]
                        dst = MG[:, t, c * 512:(c + 1) * 512]
                        if s_ == 0:
                            TT(dst, ps[:, b, :], gate, ALU.mult).then_inc(free["v"][b], 1)
                            T.add(free["v"][b])
                        else:
                            TT(XS[:, t, c * 512:(c + 1) * 512], ps[:, b, :], gate, ALU.mult).then_inc(free["v"][b], 1)
                            T.add(free["v"][b])
            settled(*range(8))
            TT(MG[:], MG[:], XS[:], ALU.add).then_inc(chain, 1)
            dve.wait_ge(chain, T.next(chain))
            signal("merged_ready")
            for g in range(4):
                dve.wait_ge(full["v"][g], T.next(full["v"][g]))
                dve.tensor_copy(XT2[:, 2 * g:2 * g + 2, :], view(ps[:, g, :], 2, S)).then_inc(free["v"][g], 1)
                T.add(free["v"][g])
            residual()
            signal("mix_done")
            dve.wait_ge(sem("mem_here"), T.next(sem("mem_here"), 16))
            norm("mem", X=XT2, src=MEM)
            settled(0, 1, 2, 3)
            norm("cross")
            values(lambda c, t: 2 * c + t)

            def cross_scores():
                dve.wait_ge(full["v"][1], T.next(full["v"][1]))
                dve.tensor_copy(LG[:, 0, :], ps[:, 1, :]).then_inc(free["v"][1], 1)
                T.add(free["v"][1])
                settled(1)
                dve.tensor_reduce(SM[:, 0:2], view(LG[:, 0, :], 2, S), AX, ALU.max, negate=True).then_inc(sem("max_ready"), 1)

            def cross_tail():
                dve.wait_ge(sem("probs_ready"), T.next(sem("probs_ready")))
                dve.reciprocal(SM[:, 16:18], SM[:, 8:10]).then_inc(chain, 1)
                dve.wait_ge(chain, T.next(chain))
                dve.wait_ge(full["v"][4], T.next(full["v"][4]))
                for t in range(NT):
                    m = TS(ONX[:, t, :], ps[:, 4, t * XD:(t + 1) * XD], SM[:, 16 + t:17 + t], None, ALU.mult)
                m.then_inc(free["v"][4], 1)
                T.add(free["v"][4])

            with T.loop("cross", 3) as i:
                cross_scores()
                cross_tail()
            cross_scores()
            cross_tail()
            residual()
            norm("peer")
            dve.wait_ge(sem("rowg_here"), T.next(sem("rowg_here"), 16))
            TT(V[:], XS[:], outer(ROWG[:], NT), ALU.mult).then_inc(chain, 1)
            dve.wait_ge(chain, T.next(chain))
            signal("rowg_used")
            four = [(t, q) for t in range(NT) for q in range(2)]
            def keys():
                dve.wait_ge(full["v"][6], T.next(full["v"][6]))
                dve.tensor_copy(SKT[:], view(ps[:, 6, 0:2 * P], 2, P)).then_inc(free["v"][6], 1)
                T.add(free["v"][6])

            def route(h):
                keys()
                dve.wait_ge(full["v"][7], T.next(full["v"][7]))
                dve.tensor_copy(SC[:], view(ps[:, 7, :], NT, 2, P)).then_inc(free["v"][7], 1)
                T.add(free["v"][7])
                settled(7)

                def bear():
                    spare.append(34 + len(spare) % 24)
                    dve.tensor_copy(SM[:, spare[-1]:spare[-1] + 1], SM[:, 33:34])

                def top16(sets, values_, replaced, vals, idx):
                    bear()
                    for s_ in sets:
                        m = dve.max(vals(s_)[:, 0:8], values_(s_))
                    m.then_inc(chain, 1)
                    dve.wait_ge(chain, T.next(chain))
                    bear()
                    for s_ in sets:
                        dve.max_index(idx(s_)[:, 0:8], vals(s_)[:, 0:8], values_(s_))
                        m = dve.match_replace(replaced(s_), vals(s_)[:, 0:8], values_(s_), -3.0e38)
                    m.then_inc(chain, 1)
                    dve.wait_ge(chain, T.next(chain))
                    bear()
                    for s_ in sets:
                        m = dve.max(vals(s_)[:, 8:16], replaced(s_))
                    m.then_inc(chain, 1)
                    dve.wait_ge(chain, T.next(chain))
                    bear()
                    for s_ in sets:
                        m = dve.max_index(idx(s_)[:, 8:16], vals(s_)[:, 8:16], replaced(s_))
                    m.then_inc(chain, 1)
                    dve.wait_ge(chain, T.next(chain))

                top16(four, lambda s_: SC[:, s_[0], s_[1], :], lambda s_: SCR[:, s_[0], s_[1], :],
                      lambda s_: TV[:, s_[0], s_[1], :], lambda s_: TIX[:, s_[0], s_[1], :])
                dve.tensor_copy(TIF[:], TIX[:])
                for t in range(NT):
                    m = TT(view(CAND[:, t, :], 16, 16), inner(TV[:, t, 0, :], 16), outer(TV[:, t, 1, :], 16), ALU.add)
                m.then_inc(chain, 1)
                dve.wait_ge(chain, T.next(chain))
                top16(range(NT), lambda t: CAND[:, t, :], lambda t: CANDR[:, t, :], lambda t: BV[:, t, :], lambda t: BP[:, t, :])
                dve.tensor_single_scalar(PA[:], BP[:], 4, ALU.logical_shift_right)
                dve.tensor_single_scalar(PB[:], BP[:], 15, ALU.bitwise_and).then_inc(chain, 1)
                dve.wait_ge(chain, T.next(chain))
                dve.tensor_copy(PAF[:], PA[:])
                dve.tensor_copy(PBF[:], PB[:]).then_inc(chain, 1)
                dve.wait_ge(chain, T.next(chain))
                for q, where in ((0, PAF), (1, PBF)):
                    for t in range(NT):
                        m = TT(view(OH[:, t, :], 16, 16), inner(where[:, t, :], 16), outer(const("iota16"), 16), ALU.is_equal)
                    m.then_inc(chain, 1)
                    dve.wait_ge(chain, T.next(chain))
                    for t in range(NT):
                        m = TT(view(OH[:, t, :], 16, 16), view(OH[:, t, :], 16, 16), outer(TIF[:, t, q, :], 16), ALU.mult)
                    m.then_inc(chain, 1)
                    dve.wait_ge(chain, T.next(chain))
                    dve.tensor_reduce(where[:].rearrange("p t k -> p (t k)"), OH[:].rearrange("p t (k b) -> p (t k) b", b=16), AX, ALU.add).then_inc(chain, 1)
                    dve.wait_ge(chain, T.next(chain))
                STT(PAF[:], PAF[:], float(P), PBF[:], ALU.mult, ALU.add).then_inc(chain, 1)
                dve.wait_ge(chain, T.next(chain))
                dve.tensor_copy(EXU[:, :, ds(h * 16, 16)], PAF[:]).then_inc(sem("expert_ready"), 1)
                TT(BSX[:], BV[:], BV[:, :, 0:1].to_broadcast([P, NT, 16]), ALU.subtract).then_inc(sem("best_ready"), 1)

            def dots():
                for t in range(NT):
                    for j in range(RING):
                        dve.wait_ge(gathered[j], T.next(gathered[j], 16))
                        STT(ring(j), ring(j), 1.0, V[:, t, :], ALU.mult, ALU.mult, accum_out=DOT[:, t, j:j + 1]).then_inc(ring_used[j], 1)

            def weigh(h):
                dve.wait_ge(sem("gate_exp"), T.next(sem("gate_exp")))
                dve.tensor_reduce(GS[:, 0:NT], GX[:], AX, ALU.add).then_inc(chain, 1)
                dve.wait_ge(chain, T.next(chain))
                dve.reciprocal(GS[:, 0:NT], GS[:, 0:NT]).then_inc(chain, 1)
                dve.wait_ge(chain, T.next(chain))
                TT(GX[:], GX[:], inner(GS[:, 0:NT], TOPK), ALU.mult).then_inc(chain, 1)
                dve.wait_ge(chain, T.next(chain))
                dve.wait_ge(sem("gelu_ready"), T.next(sem("gelu_ready")))
                TT(AV[:, :, ds(h * TOPK, TOPK)], AX_[:], GX[:], ALU.mult).then_inc(sem("av_ready"), 1)

            def skip_v():
                for j in range(RING):
                    T.add(gathered[j], 16 * NT)

            route(0)
            dots()
            weigh(0)
            route(1)
            with T.loop("peer", PH - 2) as i:
                dots()
                weigh(i + 1)
                skip_v()
                route(i + 2)
            dots()
            weigh(PH - 1)
            residual(lambda c, t: 2 * t + c)
            scaled(H, D).then_inc(chain, 1)
            dve.wait_ge(chain, T.next(chain))
            dve.wait_ge(sem("rowg_here"), T.next(sem("rowg_here"), 16))
            TT(XS[:], XS[:], outer(ROWG[:], NT), ALU.mult).then_inc(sem("result"), 1)


PER_ITER = {
    "sp:fox": dict(slot_used0=1, slot_used1=1),
    "sp:ffn0": dict(slot_used0=1, slot_used1=1, slot_used2=1, slot_used3=1),
    "sp:mla": dict(slot_used0=1, slot_used1=1),
    "sp:ffn1": dict(slot_used0=1, slot_used1=1, slot_used2=1, slot_used3=1),
    "sp:sb": dict(slot_used0=1, slot_used1=1),
    "sp:cross": dict(slot_used0=1, slot_used1=1),
    "sp:route": dict(slot_used0=1, slot_used1=1),
    "pe:fox": dict(free_v1=1, free_v2=1, slot_here0=16, slot_here1=16, free_a0=1, probs_ready=2, free_a3=2, free_v4=1,
        free_a5=1),
    "pe:ffn0": dict(gu_split0=1, free_v4=1, gu_split1=1, free_v5=1, dn_split0=1, dn_split1=1),
    "pe:mla": dict(free_v1=1, free_v2=1, slot_here0=16, free_a0=1, slot_here1=16, free_a6=1, free_v7=1, probs_ready=2,
        free_a3=2, free_v4=1, free_a5=1),
    "pe:ffn1": dict(gu_split0=1, free_v4=1, gu_split1=1, free_v5=1, dn_split0=1, dn_split1=1),
    "pe:sb": dict(free_v1=1, free_v2=1, slot_here0=16, slot_here1=16, free_a0=1, keep_ready=2, free_v3=1, free_v4=1,
        probs_ready=2, free_v5=1, free_a6=1),
    "pe:cross": dict(free_v1=1, slot_here0=16, free_a0=1, slot_here1=16, free_a6=1, probs_ready=1, free_a3=1, free_v4=1,
        free_a5=1),
    "pe:peer": dict(slot_here0=32, free_a4=1, free_a5=1, slot_here1=16, free_v6=1, free_v7=1, gathered0=64, gathered1=64,
        gathered2=64, gathered3=64, gathered4=64, gathered5=64, gathered6=64, gathered7=64, gathered8=64,
        gathered9=64, gathered10=64, gathered11=64, gathered12=64, gathered13=64, gathered14=64, gathered15=64,
        diag_ready=32),
    "act:fox": dict(max_ready=2, full_a0=1, full_a3=2, full_a5=1),
    "act:ffn0": dict(full_a4=1, raw_here0=32, full_a5=1, raw_here1=32, raw_here2=16, dn_used0=1, raw_here3=16, dn_used1=1),
    "act:mla": dict(max_ready=2, full_a0=1, full_a6=1, full_a3=2, full_a5=1),
    "act:ffn1": dict(full_a4=1, raw_here0=32, full_a5=1, raw_here1=32, raw_here2=16, dn_used0=1, raw_here3=16, dn_used1=1),
    "act:sb": dict(absz_ready=2, act_chain=2, full_a0=1, expo_ready=2, full_a6=1),
    "act:cross": dict(max_ready=1, full_a0=1, full_a6=1, full_a3=1, full_a5=1),
    "act:peer": dict(full_a4=1, full_a5=1, ring_used0=4, ring_used1=4, ring_used2=4, ring_used3=4, ring_used4=4, ring_used5=4,
        ring_used6=4, ring_used7=4, ring_used8=4, ring_used9=4, ring_used10=4, ring_used11=4, ring_used12=4,
        ring_used13=4, ring_used14=4, ring_used15=4, av_ready=1, best_ready=1),
    "pool:peer": dict(expert_ready=1, ring_used0=4, ring_used1=4, ring_used2=4, ring_used3=4, pool_chain=16, ring_used4=4,
        ring_used5=4, ring_used6=4, ring_used7=4, ring_used8=4, ring_used9=4, ring_used10=4, ring_used11=4,
        ring_used12=4, ring_used13=4, ring_used14=4, ring_used15=4),
    "dve:fox": dict(full_v1=1, free_v1=1, full_v2=1, free_v2=1, probs_ready=2, dve_chain=1, full_v4=1, free_v4=1),
    "dve:ffn0": dict(silu_ready=2, dve_chain=4, free_v4=1, high_ready=4, free_v5=1),
    "dve:mla": dict(full_v1=1, free_v1=1, full_v2=1, free_v2=1, full_v7=1, dve_chain=2, free_v7=1, probs_ready=2, full_v4=1,
        free_v4=1),
    "dve:ffn1": dict(silu_ready=2, dve_chain=4, free_v4=1, high_ready=4, free_v5=1),
    "dve:sb": dict(full_v1=1, free_v1=1, full_v2=1, free_v2=1, ln_ready=2, dve_chain=2, full_v3=1, free_v3=1, full_v4=1,
        free_v4=1, full_v5=1, free_v5=1),
    "dve:cross": dict(full_v1=1, free_v1=1, probs_ready=1, dve_chain=1, full_v4=1, free_v4=1),
    "dve:peer": dict(gathered0=64, gathered1=64, gathered2=64, gathered3=64, gathered4=64, gathered5=64, gathered6=64,
        gathered7=64, gathered8=64, gathered9=64, gathered10=64, gathered11=64, gathered12=64, gathered13=64,
        gathered14=64, gathered15=64, gate_exp=1, dve_chain=21, gelu_ready=1, full_v6=1, free_v6=1, full_v7=1,
        free_v7=1),
}

_INS = ["x", "positions", "attn_norm", "ffn_norm", "w_gate", "w_up", "w_down", "fox_w_in", "fox_b_f", "fox_w_o", "kv_norm", "w_kv_a",
        "ckv_norm", "w_uk", "w_uv", "mla_w_dq", "cq_norm", "mla_w_uq", "mla_w_o", "final_norm", "mem_2", "g_mix_2", "w_in_2",
        "gdn_conv_2", "gdn_a_log_2", "gdn_dt_bias_2", "gdn_norm_g_2", "w_sb_up_2", "w_gdn_up_2", "w_mix_out_2", "g_cross_2", "g_mem_2",
        "w_cq_2", "w_ckv_2", "w_co_2", "g_peer_2", "w_pq_2", "peer_subkeys_2", "peer_u_2", "peer_v_2", "g_final_2"]


def kernel(**inputs):
    import concourse.bacc as bacc
    from concourse.bass_utils import run_bass_kernel_spmd

    nc = bacc.Bacc("TRN2", target_bir_lowering=False, num_devices=1)
    arrays, aps = {}, {}
    for name in _INS:
        arrays[f"in_{name}"] = np.ascontiguousarray(inputs[name])
    arrays["in_consts"] = constant_table()
    for name, v in arrays.items():
        aps[name[3:]] = nc.dram_tensor(name, v.shape, mybir.dt.from_np(v.dtype), kind="ExternalInput").ap()
    out = nc.dram_tensor("out_0", (1, S, D), F32, kind="ExternalOutput").ap()
    program(nc, aps, out, PER_ITER)
    r = run_bass_kernel_spmd(nc, [arrays], core_ids=[0])
    return r.results[0]["out_0"]
```

```python
from contextlib import ExitStack, contextmanager

import numpy as np
import concourse.bass as bass
from concourse import mybir

F32, F32R, U32, I32 = mybir.dt.float32, mybir.dt.float32r, mybir.dt.uint32, mybir.dt.int32
ALU, ACT = mybir.AluOpType, mybir.ActivationFunctionType
AX = mybir.AxisListType.X
ds = bass.ds

P = 128
NT = 2
S = NT * P
D = 1024
KC = D // P
DFF = 2816
FB = DFF // P
EPS = 1e-6
NEG = -1e30
TWO_PI = 6.283185307179586
PAIRS = 8
KVR, QR, ROPE, NOPE = 256, 768, 32, 64
SBW, GH, XD = 512, 4, 256
TOPK, PH = 16, 8
PICKS = TOPK * PH
RING = 16
CONV = 4

MLA_SCALE = (NOPE + ROPE) ** -0.5
_C1 = 6.28125
_C2 = float((np.array([TWO_PI - _C1], np.float32).view(np.uint32) & np.uint32(0xFFFFF000)).view(np.float32)[0])
PI_PARTS = (_C1, _C2, TWO_PI - _C1 - _C2)

_COLS = {}
_at = 0
for _n, _w in [("ident", 128), ("ones", 128), ("upto", 128), ("from_", 128), ("blk_upto", 128), ("blk", 128),
               ("half0", 128), ("half1", 128), ("dmask", 128), ("causal", 256), ("sb_neg", 384), ("sb_keep", 384),
               ("lev", 6 * 128), ("levT", 6 * 128), ("rot", 96), ("inv_freq", 1), ("iota16", 16), ("zero", 128)]:
    _COLS[_n] = (_at, _w)
    _at += _w
NCONST = _at


def constant_table():
    c = np.zeros((P, NCONST), np.float32)

    def put(name, a):
        o, w = _COLS[name]
        c[:a.shape[0], o:o + w] = a.reshape(a.shape[0], -1)

    i, j = np.arange(P)[:, None], np.arange(P)[None, :]
    same = i // 64 == j // 64
    put("ident", np.eye(P))
    put("ones", np.ones((P, P)))
    put("upto", (i <= j) * 1.0)
    put("from_", (i >= j) * 1.0)
    put("blk_upto", ((i <= j) & same) * 1.0)
    put("blk", same * 1.0)
    put("half0", np.repeat((i < 64) * 1.0, P, 1))
    put("half1", np.repeat((i >= 64) * 1.0, P, 1))
    put("dmask", np.where((i >= j) & same, 0.0, NEG))
    put("causal", np.concatenate([np.zeros((P, P)), np.where(j <= i, 0.0, NEG)], 1))
    put("sb_neg", np.concatenate([np.where(i < j, 0.0, NEG), np.zeros((P, P)), np.where(i < j, 0.0, NEG)], 1))
    put("sb_keep", -np.concatenate([(i < j) * 1.0, np.ones((P, P)), (i < j) * 1.0], 1))
    lev = [((i // (2 * s) == j // (2 * s)) & (i // s > j // s)) * 1.0 for s in (1, 2, 4, 8, 16, 32)]
    put("lev", np.concatenate(lev, 1))
    put("levT", np.concatenate([a.T for a in lev], 1))
    rot = np.zeros((96, 96))
    for r in range(ROPE // 2):
        rot[NOPE + 16 + r, NOPE + r] = -1.0
        rot[NOPE + r, NOPE + 16 + r] = 1.0
    put("rot", rot)
    inv = np.float32(10000.0) ** (-np.arange(ROPE // 2, dtype=np.float32) * np.float32(2.0) / np.float32(ROPE))
    put("inv_freq", np.concatenate([np.zeros(NOPE), inv, inv])[:, None])
    put("iota16", np.repeat(np.arange(16)[None], P, 0))
    return c


class Tally:

    def __init__(self, eng, name, per_iter):
        self.eng, self.name, self.per_iter = eng, name, per_iter
        self.base, self.local, self.i, self.per = {}, {}, None, {}

    def add(self, sem, n=1):
        if self.i is None:
            self.base[sem] = self.base.get(sem, 0) + n
        else:
            self.local[sem] = self.local.get(sem, 0) + n

    def due(self, sem):
        fixed = self.base.get(sem, 0) + self.local.get(sem, 0)
        per = self.per.get(sem.name, 0) if self.i is not None else 0
        return self.i * per + fixed if per else fixed

    def next(self, sem, n=1):
        self.add(sem, n)
        return self.due(sem)

    @contextmanager
    def loop(self, label, n):
        key = f"{self.name}:{label}"
        self.per = self.per_iter.get(key, {})
        with self.eng.Fori(0, n) as i:
            self.i = i
            yield i
        found = {s.name: k for s, k in self.local.items()}
        self.per_iter[key] = found
        for s, k in self.local.items():
            self.base[s] = self.base.get(s, 0) + n * k
        self.local, self.i, self.per = {}, None, {}


def program(nc, a, out, per_iter):
    with ExitStack() as ctx:
        def sb(name, shape, dt=F32):
            return ctx.enter_context(nc.sbuf_tensor(name, shape, dt))

        sems = {}

        def sem(name):
            if name not in sems:
                sems[name] = ctx.enter_context(nc.semaphore(name))
            return sems[name]

        ctx.enter_context(nc.allow_non_contiguous_dma(reason="small columns and weight blocks"))
        arena_at = -(-nc.sbuf_base // 32) * 32
        AR = sb("AR", [P, 18200])
        ARH = nc.alloc_sbuf_tensor_at("ARH", [P, 17408], F32R, offset=arena_at)
        ps = ctx.enter_context(nc.psum_tensor("ps", [P, 8, 512], F32))
        CT = sb("CT", [P, NCONST])
        SLOT = [sb(f"SLOT{s}", [P, 4096]) for s in range(4)]
        H = sb("H", [P, NT, D])
        XS = sb("XS", [P, NT, D])
        XT = sb("XT", [P, KC, S])
        XT2 = sb("XT2", [P, KC, S])
        V = sb("V", [P, NT, D])
        OT = sb("OT", [P, KC, S])
        ROWG = sb("ROWG", [P, D])
        GCOL = sb("GCOL", [P, P])
        WF = sb("WF", [P, KC, 16])
        SS = sb("SS", [P, 16])
        RS = sb("RS", [P, 16])
        BF = sb("BF", [P, 16])
        SM = sb("SM", [P, 64])

        def const(name, rows=P):
            o, w = _COLS[name]
            return CT[0:rows, o:o + w]

        IDENT = const("ident")

        def arena(off, *shape, parts=P):
            n = int(np.prod(shape))
            v = AR[0:parts, off:off + n]
            assert off + n <= 18200, (off, n)
            if len(shape) == 1:
                return v
            names = "abcde"[:len(shape)]
            return v.rearrange(f"p ({' '.join(names)}) -> p {' '.join(names)}", **{m: k for m, k in zip(names, shape)})

        def halves(off, *shape):
            return view(ARH[:, off:off + int(np.prod(shape))], *shape)

        def view(x, *shape):
            names = "abcde"[:len(shape)]
            return x.rearrange(f"p ({' '.join(names)}) -> p {' '.join(names)}", **{m: k for m, k in zip(names, shape)})

        QT = arena(0, 2, S)
        KT = arena(512, 2, S)
        LG = arena(1024, 2, 512)
        PR = arena(2048, 2, 512)
        PT = arena(3072, 2, 512)
        ON = arena(4096, 2, 128)
        NEGCUM = arena(4608, 4096, parts=1)
        LF = arena(8704, NT, 16)
        LF2 = arena(8736, NT, 16)
        CQ = arena(8768, NT, 16)
        CUMT = arena(8800, S, parts=16)
        QRAW = arena(9056, 2, S)
        COS = arena(9568, 2, S)
        SIN = arena(10080, 2, S)
        WPAD = arena(10592, KC, 96)
        KVA = arena(11360, NT, 768)
        CKT = arena(12896, 2, S)
        CQT = arena(13408, 6, S)
        KRT = arena(14944, S)
        ANG = arena(15200, 4, S)
        SG = arena(17408, 2, S)
        WGU = halves(0, 2, 2, 2, KC, P)
        WDN = halves(8192, 2, 2, D)
        XH = halves(12288, 2, KC, S)
        HT = halves(16384, 2, 2, S)
        DG = arena(17920, NT, P)
        PRE = arena(0, 12, S + CONV - 1)
        G = arena(3108, 12, S)
        SQ = arena(6180, 8, S)
        KBG, VB = arena(0, NT, 512), arena(1024, NT, 512)
        KD = arena(6180, NT, 512)
        DEC = arena(8228, NT, 512)
        AA, AT = arena(9252, NT, 512), arena(10276, NT, 512)
        TI_, UI = arena(11300, NT, 512), arena(12324, NT, 512)
        LT, PP = arena(13348, NT, 512), arena(14372, NT, 512)
        ER, QK = LT, PP
        QKT = arena(2048, NT, 512)
        QD = arena(15396, NT, 512)
        WT = arena(16420, NT, 512)
        UU = arena(7204, NT, 512)
        ST = arena(17444, 512)
        VN, OI = view(ROWG[:], NT, 512), V[:, :, 0:512]
        GT = (view(XT2[:].rearrange("p a b -> p (a b)"), NT, D), XS)
        MG = arena(4096, NT, D)
        MEM = arena(8192, NT, D)
        ONX = arena(4096, NT, XD)
        QP, SKT = arena(0, 2, S), arena(512, 2, P)
        SC, SCR = arena(768, NT, 2, P), arena(1280, NT, 2, P)
        TV, TIF = arena(1792, NT, 2, 16), arena(1920, NT, 2, 16)
        CAND, CANDR = arena(1984, NT, 256), arena(2496, NT, 256)
        BV, PAF, PBF = arena(3008, NT, 16), arena(3104, NT, 16), arena(3136, NT, 16)
        OH = arena(3300, NT, 256)
        DOT, AV = arena(5024, NT, TOPK), arena(5280, NT, PICKS)
        GS = arena(5536, NT * PH)
        GX, AX_, BSX = arena(4000, NT, TOPK), arena(4032, NT, TOPK), arena(4064, NT, TOPK)
        SUBK = arena(10000, 2, P)
        PW = view(XT2[:].rearrange("p a b -> p (a b)"), 2, KC, P)
        DIAG = arena(7700, RING, P)
        SHARED = range(3, RING, 4)
        TIX, BP, PA, PB = (sb(n_, s_, U32) for n_, s_ in (("TIX", [P, NT, 2, 16]), ("BP", [P, NT, 16]), ("PA", [P, NT, 16]), ("PB", [P, NT, 16])))
        EXU, IX = sb("EXU", [P, NT, PICKS], U32), sb("IX", [P, RING], U32)
        BA, BT, BE = sb("BA", [P, NT, 8]), sb("BT", [P, NT, 4]), sb("BE", [P, NT, 4])
        SMALL = sb("SMALL", [P, 128])
        GSM, AEXP, GDNG = SMALL[:, 0:8], SMALL[:, 8:12], SMALL[:, 12:13]
        GZ, GL, GG = (view(SMALL[:, 16 + 8 * n_:24 + 8 * n_], NT, 4) for n_ in range(3))
        RAW, EX = SMALL[:, 40:72], SMALL[:, 72:104]
        PSCR = sb("PSCR", [P, 16])
        ASCR = sb("ASCR", [P, 64])
        POSI = sb("POSI", [P, S], I32)

        full = {r: [sem(f"full_{r}{b}") for b in range(8)] for r in "va"}
        free = {r: [sem(f"free_{r}{b}") for b in range(8)] for r in "va"}
        here = [sem(f"slot_here{s}") for s in range(4)]
        used = [sem(f"slot_used{s}") for s in range(4)]

        raw_here = [sem(f"raw_here{s}") for s in range(4)]
        ring_used = [sem(f"ring_used{j}") for j in range(RING)]
        gathered = [sem(f"gathered{j}") for j in range(RING)]

        def inner(x, n):
            shape = list(x.shape)
            names = "abc"[:len(shape) - 1]
            lhs = " ".join(names[:-1]) + f" ({names[-1]} o)"
            return x.rearrange(f"p {lhs} -> p {' '.join(names)} o", o=1).to_broadcast(shape + [n])

        def outer(x, n):
            return x.rearrange("p (o m) -> p o m", o=1).to_broadcast([x.shape[0], n, x.shape[1]])

        def hd(X, t, h):
            return X[:, t, h * P:(h + 1) * P]

        def ring(j):
            return SLOT[j // 4][:, (j % 4) * D:(j % 4 + 1) * D]

        g_at = dict(attn0=0, attn1=8, ffn0=16, ffn1=24, kv=32, ckv=40, cq=42, mix=48, cross=56, mem=64, peer=72, conv=80)

        def gcol(name, k, n):
            o = g_at[name] + k
            return GCOL[:, o:o + n]

        def rows(w, c0, c1):
            return w[:, c0:c1].rearrange("(k p) n -> p k n", p=P)

        x_in, mem_in = a["x"][0].rearrange("(t p) d -> p t d", p=P), a["mem_2"][0].rearrange("(t p) d -> p t d", p=P)
        fw = a["fox_w_in"][0]
        w_in = a["w_in_2"][0]
        w_uk = a["w_uk"].rearrange("(k p) h d -> p k (h d)", p=P)
        w_uv = a["w_uv"].rearrange("(k p) h d -> p k (h d)", p=P)
        w_uq = a["mla_w_uq"][0]
        w_dq = a["mla_w_dq"][0].rearrange("(k p) n -> p k n", p=P)
        subkeys = a["peer_subkeys_2"][0].rearrange("h q n d -> n (h q) d")

        def flat_rows(x):
            while len(x.shape) > 1:
                x = x.rearrange("a b -> (a b)") if len(x.shape) == 2 else x.rearrange("a b c -> (a b c)")
            return x.rearrange("(r c) -> r c", c=P)

        GAINS = [(n_, flat_rows(a[src])) for n_, src in (
            ("attn0", "attn_norm"), ("ffn0", "ffn_norm"), ("kv", "kv_norm"), ("ckv", "ckv_norm"), ("cq", "cq_norm"), ("mix", "g_mix_2"),
            ("cross", "g_cross_2"), ("mem", "g_mem_2"), ("peer", "g_peer_2"), ("conv", "gdn_conv_2"))]

        block = ctx.enter_context(nc.Block())

        @block.sync
        def _(sp):
            T = Tally(sp, "sp", per_iter)

            def fill(s, *pairs, arrival=here):
                sp.wait_ge(used[s], T.due(used[s]))
                for dst, src in pairs:
                    sp.dma_start(dst, src).then_inc(arrival[s], 16)
                T.add(used[s])

            def slot(s, *shape):
                return view(SLOT[s][:, 0:int(np.prod(shape))], *shape)

            def row_gain(src):
                sp.wait_ge(sem("rowg_used"), T.due(sem("rowg_used")))
                sp.dma_start(ROWG[:], src.to_broadcast([P, D])).then_inc(sem("rowg_here"), 16)
                T.add(sem("rowg_used"))

            def qk(q_src, k_src):
                fill(0, (slot(0, q_src.shape[1], q_src.shape[2]), q_src))
                fill(1, (slot(1, k_src.shape[1], k_src.shape[2]), k_src))

            def dyn(w, off, n=P):
                return w[:, ds(off, n)].rearrange("(k p) n -> p k n", p=P)

            def two_tiles(w, c0=0):
                for c in range(2):
                    fill(2 + c, (slot(2 + c, KC, 512), rows(w, c0 + 512 * c, c0 + 512 * c + 512)))

            def ffn(l):
                wg, wu, wd = a["w_gate"][l], a["w_up"][l], a["w_down"][l]
                with T.loop(f"ffn{l}", FB // 2) as i:
                    for b in range(2):
                        w = slot(b, 2, KC, P)
                        fill(b, (w[:, 0], dyn(wg, i * 256 + b * P)), (w[:, 1], dyn(wu, i * 256 + b * P)), arrival=raw_here)
                    for b in range(2):
                        fill(2 + b, (SLOT[2 + b][:, 0:D], wd[ds(i * 256 + b * P, P), :]), arrival=raw_here)

            sp.dma_start(IDENT, a["consts"][:, 0:P]).then_inc(sem("ident_here"), 16)
            sp.dma_start(H[:], x_in).then_inc(sem("x_here"), 16)
            for name, src in GAINS:
                r0 = g_at[name]
                sp.dma_start(SLOT[0][r0:r0 + src.shape[0], 0:P], src).then_inc(here[0], 16)
            T.add(used[0])
            sp.dma_start(WF[:], rows(fw, 3072, 3088)).then_inc(sem("wf_here"), 16)
            sp.dma_start(BF[:], a["fox_b_f"].to_broadcast([P, 16])).then_inc(sem("wf_here"), 16)
            fill(2, (slot(2, KC, 512), rows(fw, 2048, 2560)))
            sp.dma_start(CT[:, P:], a["consts"][:, P:]).then_inc(sem("const_here"), 16)
            fill(3, (slot(3, KC, 512), rows(fw, 2560, 3072)))
            sp.wait_ge(sem("cumt_ready"), 1)
            sp.dma_start(NEGCUM[0:1, :], CUMT).then_inc(sem("negcum_here"), 16)
            qk(rows(fw, 0, P), rows(fw, D, D + P))
            with T.loop("fox", PAIRS - 1) as i:
                qk(dyn(fw, i * P + P), dyn(fw, i * P + (D + P)))
            two_tiles(a["fox_w_o"][0])
            ffn(0)
            fill(0, (slot(0, KC, 288), rows(a["w_kv_a"], 0, 288)))
            sp.dma_start(POSI[0:96, :], a["positions"].to_broadcast([96, S])).then_inc(sem("pos_here"), 16)
            fill(1, (slot(1, 4, QR), w_dq[:, 0:4, :]))
            fill(2, (slot(2, 4, QR), w_dq[:, 4:8, :]))
            fill(3, (slot(3, 2, D), w_uv))
            qk(rows(w_uq, 0, 192), w_uk[:, :, 0:P])
            with T.loop("mla", PAIRS - 1) as i:
                qk(dyn(w_uq, i * 192 + 192, 192), w_uk[:, :, ds(i * P + P, P)])
            two_tiles(a["mla_w_o"][0])
            ffn(1)
            row_gain(a["final_norm"].rearrange("(o d) -> o d", o=1))
            fill(2, (slot(2, KC, 512), rows(w_in, 1024, 1536)))
            qk(rows(w_in, 0, P), rows(w_in, SBW, SBW + P))
            with T.loop("sb", 3) as i:
                qk(dyn(w_in, i * P + P), dyn(w_in, i * P + (SBW + P)))
            for n_, s_ in enumerate((3, 2, 3)):
                fill(s_, (slot(s_, KC, 512), rows(w_in, 1536 + 512 * n_, 2048 + 512 * n_)))
            fill(2, (slot(2, KC, 512), rows(w_in, 3072, 3584)))
            sp.wait_ge(used[0], T.due(used[0]))
            fill(0, (slot(0, KC, 8), rows(w_in, 3584, 3592)))
            for k_, name in enumerate(("gdn_a_log_2", "gdn_dt_bias_2")):
                sp.dma_start(GSM[:, 4 * k_:4 * k_ + 4], a[name].to_broadcast([P, 4])).then_inc(sem("gsm_here"), 16)
            sp.dma_start(GDNG, a["gdn_norm_g_2"].rearrange("o d -> d o")).then_inc(sem("gsm_here"), 16)
            for n_, s_ in enumerate((3, 2, 3, 2)):
                fill(s_, (slot(s_, KC, 512), rows(w_in, 3592 + 512 * n_, 4104 + 512 * n_)))
            fill(0, (slot(0, 4, D), a["w_sb_up_2"][0].rearrange("(k p) n -> p k n", p=P)))
            fill(1, (slot(1, 4, D), a["w_gdn_up_2"][0].rearrange("(k p) n -> p k n", p=P)))
            two_tiles(a["w_mix_out_2"][0])
            wckv, wcq = a["w_ckv_2"][0], a["w_cq_2"][0]
            sp.wait_ge(sem("merged_ready"), 1)
            sp.dma_start(MEM, mem_in).then_inc(sem("mem_here"), 16)
            two_tiles(wckv, D)
            qk(rows(wcq, 0, XD), rows(wckv, 0, XD))
            with T.loop("cross", 3) as i:
                qk(dyn(wcq, i * XD + XD, XD), dyn(wckv, i * XD + XD, XD))
            two_tiles(a["w_co_2"][0])
            row_gain(a["g_peer_2"])
            def head_weights(h):
                wq = a["w_pq_2"][0]
                fill(0, *((PW[:, q], dyn(wq, h * 256 + q * P)) for q in range(2)))
                fill(1, (SUBK[:], subkeys[:, ds(h * 2, 2), :]))

            sp.wait_ge(used[1], T.due(used[1]))
            head_weights(0)
            with T.loop("route", PH - 1) as i:
                head_weights(i + 1)
            row_gain(a["g_final_2"].rearrange("(o d) -> o d", o=1))
            sp.wait_ge(sem("result"), 1)
            sp.dma_start(out[0].rearrange("(t p) d -> p t d", p=P), XS[:]).then_inc(sem("out_done"), 16)
            sp.wait_ge(sem("out_done"), 16)

        @block.tensor
        def _(pe):
            T = Tally(pe, "pe", per_iter)
            pending = []

            def first(ins):
                if pending:
                    ins.then_inc(pending.pop(0), 1)

            def take(*banks):
                for b in banks:
                    pe.wait_ge(free["v"][b], T.due(free["v"][b]))
                    pe.wait_ge(free["a"][b], T.due(free["a"][b]))

            evacuated = take

            def release(s):
                pending.append(used[s])

            def flush():
                for _ in range(len(pending)):
                    take(7)
                    first(pe.matmul(ps[:, 7, 0:1], const("zero"), CT[:, 0:1], start=True, stop=True))

            def group(outp, pairs):
                pairs = list(pairs)
                for n_, (l, r) in enumerate(pairs):
                    m = pe.matmul(outp, l, r, start=(n_ == 0), stop=(n_ == len(pairs) - 1))
                    if n_ < len(pairs) - 1:
                        first(m)
                return m

            def tr(outp, src):
                return pe.transpose(outp, src, IDENT)

            def slot(s, *shape):
                return view(SLOT[s][:, 0:int(np.prod(shape))], *shape)

            def transposes(src, n_chunks, banks=(0, 1, 2, 3)):
                for g in range(n_chunks // 2):
                    b = banks[g % len(banks)]
                    take(b)
                    for n_ in range(4):
                        m = tr(ps[:, b, n_ * P:(n_ + 1) * P], src(n_ % 2, 2 * g + n_ // 2))
                        if n_ < 3:
                            first(m)
                    m.then_inc(full["v"][b], 1)
                    T.add(free["v"][b])

            def turned(src, n_chunks, banks=(0, 1, 2, 3)):
                pe.wait_ge(sem("xs_ready"), T.next(sem("xs_ready")))
                for g in range(n_chunks // 2):
                    b = banks[g % len(banks)]
                    take(b)
                    for n_ in range(4):
                        k = 2 * g + n_ // 2
                        m = pe.matmul(ps[:, b, n_ * P:(n_ + 1) * P], src[:, n_ % 2, k * P:(k + 1) * P], DG[:, n_ % 2, :], start=True, stop=True)
                        if n_ < 3:
                            first(m)
                    m.then_inc(full["v"][b], 1)
                    T.add(free["v"][b])

            def norm_t():
                turned(H, KC)
                evacuated(0, 1, 2, 3)

            def cols(X, t, k):
                return X[:, k, t * P:(t + 1) * P]

            def row_tile(s, banks, X, n=512, reader="v"):
                pe.wait_ge(here[s], T.next(here[s], 16))
                w = slot(s, KC, n)
                for t in range(NT):
                    take(banks[t])
                    group(ps[:, banks[t], 0:n], ((cols(X, t, k), w[:, k, :]) for k in range(KC))).then_inc(full[reader][banks[t]], 1)
                    T.add(free[reader][banks[t]])
                release(s)

            def out_proj(X, bank):
                evacuated(bank)
                for c in range(2):
                    row_tile(2 + c, (2 * c, 2 * c + 1), X)

            def out_begin(ready):
                pe.wait_ge(here[2], T.next(here[2], 16))
                for t in range(NT):
                    take(6 + t)
                    for k in range(ready):
                        first(pe.matmul(ps[:, 6 + t, :], cols(OT, t, k), slot(2, KC, 512)[:, k, :], start=(k == 0), stop=False))

            def out_end(ready, bank):
                evacuated(bank)
                for t in range(NT):
                    for k in range(ready, KC):
                        m = pe.matmul(ps[:, 6 + t, :], cols(OT, t, k), slot(2, KC, 512)[:, k, :], start=False, stop=(k == KC - 1))
                    m.then_inc(full["v"][6 + t], 1)
                    T.add(free["v"][6 + t])
                release(2)
                row_tile(3, (2, 3), OT)

            def qk_part(s_):
                if s_ == 0:
                    take(0)
                pe.wait_ge(here[s_], T.next(here[s_], 16))
                m = group(ps[:, 0, s_ * S:(s_ + 1) * S], ((slot(s_, KC, P)[:, k, :], XT[:, k, :]) for k in range(KC)))
                release(s_)
                if s_ == 1:
                    m.then_inc(full["a"][0], 1)
                    T.add(free["a"][0])

            def qk_proj():
                qk_part(0)
                qk_part(1)

            def flip(hh):
                pe.wait_ge(sem("probs_ready"), T.next(sem("probs_ready")))
                take(3 + hh)
                for n_ in range(3):
                    m = tr(ps[:, 3 + hh, n_ * P:(n_ + 1) * P], PR[:, hh, n_ * P:(n_ + 1) * P])
                    if n_ < 2:
                        first(m)
                m.then_inc(full["a"][3 + hh], 1)
                T.add(free["a"][3 + hh])

            def mix_values(i, hh):
                evacuated(3 + hh)
                if hh == 0:
                    take(5)
                v0, v1 = (V[:, kt, ds((i * 2 + hh) * 64, 64)] for kt in range(2))
                group(ps[:, 5, hh * 64:hh * 64 + 64], [(PT[:, hh, 0:P], v0)])
                m = group(ps[:, 5, P + hh * 64:P + hh * 64 + 64], [(PT[:, hh, P:2 * P], v0), (PT[:, hh, 2 * P:3 * P], v1)])
                if hh == 1:
                    m.then_inc(full["v"][5], 1)
                    T.add(free["v"][5])

            def turn():
                evacuated(5)
                take(2)
                for t in range(NT):
                    m = tr(ps[:, 2, t * P:(t + 1) * P], ON[:, t, :])
                m.then_inc(full["a"][2], 1)
                T.add(free["a"][2])

            def attend(i, turn_before=True):
                flip(0)
                flip(1)
                mix_values(i, 0)
                if turn_before:
                    turn()
                mix_values(i, 1)

            def thirds(l, r):
                return [(l(0), r(0)), (l(0), r(1)), (l(1), r(0))]

            def ffn(l):
                norm_t()
                for b in range(4):
                    take(b)
                    first(pe.matmul(ps[:, b, :], const("zero"), XT[:, 0:2, :], start=True, stop=False))
                pe.wait_ge(sem("xh_ready"), T.next(sem("xh_ready")))
                assert not pending
                with T.loop(f"ffn{l}", FB // 2) as i:
                    for b in range(2):
                        pe.wait_ge(sem(f"gu_split{b}"), T.next(sem(f"gu_split{b}")))
                        take(4 + b)
                        for g in range(2):
                            m = group(ps[:, 4 + b, g * S:(g + 1) * S],
                                      sum((thirds(lambda h: WGU[:, b, h, g, k, :], lambda h: XH[:, h, k, :]) for k in range(KC)), []))
                        m.then_inc(full["a"][4 + b], 1)
                        T.add(free["v"][4 + b])
                    for b in range(2):
                        pe.wait_ge(sem(f"dn_split{b}"), T.next(sem(f"dn_split{b}")))
                        evacuated(4 + b)
                        for t in range(NT):
                            for c in range(2):
                                for l_, r_ in thirds(lambda h: HT[:, b, h, t * P:(t + 1) * P], lambda h: WDN[:, b, h, c * 512:(c + 1) * 512]):
                                    m = pe.matmul(ps[:, 2 * t + c, :], l_, r_, start=False, stop=False)
                        m.then_inc(sem(f"dn_used{b}"), 1)
                for b in range(4):
                    pe.matmul(ps[:, b, 0:1], const("zero"), XT[:, 0, 0:1], start=False, stop=True).then_inc(full["v"][b], 1)
                    T.add(free["v"][b])

            pe.wait_ge(sem("ident_here"), T.next(sem("ident_here"), 16))
            T.add(free["a"][3])
            T.add(free["a"][5])
            T.add(free["a"][2])
            pe.wait_ge(here[0], T.next(here[0], 16 * len(GAINS)))
            take(0)
            tr(ps[:, 0, 0:P], SLOT[0][:, 0:P]).then_inc(full["v"][0], 1)
            T.add(free["v"][0])
            release(0)
            norm_t()
            pe.wait_ge(sem("wf_here"), T.next(sem("wf_here"), 32))
            take(4)
            for t in range(NT):
                m = group(ps[:, 4, 16 * t:16 * t + 16], ((cols(XT, t, k), WF[:, k, :]) for k in range(KC)))
            m.then_inc(full["v"][4], 1)
            T.add(free["v"][4])
            row_tile(2, (0, 1), XT)
            pe.wait_ge(sem("logf_ready"), T.next(sem("logf_ready")))
            pe.wait_ge(sem("const_here"), T.next(sem("const_here"), 16))
            take(4)
            group(ps[:, 4, 0:16], [(const("upto"), LF[:, 0, :])])
            m = group(ps[:, 4, 16:32], [(const("upto"), LF[:, 1, :]), (const("ones"), LF[:, 0, :])])
            m.then_inc(full["v"][4], 1)
            T.add(free["v"][4])
            evacuated(4)
            take(5)
            for t in range(NT):
                m = tr(ps[0:16, 5, t * P:(t + 1) * P], CQ[:, t, :])
            m.then_inc(full["v"][5], 1)
            T.add(free["v"][5])
            row_tile(3, (2, 3), XT)
            evacuated(2, 3)

            def fox_scores(i):
                evacuated(0)
                one = const("ones")[0:1, :]
                for hh in range(2):
                    take(1 + hh)
                    r = slice(64 * hh, 64 * hh + 64)
                    for c0, q, n in ((0, 0, P), (P, P, S)):
                        first(pe.matmul(ps[:, 1 + hh, c0:c0 + n], one, NEGCUM[0:1, ds((i * 2 + hh) * S, n)], start=True, stop=False))
                        m = pe.matmul(ps[:, 1 + hh, c0:c0 + n], QT[r, 0, q:q + P], KT[r, 0, 0:n], start=False, stop=True)
                    m.then_inc(full["v"][1 + hh], 1)
                    T.add(free["v"][1 + hh])

            qk_proj()
            pe.wait_ge(sem("negcum_here"), T.next(sem("negcum_here"), 16))
            flush()
            assert not pending
            fox_scores(0)
            qk_proj()
            attend(0, turn_before=False)
            assert not pending
            with T.loop("fox", PAIRS - 2) as i:
                fox_scores(i + 1)
                qk_proj()
                attend(i + 1)
                assert not pending
            fox_scores(PAIRS - 1)
            out_begin(PAIRS - 2)
            attend(PAIRS - 1)
            turn()
            out_end(PAIRS - 2, 2)
            ffn(0)
            norm_t()
            pe.wait_ge(sem("wpad_here"), T.next(sem("wpad_here"), 17))
            take(4)
            group(ps[0:96, 4, 0:S], ((WPAD[:, k, :], XT2[:, k, :]) for k in range(KC))).then_inc(full["a"][4], 1)
            T.add(free["a"][4])
            pe.wait_ge(here[0], T.next(here[0], 16))
            for t in range(NT):
                take(t)
                group(ps[:, t, 0:KVR], ((cols(XT2, t, k), slot(0, KC, 288)[:, k, 0:KVR]) for k in range(KC))).then_inc(full["a"][t], 1)
                T.add(free["a"][t])
            release(0)
            pe.wait_ge(here[1], T.next(here[1], 16))
            pe.wait_ge(here[2], T.next(here[2], 16))
            for t in range(NT):
                for c in range(2):
                    b = (2, 3, 6, 7)[2 * t + c]
                    take(b)
                    group(ps[:, b, 0:384], ((cols(XT, t, k), slot(1 + k // 4, 4, QR)[:, k % 4, 384 * c:384 * c + 384])
                                                 for k in range(KC))).then_inc(full["a"][b], 1)
                    T.add(free["a"][b])
            release(1)
            release(2)
            evacuated(4)
            take(5)
            pe.matmul(ps[0:96, 5, 0:S], const("rot", 96), KRT[0:96, :], start=True, stop=True).then_inc(full["v"][5], 1)
            T.add(free["v"][5])
            turned(KVA, 2)
            evacuated(0)
            pe.wait_ge(here[3], T.next(here[3], 16))
            for c in range(2):
                for t in range(NT):
                    b = (4, 5)[t]
                    take(b)
                    group(ps[:, b, :], ((cols(CKT, t, k), slot(3, 2, D)[:, k, 512 * c:512 * c + 512]) for k in range(2))).then_inc(full["v"][b], 1)
                    T.add(free["v"][b])
            release(3)
            turned(KVA, 6, (0, 1, 2))
            evacuated(0, 1, 2, 4, 5)

            def mla_proj():
                pe.wait_ge(here[0], T.next(here[0], 16))
                take(0)
                for hh in range(2):
                    m = group(ps[0:96, 0, hh * S:(hh + 1) * S], ((slot(0, 6, 192)[:, k, 96 * hh:96 * hh + 96], CQT[:, k, :]) for k in range(6)))
                release(0)
                m.then_inc(full["a"][0], 1)
                T.add(free["a"][0])
                pe.wait_ge(here[1], T.next(here[1], 16))
                take(6)
                for hh in range(2):
                    m = group(ps[0:64, 6, hh * S:(hh + 1) * S], ((slot(1, 2, P)[:, k, 64 * hh:64 * hh + 64], CKT[:, k, :]) for k in range(2)))
                release(1)
                m.then_inc(full["a"][6], 1)
                T.add(free["a"][6])
                take(7)
                evacuated(0)
                first(pe.matmul(ps[0:96, 7, 0:S], const("rot", 96), QRAW[0:96, 0, :], start=True, stop=True))
                pe.matmul(ps[0:96, 7, S:2 * S], const("rot", 96), QRAW[0:96, 1, :], start=True, stop=True).then_inc(full["v"][7], 1)
                T.add(free["v"][7])

            def mla_scores(i):
                evacuated(6, 7)
                for hh in range(2):
                    take(1 + hh)
                    pe.matmul(ps[:, 1 + hh, 0:P], QT[0:96, hh, 0:P], KT[0:96, hh, 0:P], start=True, stop=True)
                    pe.matmul(ps[:, 1 + hh, P:3 * P], QT[0:96, hh, P:S], KT[0:96, hh, :], start=True, stop=True).then_inc(full["v"][1 + hh], 1)
                    T.add(free["v"][1 + hh])

            pe.wait_ge(sem("krope_ready"), T.next(sem("krope_ready")))
            mla_proj()
            assert not pending
            mla_scores(0)
            mla_proj()
            attend(0, turn_before=False)
            assert not pending
            with T.loop("mla", PAIRS - 2) as i:
                mla_scores(i + 1)
                mla_proj()
                attend(i + 1)
                assert not pending
            mla_scores(PAIRS - 1)
            out_begin(PAIRS - 2)
            attend(PAIRS - 1)
            turn()
            out_end(PAIRS - 2, 2)
            ffn(1)
            norm_t()
            row_tile(2, (6, 7), XT)

            def sb_scores(i):
                evacuated(0)
                for hh in range(2):
                    take(1 + hh)
                    r = slice(64 * hh, 64 * hh + 64)
                    first(pe.matmul(ps[:, 1 + hh, 0:S], KT[r, 0, 0:P], QT[r, 0, :], start=True, stop=True))
                    pe.matmul(ps[:, 1 + hh, S:3 * P], KT[r, 0, P:S], QT[r, 0, P:S], start=True, stop=True).then_inc(full["v"][1 + hh], 1)
                    T.add(free["v"][1 + hh])

            def sb_sums():
                for hh in range(2):
                    pe.wait_ge(sem("keep_ready"), T.next(sem("keep_ready")))
                    take(3 + hh)
                    k_ = PT[:, hh, :]
                    o_ = ps[:, 3 + hh, :]
                    group(o_[:, 0:P], [(const("from_"), k_[:, 0:P])])
                    group(o_[:, P:S], [(const("from_"), k_[:, P:S]), (const("ones"), k_[:, S:3 * P])])
                    group(o_[:, S:3 * P], [(const("from_"), k_[:, S:3 * P])]).then_inc(full["v"][3 + hh], 1)
                    T.add(free["v"][3 + hh])

            def sb_mix(i):
                take(5)
                for hh in range(2):
                    pe.wait_ge(sem("probs_ready"), T.next(sem("probs_ready")))
                    v0, v1 = (V[:, kt, ds((i * 2 + hh) * 64, 64)] for kt in range(2))
                    group(ps[:, 5, hh * 64:hh * 64 + 64], [(PR[:, hh, 0:P], v0)])
                    m = group(ps[:, 5, P + hh * 64:P + hh * 64 + 64], [(PR[:, hh, P:S], v0), (PR[:, hh, S:3 * P], v1)])
                m.then_inc(full["v"][5], 1)
                T.add(free["v"][5])

            def sb_turn():
                evacuated(5)
                take(6)
                for t in range(NT):
                    m = tr(ps[:, 6, t * P:(t + 1) * P], ON[:, t, :])
                m.then_inc(full["a"][6], 1)
                T.add(free["a"][6])

            qk_proj()
            evacuated(6, 7)
            flush()
            assert not pending
            sb_scores(0)
            qk_proj()
            sb_sums()
            sb_mix(0)
            assert not pending
            with T.loop("sb", 2) as i:
                sb_scores(i + 1)
                qk_proj()
                sb_sums()
                sb_turn()
                sb_mix(i + 1)
                assert not pending

            def channels(s_, g, b):
                take(b)
                for c in range(2):
                    m = group(ps[:, b, c * S:(c + 1) * S], ((slot(s_, KC, 512)[:, k, (2 * g + c) * P:(2 * g + c + 1) * P], XT[:, k, :])
                                                             for k in range(KC)))
                m.then_inc(full["a"][b], 1)
                T.add(free["a"][b])

            sb_scores(3)
            pe.wait_ge(here[3], T.next(here[3], 16))
            channels(3, 0, 0)
            sb_sums()
            sb_turn()
            channels(3, 1, 7)
            release(3)
            sb_mix(3)
            sb_turn()
            for n_, s_ in ((1, 2), (2, 3)):
                pe.wait_ge(here[s_], T.next(here[s_], 16))
                for g in range(2):
                    channels(s_, g, 2 * n_ + g)
                release(s_)
            pe.wait_ge(here[0], T.next(here[0], 16))
            take(0)
            for t in range(NT):
                m = group(ps[:, 0, 8 * t:8 * t + 8], ((cols(XT, t, k), slot(0, KC, 8)[:, k, :]) for k in range(KC)))
            m.then_inc(full["v"][0], 1)
            T.add(free["v"][0])
            release(0)
            row_tile(2, (6, 7), XT, reader="a")

            def gate_part(n_, b, ks=range(KC)):
                c, t = n_ // 2, n_ % 2
                s_ = 3 - c % 2
                if ks[0] == 0:
                    if t == 0:
                        pe.wait_ge(here[s_], T.next(here[s_], 16))
                    take(b)
                for k in ks:
                    m = pe.matmul(ps[:, b, :], cols(XT, t, k), slot(s_, KC, 512)[:, k, :], start=(k == 0), stop=(k == KC - 1))
                    if k < KC - 1:
                        first(m)
                if ks[-1] == KC - 1:
                    m.then_inc(full["a"][b], 1)
                    T.add(free["a"][b])
                    if t == 1:
                        release(s_)

            def heads(b, l, r, reader="v", freer=None, base=None):
                take(b)
                for h in range(GH):
                    m = pe.matmul(ps[:, b, h * P:(h + 1) * P], l(h), r(h), start=True, stop=True)
                    if h < GH - 1:
                        first(m)
                m.then_inc(full[reader][b], 1)
                T.add(free[freer or reader][b])

            def heads_t(b, src, reader="v"):
                take(b)
                for h in range(GH):
                    m = tr(ps[:, b, h * P:(h + 1) * P], src(h))
                m.then_inc(full[reader][b], 1)
                T.add(free[reader][b])

            pe.wait_ge(sem("sq_ready"), T.next(sem("sq_ready")))
            for n_ in range(4):
                b = 4 + n_
                take(b)
                pe.matmul(ps[:, b, :], const("ones"), SQ[:, 2 * n_:2 * n_ + 2, :], start=True, stop=True).then_inc(full["v"][b], 1)
                T.add(free["v"][b])
            pe.wait_ge(sem("g_ready"), T.next(sem("g_ready")))
            take(1)
            for t in range(NT):
                g_ = GG[:, t, :]
                for o_, c_ in ((4 * t, "blk_upto"), (8 + 4 * t, "blk"), (16 + 8 * t, "half0"), (20 + 8 * t, "half1")):
                    m = pe.matmul(ps[:, 1, o_:o_ + 4], const(c_), g_, start=True, stop=True)
                    if c_ != "half1":
                        first(m)
            m.then_inc(full["v"][1], 1)
            T.add(free["v"][1])
            for t in range(NT):
                heads(2 + t, lambda h: GG[:, t, h:h + 1].to_broadcast([P, P]), lambda h: const("blk_upto"), "v", "a")
            for n_ in range(2):
                gate_part(n_, n_)
            pe.wait_ge(sem("unit_ready"), T.next(sem("unit_ready")))
            for t in range(NT):
                heads_t(t, lambda h: cols(G, t, 4 + h))
            for t in range(NT):
                heads_t(2 + t, lambda h: cols(G, t, 8 + h))
            for t in range(NT):
                heads(4 + t, lambda h: cols(G, t, 4 + h), lambda h: cols(G, t, 4 + h))
            for t in range(NT):
                heads(6 + t, lambda h: cols(G, t, h), lambda h: cols(G, t, 4 + h))
            gate_part(2, 0)
            evacuated(4, 5)
            for t in range(NT):
                heads_t(4 + t, lambda h: hd(AA, t, h), "a")
            gate_part(3, 1)
            evacuated(6, 7)
            for t in range(NT):
                heads_t(6 + t, lambda h: hd(QK, t, h), "a")
            for lev in range(1, 6):
                for t in range(NT):
                    pe.wait_ge(sem("lt_ready"), T.next(sem("lt_ready")))
                    heads(t, lambda h: hd(LT, t, h), lambda h: hd(TI_, t, h), "a")
                if 1 < lev < 5:
                    gate_part(lev + 2, 6 + lev % 2, range(0, KC // 2))
                for t in range(NT):
                    evacuated(t)
                    heads(2 + t, lambda h: hd(UI, t, h), lambda h: hd(PP, t, h))
                    heads(4 + t, lambda h: hd(PP, t, h), lambda h: hd(UI, t, h))
                if 1 < lev < 5:
                    gate_part(lev + 2, 6 + lev % 2, range(KC // 2, KC))
            evacuated(2, 3, 4, 5, 6, 7)
            pe.wait_ge(sem("kb_ready"), T.next(sem("kb_ready")))
            for t in range(NT):
                heads(t, lambda h: hd(UI, t, h), lambda h: hd(VB, t, h))
                heads(2 + t, lambda h: hd(KBG, t, h), lambda h: hd(UI, t, h), "a")
            evacuated(0, 1, 2, 3)
            def up_part(n_, ks):
                c, t = n_ // 2, n_ % 2
                if n_ == 0 and ks[0] == 0:
                    pe.wait_ge(here[0], T.next(here[0], 16))
                if ks[0] == 0:
                    take(n_)
                for k in ks:
                    m = pe.matmul(ps[:, n_, :], cols(OT, t, k), slot(0, 4, D)[:, k, c * 512:(c + 1) * 512], start=(k == 0), stop=(k == 3))
                    if k < 3:
                        first(m)
                if ks[-1] == 3:
                    m.then_inc(full["v"][n_], 1)
                    T.add(free["v"][n_])
                    if n_ == 3:
                        release(0)

            pe.wait_ge(sem("state_ready"), T.next(sem("state_ready")))
            for c in range(4):
                t, r = c // 2, slice(64 * (c % 2), 64 * (c % 2) + 64)
                heads(4, lambda h: hd(WT, t, h), lambda h: ST[:, h * P:(h + 1) * P])
                heads(5, lambda h: hd(QD, t, h), lambda h: ST[:, h * P:(h + 1) * P])
                up_part(c, range(0, 2))
                evacuated(4)
                heads(6, lambda h: hd(KD, t, h)[r, :], lambda h: hd(VN, t, h)[r, :])
                if c % 2:
                    heads(7, lambda h: hd(QKT, t, h), lambda h: hd(VN, t, h))
                up_part(c, range(2, 4))
                evacuated(6)
            gate_part(7, 2)
            pe.wait_ge(sem("og_ready"), T.next(sem("og_ready")))
            transposes(lambda t, k: hd(OI, t, k), 4)
            evacuated(0, 1)
            pe.wait_ge(here[1], T.next(here[1], 16))
            for c in range(2):
                for t in range(NT):
                    b = 4 + 2 * c + t
                    take(b)
                    group(ps[:, b, :], ((cols(OT, t, 4 + k), slot(1, 4, D)[:, k, c * 512:(c + 1) * 512]) for k in range(4))).then_inc(full["v"][b], 1)
                    T.add(free["v"][b])
            release(1)
            pe.wait_ge(sem("merged_ready"), T.next(sem("merged_ready")))
            transposes(lambda t, k: MG[:, t, k * P:(k + 1) * P], KC)
            evacuated(0, 1, 2, 3)
            out_proj(XT2, 3)
            turned(MEM, KC, (4, 5, 6, 7))
            evacuated(4, 5, 6, 7)
            for c in range(2):
                row_tile(2 + c, (4 + 2 * c, 5 + 2 * c), XT2)
            norm_t()

            def cross_proj():
                for s_, X in ((0, XT), (1, XT2)):
                    pe.wait_ge(here[s_], T.next(here[s_], 16))
                    b = (0, 6)[s_]
                    take(b)
                    for c in range(2):
                        m = group(ps[:, b, c * S:(c + 1) * S], ((slot(s_, KC, XD)[:, k, c * P:(c + 1) * P], X[:, k, :]) for k in range(KC)))
                    release(s_)
                    m.then_inc(full["a"][b], 1)
                    T.add(free["a"][b])

            def cross_scores():
                evacuated(0, 6)
                take(1)
                for t in range(NT):
                    m = group(ps[:, 1, t * S:(t + 1) * S], ((cols(QT, t, c), KT[:, c, :]) for c in range(2)))
                m.then_inc(full["v"][1], 1)
                T.add(free["v"][1])

            def cross_attend(i, turn_before=True):
                pe.wait_ge(sem("probs_ready"), T.next(sem("probs_ready")))
                take(3)
                for n_ in range(4):
                    t, k = n_ // 2, n_ % 2
                    m = tr(ps[:, 3, n_ * P:(n_ + 1) * P], PR[:, 0, t * S + k * P:t * S + (k + 1) * P])
                    if n_ < 3:
                        first(m)
                m.then_inc(full["a"][3], 1)
                T.add(free["a"][3])
                if turn_before:
                    cross_turn()
                evacuated(3)
                take(4)
                for t in range(NT):
                    m = group(ps[:, 4, t * XD:(t + 1) * XD], ((PT[:, 0, (2 * t + k) * P:(2 * t + k + 1) * P], V[:, k, ds(i * XD, XD)]) for k in range(2)))
                m.then_inc(full["v"][4], 1)
                T.add(free["v"][4])

            def cross_turn():
                evacuated(4)
                take(5)
                for n_ in range(4):
                    c, t = n_ // 2, n_ % 2
                    m = tr(ps[:, 5, n_ * P:(n_ + 1) * P], ONX[:, t, c * P:(c + 1) * P])
                m.then_inc(full["a"][5], 1)
                T.add(free["a"][5])

            cross_proj()
            evacuated(4, 5, 6, 7)
            flush()
            assert not pending
            cross_scores()
            cross_proj()
            cross_attend(0, turn_before=False)
            assert not pending
            with T.loop("cross", 2) as i:
                cross_scores()
                cross_proj()
                cross_attend(i + 1)
                assert not pending
            cross_scores()
            evacuated(5)
            out_begin(4)
            cross_attend(3)
            cross_turn()
            out_end(4, 5)
            norm_t()
            def route():
                pe.wait_ge(here[0], T.next(here[0], 32))
                for q in range(2):
                    take(4 + q)
                    group(ps[:, 4 + q, 0:S], ((PW[:, q, k, :], XT[:, k, :]) for k in range(KC))).then_inc(full["a"][4 + q], 1)
                    T.add(free["a"][4 + q])
                release(0)
                pe.wait_ge(here[1], T.next(here[1], 16))
                take(6)
                first(tr(ps[:, 6, 0:P], SUBK[:, 0, :]))
                tr(ps[:, 6, P:2 * P], SUBK[:, 1, :]).then_inc(full["v"][6], 1)
                T.add(free["v"][6])
                release(1)
                evacuated(4, 5, 6)
                take(7)
                for n_ in range(4):
                    t, q = n_ // 2, n_ % 2
                    m = pe.matmul(ps[:, 7, n_ * P:(n_ + 1) * P], QP[:, q, t * P:(t + 1) * P], SKT[:, q, :], start=True, stop=True)
                    if n_ < 3:
                        first(m)
                m.then_inc(full["v"][7], 1)
                T.add(free["v"][7])
                assert not pending

            def skip_u():
                for j in range(RING):
                    T.add(gathered[j], 16 * NT)

            def mix_v(shared=()):
                for t in range(NT):
                    for j in range(RING):
                        if j in shared:
                            T.add(gathered[j], 16)
                            continue
                        pe.wait_ge(sem("diag_ready"), T.next(sem("diag_ready")))
                        pe.wait_ge(gathered[j], T.next(gathered[j], 16))
                        for c in range(2):
                            m = pe.matmul(ps[:, 2 * t + c, :], DIAG[:, j, :], ring(j)[:, c * 512:(c + 1) * 512], start=False, stop=False)
                        m.then_inc(ring_used[j], 1)

            route()
            take(0, 1, 2, 3)
            for b in range(4):
                pe.matmul(ps[:, b, :], const("zero"), XT[:, 0:2, :], start=True, stop=False)
            route()
            skip_u()
            with T.loop("peer", PH - 2) as i:
                route()
                skip_u()
                mix_v()
            skip_u()
            mix_v(shared=SHARED)
            mix_v(shared=SHARED)
            for b in range(4):
                pe.matmul(ps[:, b, 0:1], const("zero"), XT[:, 0, 0:1], start=False, stop=True).then_inc(full["v"][b], 1)
                T.add(free["v"][b])

        @block.scalar
        def _(act):
            T = Tally(act, "act", per_iter)
            chain = sem("act_chain")

            spare = []

            def signal(name):
                spare.append(len(spare) % 64)
                act.copy(ASCR[:, spare[-1]:spare[-1] + 1], CT[:, 0:1]).then_inc(sem(name) if isinstance(name, str) else name, 1)

            def root(n=NT):
                act.wait_ge(sem("rms_ready"), T.next(sem("rms_ready")))
                act.activation(RS[:, 0:n], RS[:, 0:n], ACT.Sqrt).then_inc(sem("rstd_ready"), 1)

            def softplus_part(x):
                act.activation(x, x, ACT.Exp, scale=-1.0).then_inc(chain, 1)
                act.wait_ge(chain, T.next(chain))
                return act.activation(x, x, ACT.Ln, bias=1.0)

            def probs(blocks):
                act.wait_ge(sem("max_ready"), T.next(sem("max_ready")))
                for n_, (dst, src) in blocks:
                    m = act.activation(dst, src, ACT.Exp, bias=SM[:, n_:n_ + 1], accum_out=SM[:, 8 + n_:9 + n_])
                m.then_inc(sem("probs_ready"), 1)

            def two_probs():
                for hh in range(2):
                    probs([(4 * hh + t, (PR[:, hh, c], LG[:, hh, c])) for t, c in enumerate((slice(0, P), slice(P, 3 * P)))])

            def turned_probs():
                for hh in range(2):
                    act.wait_ge(full["a"][3 + hh], T.next(full["a"][3 + hh]))
                    act.copy(PT[:, hh, 0:384], ps[:, 3 + hh, 0:384]).then_inc(free["a"][3 + hh], 1)

            def ot_copy(i, b=2):
                act.wait_ge(full["a"][b], T.next(full["a"][b]))
                act.copy(OT[:, ds(i, 1), :].rearrange("p o s -> p (o s)"), ps[:, b, 0:S]).then_inc(free["a"][b], 1)

            def qk_copy(scale):
                act.wait_ge(full["a"][0], T.next(full["a"][0]))
                act.mul(QT[:, 0, :], ps[:, 0, 0:S], scale)
                act.copy(KT[:, 0, :], ps[:, 0, S:2 * S]).then_inc(free["a"][0], 1)

            def high_gu(b):
                act.wait_ge(raw_here[b], T.next(raw_here[b], 32))
                act.copy(WGU[:, b, 0].rearrange("p g k n -> p (g k n)"), SLOT[b][:, 0:2 * KC * P]).then_inc(sem("high_ready"), 1)

            def high_dn(b):
                act.wait_ge(raw_here[2 + b], T.next(raw_here[2 + b], 16))
                act.wait_ge(sem(f"dn_used{b}"), T.due(sem(f"dn_used{b}")))
                act.copy(WDN[:, b, 0, :], SLOT[2 + b][:, 0:D]).then_inc(sem("high_ready"), 1)
                T.add(sem(f"dn_used{b}"))

            def gated(b):
                act.wait_ge(full["a"][4 + b], T.next(full["a"][4 + b]))
                act.activation(SG[:, b, :], ps[:, 4 + b, 0:S], ACT.Silu).then_inc(sem("silu_ready"), 1)

            def ffn(l):
                for b in range(2):
                    high_gu(b)
                root()
                for g in range(4):
                    act.wait_ge(sem("xt_ready"), T.next(sem("xt_ready")))
                    act.copy(XH[:, 0, 2 * g:2 * g + 2, :], XT[:, 2 * g:2 * g + 2, :]).then_inc(sem("high_ready"), 1)
                for b in range(2):
                    high_dn(b)
                with T.loop(f"ffn{l}", FB // 2 - 1) as i:
                    for b in range(2):
                        gated(b)
                        high_gu(b)
                    for b in range(2):
                        high_dn(b)
                for b in range(2):
                    gated(b)

            root()
            act.wait_ge(sem("ident_here"), T.next(sem("ident_here"), 16))
            for credit in (free["a"][3], free["a"][5], free["a"][2], *ring_used):
                signal(credit)
            act.wait_ge(sem("absz_ready"), T.next(sem("absz_ready")))
            softplus_part(LF2[:]).then_inc(sem("ln_ready"), 1)
            qk_copy(0.125)
            two_probs()
            qk_copy(0.125)
            turned_probs()
            with T.loop("fox", PAIRS - 2) as i:
                two_probs()
                qk_copy(0.125)
                turned_probs()
                ot_copy(i)
            two_probs()
            turned_probs()
            ot_copy(PAIRS - 2)
            ot_copy(PAIRS - 1)
            ffn(0)
            root()
            act.wait_ge(sem("wpad_here"), 1)
            act.dma_start(WPAD[:, :, 64:96], rows(a["w_kv_a"], 256, 288)).then_inc(sem("wpad_here"), 16)
            act.wait_ge(sem("angle_ready"), T.next(sem("angle_ready")))
            act.activation(COS[0:96, 0, :], ANG[0:96, 0, :], ACT.Sin)
            act.activation(SIN[0:96, 0, :], ANG[0:96, 1, :], ACT.Sin).then_inc(sem("sin_ready"), 1)
            act.wait_ge(full["a"][4], T.next(full["a"][4]))
            act.copy(KRT[0:96, :], ps[0:96, 4, 0:S]).then_inc(free["a"][4], 1)
            for t in range(NT):
                act.wait_ge(full["a"][t], T.next(full["a"][t]))
                act.copy(KVA[:, t, 0:KVR], ps[:, t, 0:KVR]).then_inc(free["a"][t], 1)
            signal("kva_ready")
            root()
            act.wait_ge(sem("kva_used"), T.next(sem("kva_used")))
            for t in range(NT):
                for c in range(2):
                    b = (2, 3, 6, 7)[2 * t + c]
                    act.wait_ge(full["a"][b], T.next(full["a"][b]))
                    act.copy(KVA[:, t, 384 * c:384 * c + 384], ps[:, b, 0:384]).then_inc(free["a"][b], 1)
            signal("kva_ready")
            root()

            def mla_copy():
                act.wait_ge(full["a"][0], T.next(full["a"][0]))
                act.copy(QRAW[0:96, :, :], view(ps[0:96, 0, :], 2, S)).then_inc(free["a"][0], 1)
                act.wait_ge(full["a"][6], T.next(full["a"][6]))
                act.copy(KT[0:64, :, :], view(ps[0:64, 6, :], 2, S)).then_inc(free["a"][6], 1)

            mla_copy()
            two_probs()
            mla_copy()
            turned_probs()
            with T.loop("mla", PAIRS - 2) as i:
                two_probs()
                mla_copy()
                turned_probs()
                ot_copy(i)
            two_probs()
            turned_probs()
            ot_copy(PAIRS - 2)
            ot_copy(PAIRS - 1)
            ffn(1)
            root()
            root()
            def sb_soft():
                for hh in range(2):
                    act.wait_ge(sem("absz_ready"), T.next(sem("absz_ready")))
                    act.activation(PR[:, hh, 0:384], PR[:, hh, 0:384], ACT.Exp, scale=-1.0).then_inc(chain, 1)
                act.wait_ge(chain, T.next(chain, 2))
                for hh in range(2):
                    act.activation(PR[:, hh, 0:384], PR[:, hh, 0:384], ACT.Ln, bias=1.0).then_inc(sem("ln_ready"), 1)

            def sb_probs():
                for hh in range(2):
                    act.wait_ge(sem("expo_ready"), T.next(sem("expo_ready")))
                    act.activation(PR[:, hh, 0:384], LG[:, hh, 0:384], ACT.Exp).then_inc(sem("probs_ready"), 1)

            qk_copy(0.125)
            sb_soft()
            qk_copy(0.125)
            sb_probs()
            with T.loop("sb", 2) as i:
                sb_soft()
                qk_copy(0.125)
                sb_probs()
                ot_copy(i, 6)
            sb_soft()
            sb_probs()
            ot_copy(2, 6)
            ot_copy(3, 6)
            def gate_out(n_, b):
                c, t = n_ // 2, n_ % 2
                act.wait_ge(full["a"][b], T.next(full["a"][b]))
                act.activation(GT[c // 2][:, t, c % 2 * 512:c % 2 * 512 + 512], ps[:, b, :], ACT.Sigmoid).then_inc(free["a"][b], 1)

            act.wait_ge(sem("pad_ready"), T.next(sem("pad_ready")))
            for n_, b in enumerate((0, 7, 2, 3, 4, 5)):
                act.wait_ge(full["a"][b], T.next(full["a"][b]))
                act.copy(PRE[:, 2 * n_:2 * n_ + 2, CONV - 1:], view(ps[:, b, :], 2, S)).then_inc(free["a"][b], 1)
                signal("pre_ready")
            act.wait_ge(sem("conv_ready"), T.next(sem("conv_ready")))
            act.activation(G[:], G[:], ACT.Silu).then_inc(sem("silu_ready"), 1)
            act.wait_ge(sem("gates_ready"), T.next(sem("gates_ready")))
            act.activation(BT[:], BA[:, :, 0:4], ACT.Sigmoid)
            act.activation(AEXP, GSM[:, 0:4], ACT.Exp)
            softplus_part(GL).then_inc(sem("ln_ready"), 1)
            for t in range(NT):
                act.wait_ge(full["a"][6 + t], T.next(full["a"][6 + t]))
                act.activation(V[:, t, 512:], ps[:, 6 + t, :], ACT.Silu).then_inc(free["a"][6 + t], 1)
            act.wait_ge(sem("rnorm_ready"), T.next(sem("rnorm_ready")))
            act.activation(SQ[:], SQ[:], ACT.Sqrt).then_inc(sem("sqrt_ready"), 1)
            act.wait_ge(sem("sums_ready"), T.next(sem("sums_ready")))
            act.activation(EX, RAW, ACT.Exp).then_inc(sem("ex_ready"), 1)
            for t in range(NT):
                act.wait_ge(sem("dec_ready"), T.next(sem("dec_ready")))
                for h in range(GH):
                    m = act.activation(hd(DEC, t, h), hd(DEC, t, h), ACT.Exp, bias=RAW[:, 4 * t + h:4 * t + h + 1])
                act.activation(ER[:, t, :], ps[:, 2 + t, :], ACT.Exp).then_inc(free["a"][2 + t], 1)
            signal("er_ready")
            for n_ in range(3):
                gate_out(n_, n_ % 2)
            for t in range(NT):
                act.wait_ge(full["a"][4 + t], T.next(full["a"][4 + t]))
                act.copy(AT[:, t, :], ps[:, 4 + t, :]).then_inc(free["a"][4 + t], 1)
            signal("at_ready")
            gate_out(3, 1)
            for t in range(NT):
                act.wait_ge(full["a"][6 + t], T.next(full["a"][6 + t]))
                act.copy(QKT[:, t, :], ps[:, 6 + t, :]).then_inc(free["a"][6 + t], 1)
            for lev in range(1, 6):
                for t in range(NT):
                    act.wait_ge(full["a"][t], T.next(full["a"][t]))
                    act.copy(PP[:, t, :], ps[:, t, :]).then_inc(free["a"][t], 1)
                if lev > 2:
                    gate_out(lev + 1, 6 + (lev - 1) % 2)
            signal("gt_ready")
            for t in range(NT):
                act.wait_ge(full["a"][2 + t], T.next(full["a"][2 + t]))
                act.copy(WT[:, t, :], ps[:, 2 + t, :]).then_inc(free["a"][2 + t], 1)
            root(8)
            gate_out(7, 2)
            signal("gt_ready")
            root()
            root()
            def cross_copy():
                act.wait_ge(full["a"][0], T.next(full["a"][0]))
                act.mul(QT[:], view(ps[:, 0, :], 2, S), 0.0625).then_inc(free["a"][0], 1)
                act.wait_ge(full["a"][6], T.next(full["a"][6]))
                act.copy(KT[:], view(ps[:, 6, :], 2, S)).then_inc(free["a"][6], 1)

            def cross_turned():
                act.wait_ge(full["a"][3], T.next(full["a"][3]))
                act.copy(PT[:, 0, :], ps[:, 3, :]).then_inc(free["a"][3], 1)

            def cross_out(i):
                act.wait_ge(full["a"][5], T.next(full["a"][5]))
                act.copy(OT[:, ds(i * 2, 2), :], view(ps[:, 5, :], 2, S)).then_inc(free["a"][5], 1)

            def cross_probs():
                probs([(t, (PR[:, 0, t * S:(t + 1) * S], LG[:, 0, t * S:(t + 1) * S])) for t in range(NT)])

            cross_copy()
            cross_probs()
            cross_copy()
            cross_turned()
            with T.loop("cross", 2) as i:
                cross_probs()
                cross_copy()
                cross_turned()
                cross_out(i)
            cross_probs()
            cross_turned()
            cross_out(2)
            cross_out(3)
            root()
            def queries():
                for q in range(2):
                    act.wait_ge(full["a"][4 + q], T.next(full["a"][4 + q]))
                    act.copy(QP[:, q, :], ps[:, 4 + q, 0:S]).then_inc(free["a"][4 + q], 1)

            def gate_exp():
                act.wait_ge(sem("best_ready"), T.next(sem("best_ready")))
                act.activation(GX[:], BSX[:], ACT.Exp).then_inc(sem("gate_exp"), 1)

            def gelu():
                for j in range(RING):
                    T.add(ring_used[j], NT)
                act.wait_ge(ring_used[RING - 1], T.due(ring_used[RING - 1]))
                act.activation(AX_[:], DOT[:], ACT.Gelu).then_inc(sem("gelu_ready"), 1)

            def diagonals(h, shared=()):
                for t in range(NT):
                    for j in range(RING):
                        if j in shared:
                            T.add(ring_used[j])
                            continue
                        act.wait_ge(ring_used[j], T.due(ring_used[j]))
                        act.activation(DIAG[:, j, :], IDENT, ACT.Copy, scale=AV[:, t, ds(h * TOPK + j, 1)]).then_inc(sem("diag_ready"), 1)
                        T.add(ring_used[j])

            for j in range(RING):
                T.add(ring_used[j])
            queries()
            gate_exp()
            queries()
            gelu()
            gate_exp()
            with T.loop("peer", PH - 2) as i:
                queries()
                gelu()
                act.wait_ge(sem("av_ready"), T.next(sem("av_ready")))
                diagonals(i)
                gate_exp()
            gelu()
            act.wait_ge(sem("av_ready"), T.next(sem("av_ready")))
            diagonals(PH - 2, SHARED)
            act.wait_ge(sem("av_ready"), T.next(sem("av_ready")))
            diagonals(PH - 1, SHARED)
            root()

        @block.gpsimd
        def _(pool):
            T = Tally(pool, "pool", per_iter)

            for j in range(RING):
                T.add(ring_used[j])
            pool.memset(PSCR[:], 0.0).then_inc(sem("pool_chain"), 1)
            pool.wait_ge(sem("pool_chain"), T.next(sem("pool_chain")))
            u_rows, v_rows = a["peer_u_2"][0], a["peer_v_2"][0]

            def gather(table, h):
                for t in range(NT):
                    for g in range(0, RING, 4):
                        for j in range(g, g + 4):
                            pool.wait_ge(ring_used[j], T.due(ring_used[j]))
                            T.add(ring_used[j])
                        pool.tensor_copy(IX[:, g:g + 4], EXU[:, t, ds(h * TOPK + g, 4)]).then_inc(sem("pool_chain"), 1)
                        pool.wait_ge(sem("pool_chain"), T.next(sem("pool_chain")))
                        pool.tensor_tensor(PSCR[:, g:g + 1], PSCR[:, 15:16], PSCR[:, 15:16], ALU.add)
                        for j in range(g, g + 4):
                            pool.indirect_dma_start(ring(j), None, table, bass.IndirectOffsetOnAxis(IX[:, j:j + 1], 0)).then_inc(gathered[j], 16)

            pool.wait_ge(sem("expert_ready"), T.next(sem("expert_ready")))
            gather(u_rows, 0)
            with T.loop("peer", PH - 2) as i:
                pool.wait_ge(sem("expert_ready"), T.next(sem("expert_ready")))
                gather(u_rows, i + 1)
                gather(v_rows, i)
            pool.wait_ge(sem("expert_ready"), T.next(sem("expert_ready")))
            gather(u_rows, PH - 1)
            gather(v_rows, PH - 2)
            gather(v_rows, PH - 1)

        @block.vector
        def _(dve):
            T = Tally(dve, "dve", per_iter)
            chain = sem("dve_chain")
            TT, TS, STT = dve.tensor_tensor, dve.tensor_scalar, dve.scalar_tensor_tensor

            def settled(*banks):
                for b in banks:
                    dve.wait_ge(free["v"][b], T.due(free["v"][b]))

            def rstd(width, n):
                TS(RS[:, 0:n], SS[:, 0:n], 1.0 / width, EPS, ALU.mult, ALU.add).then_inc(chain, 1)
                dve.wait_ge(chain, T.next(chain))
                dve.reciprocal(RS[:, 0:n], RS[:, 0:n]).then_inc(sem("rms_ready"), 1)
                dve.wait_ge(sem("rstd_ready"), T.next(sem("rstd_ready")))

            spare = []

            def signal(name):
                spare.append(34 + len(spare) % 24)
                dve.tensor_copy(SM[:, spare[-1]:spare[-1] + 1], SM[:, 33:34]).then_inc(sem(name), 1)

            def root_mean(src, w, squared=False):
                if squared:
                    m = TT(SS[:, 0:NT], SS[:, 10:10 + NT], SS[:, 10 + NT:10 + 2 * NT], ALU.add)
                else:
                    for t in range(NT):
                        m = STT(XS[:, t, 0:w], src[:, t, 0:w], 1.0, src[:, t, 0:w], ALU.mult, ALU.mult, accum_out=SS[:, t:t + 1])
                m.then_inc(chain, 1)
                dve.wait_ge(chain, T.next(chain))
                rstd(w, NT)

            def scaled(src, w, squared=False):
                root_mean(src, w, squared)
                for t in range(NT):
                    m = TS(DG[:, t, :], IDENT, RS[:, t:t + 1], None, ALU.mult)
                return m

            def gained_rows(dst):
                for t in range(NT):
                    m = STT(dst[:, t, :], H[:, t, :], RS[:, t:t + 1], ROWG[:], ALU.mult, ALU.mult)
                return m

            def gained(X, name, n_chunks, banks=(0, 1, 2, 3), X2=None, name2=None):
                for g in range(n_chunks // 2):
                    b = banks[g % len(banks)]
                    dve.wait_ge(full["v"][b], T.next(full["v"][b]))
                    src = view(ps[:, b, :], 2, S)
                    if X2 is not None:
                        TT(X2[:, 2 * g:2 * g + 2, :], src, inner(gcol(name2, 2 * g, 2), S), ALU.mult)
                    TT(X[:, 2 * g:2 * g + 2, :], src, inner(gcol(name, 2 * g, 2), S), ALU.mult).then_inc(free["v"][b], 1)
                    T.add(free["v"][b])

            def norm(name, X=None, X2=None, name2=None, src=None, squared=True):
                scaled(H if src is None else src, D, squared).then_inc(sem("xs_ready"), 1)
                gained(XT if X is None else X, name, KC, X2=X2, name2=name2)

            def values(banks_of):
                for c in range(2):
                    for t in range(NT):
                        b = banks_of(c, t)
                        dve.wait_ge(full["v"][b], T.next(full["v"][b]))
                        dve.tensor_copy(V[:, t, c * 512:(c + 1) * 512], ps[:, b, :]).then_inc(free["v"][b], 1)
                        T.add(free["v"][b])

            def residual(banks_of=lambda c, t: 2 * c + t, order=None):
                for c in range(2):
                    for t in range(NT):
                        b = banks_of(c, t)
                        dve.wait_ge(full["v"][b], T.next(full["v"][b]))
                        half = H[:, t, c * 512:(c + 1) * 512]
                        TT(half, half, ps[:, b, :], ALU.add).then_inc(free["v"][b], 1)
                        T.add(free["v"][b])
                        settled(b)
                        m = STT(XS[:, t, c * 512:(c + 1) * 512], half, 1.0, half, ALU.mult, ALU.mult, accum_out=SS[:, 10 + NT * c + t:11 + NT * c + t])
                m.then_inc(chain, 1)
                dve.wait_ge(chain, T.next(chain))

            def neg_max(hh):
                link_before = [(0, slice(0, P)), (1, slice(P, 3 * P))]
                for t, c in link_before:
                    m = dve.tensor_reduce(SM[:, 4 * hh + t:4 * hh + t + 1], LG[:, hh, c], AX, ALU.max, negate=True)
                m.then_inc(sem("max_ready"), 1)

            CAUSAL = const("causal")

            def attend_tail(i):
                for hh in range(2):
                    dve.wait_ge(sem("probs_ready"), T.next(sem("probs_ready")))
                dve.reciprocal(SM[:, 16:24], SM[:, 8:16]).then_inc(chain, 1)
                dve.wait_ge(chain, T.next(chain))
                dve.wait_ge(full["v"][5], T.next(full["v"][5]))
                for hh in range(2):
                    for t in range(NT):
                        m = TS(ON[:, t, hh * 64:hh * 64 + 64], ps[:, 5, t * P + hh * 64:t * P + hh * 64 + 64],
                               SM[:, 16 + 4 * hh + t:17 + 4 * hh + t], None, ALU.mult)
                m.then_inc(free["v"][5], 1)
                T.add(free["v"][5])

            def low(out_, x, high):
                return TT(out_, x, high.bitcast(F32), ALU.subtract)

            def low_gu(b):
                low(WGU[:, b, 1].rearrange("p g k n -> p (g k n)"), SLOT[b][:, 0:2 * KC * P],
                    WGU[:, b, 0].rearrange("p g k n -> p (g k n)")).then_inc(used[b], 1)
                signal(f"gu_split{b}")

            def low_dn(b):
                dve.wait_ge(sem("high_ready"), T.next(sem("high_ready")))
                low(WDN[:, b, 1, :], SLOT[2 + b][:, 0:D], WDN[:, b, 0, :]).then_inc(used[2 + b], 1)
                signal(f"dn_split{b}")

            def gated(b):
                dve.wait_ge(sem("silu_ready"), T.next(sem("silu_ready")))
                TT(SG[:, b, :], SG[:, b, :], ps[:, 4 + b, S:2 * S], ALU.mult).then_inc(chain, 1)
                dve.wait_ge(chain, T.next(chain))
                dve.tensor_copy(HT[:, b, 0, :], SG[:, b, :]).then_inc(chain, 1)
                dve.wait_ge(chain, T.next(chain))
                low(HT[:, b, 1, :], SG[:, b, :], HT[:, b, 0, :]).then_inc(free["v"][4 + b], 1)
                T.add(free["v"][4 + b])

            def first_gu():
                dve.wait_ge(sem("high_ready"), T.next(sem("high_ready"), 2))
                for b in range(2):
                    low_gu(b)

            def ffn(l):
                scaled(H, D, squared=True).then_inc(sem("xs_ready"), 1)
                for g in range(4):
                    dve.wait_ge(full["v"][g], T.next(full["v"][g]))
                    TT(XT[:, 2 * g:2 * g + 2, :], view(ps[:, g, :], 2, S), inner(gcol(f"ffn{l}", 2 * g, 2), S), ALU.mult).then_inc(free["v"][g], 1)
                    T.add(free["v"][g])
                    settled(g)
                    signal("xt_ready")
                for g in range(4):
                    dve.wait_ge(sem("high_ready"), T.next(sem("high_ready")))
                    m = low(XH[:, 1, 2 * g:2 * g + 2, :], XT[:, 2 * g:2 * g + 2, :], XH[:, 0, 2 * g:2 * g + 2, :])
                m.then_inc(sem("xh_ready"), 1)
                for b in range(2):
                    low_dn(b)
                with T.loop(f"ffn{l}", FB // 2 - 1) as i:
                    for b in range(2):
                        gated(b)
                        dve.wait_ge(sem("high_ready"), T.next(sem("high_ready")))
                        low_gu(b)
                    for b in range(2):
                        low_dn(b)
                for b in range(2):
                    gated(b)
                residual(lambda c, t: 2 * t + c)

            def absolute(out_, x):
                return STT(out_, x, -1.0, x, ALU.mult, ALU.max)

            def softplus(out_, x, part):
                return STT(out_, x, 0.0, part, ALU.max, ALU.add)

            dve.memset(SM[:], 1.0)
            dve.wait_ge(sem("x_here"), T.next(sem("x_here"), 16))
            dve.wait_ge(sem("ident_here"), T.next(sem("ident_here"), 16))
            scaled(H, D).then_inc(sem("xs_ready"), 1)
            dve.wait_ge(full["v"][0], T.next(full["v"][0]))
            dve.tensor_copy(GCOL[:], ps[:, 0, 0:P]).then_inc(free["v"][0], 1)
            T.add(free["v"][0])
            settled(0)
            gained(XT, "attn0", KC)
            dve.wait_ge(sem("wf_here"), T.next(sem("wf_here"), 32))
            dve.wait_ge(full["v"][4], T.next(full["v"][4]))
            TT(LF[:], view(ps[:, 4, 0:32], NT, 16), outer(BF[:], NT), ALU.add).then_inc(free["v"][4], 1)
            T.add(free["v"][4])
            settled(4)
            absolute(LF2[:], LF[:]).then_inc(sem("absz_ready"), 1)
            dve.wait_ge(sem("ln_ready"), T.next(sem("ln_ready")))
            STT(LF[:], LF[:], 0.0, LF2[:], ALU.min, ALU.subtract).then_inc(chain, 1)
            dve.wait_ge(chain, T.next(chain))
            signal("logf_ready")
            dve.wait_ge(full["v"][4], T.next(full["v"][4]))
            dve.tensor_copy(CQ[:], view(ps[:, 4, 0:32], NT, 16)).then_inc(free["v"][4], 1)
            T.add(free["v"][4])
            dve.wait_ge(full["v"][5], T.next(full["v"][5]))
            TS(CUMT[:], ps[0:16, 5, 0:S], -1.0, None, ALU.mult).then_inc(free["v"][5], 1)
            T.add(free["v"][5])
            settled(5)
            signal("cumt_ready")

            values(lambda c, t: 2 * c + t)

            def fox_scores(i):
                for hh in range(2):
                    dve.wait_ge(full["v"][1 + hh], T.next(full["v"][1 + hh]))
                    STT(LG[:, hh, 0:P], ps[:, 1 + hh, 0:P], CQ[:, 0, ds(i * 2 + hh, 1)], CAUSAL[:, P:2 * P], ALU.add, ALU.add)
                    STT(LG[:, hh, P:3 * P], ps[:, 1 + hh, P:3 * P], CQ[:, 1, ds(i * 2 + hh, 1)], CAUSAL, ALU.add, ALU.add).then_inc(free["v"][1 + hh], 1)
                    T.add(free["v"][1 + hh])
                    settled(1 + hh)
                    neg_max(hh)

            with T.loop("fox", PAIRS - 1) as i:
                fox_scores(i)
                attend_tail(i)
            fox_scores(PAIRS - 1)
            attend_tail(PAIRS - 1)
            first_gu()
            residual(lambda c, t: (6, 2)[c] + t)
            ffn(0)
            dve.memset(WPAD[:], 0.0).then_inc(chain, 1)
            dve.wait_ge(chain, T.next(chain))
            signal("wpad_here")
            norm("attn1", X2=XT2, name2="kv")
            dve.wait_ge(sem("pos_here"), T.next(sem("pos_here"), 16))
            R96 = slice(0, 96)
            posf, ang = ANG[R96, 2, :], ANG[R96, 3, :]
            dve.tensor_copy(posf, POSI[R96, :]).then_inc(chain, 1)
            dve.wait_ge(chain, T.next(chain))
            TS(ang, posf, const("inv_freq", 96), None, ALU.mult).then_inc(chain, 1)
            dve.wait_ge(chain, T.next(chain))
            MAGIC = 12582912.0
            for n_, quarter in ((0, 0.25), (1, 0.0)):
                x, k = ANG[R96, n_, :], posf
                TS(k, ang, 1.0 / TWO_PI, quarter, ALU.mult, ALU.add).then_inc(chain, 1)
                dve.wait_ge(chain, T.next(chain))
                TS(k, k, MAGIC, None, ALU.add).then_inc(chain, 1)
                dve.wait_ge(chain, T.next(chain))
                TS(k, k, MAGIC, None, ALU.subtract).then_inc(chain, 1)
                dve.wait_ge(chain, T.next(chain))
                STT(x, k, -PI_PARTS[0], ang, ALU.mult, ALU.add).then_inc(chain, 1)
                dve.wait_ge(chain, T.next(chain))
                STT(x, k, -PI_PARTS[1], x, ALU.mult, ALU.add).then_inc(chain, 1)
                dve.wait_ge(chain, T.next(chain))
                STT(x, k, -PI_PARTS[2], x, ALU.mult, ALU.add).then_inc(chain, 1)
                dve.wait_ge(chain, T.next(chain))
                TS(x, x, quarter * TWO_PI, 3.1415925, ALU.add, ALU.min).then_inc(chain, 1)
                dve.wait_ge(chain, T.next(chain))
                TS(x, x, -3.1415925, None, ALU.max).then_inc(chain, 1)
                dve.wait_ge(chain, T.next(chain))
            signal("angle_ready")
            dve.wait_ge(sem("sin_ready"), T.next(sem("sin_ready")))
            dve.tensor_copy(COS[R96, 1, :], COS[R96, 0, :])
            dve.tensor_copy(SIN[R96, 1, :], SIN[R96, 0, :]).then_inc(chain, 1)
            dve.wait_ge(chain, T.next(chain))
            dve.wait_ge(sem("kva_ready"), T.next(sem("kva_ready")))
            scaled(KVA, KVR).then_inc(sem("xs_ready"), 1)
            dve.wait_ge(full["v"][5], T.next(full["v"][5]))
            TT(ANG[R96, 2, :], ps[R96, 5, 0:S], SIN[R96, 0, :], ALU.mult).then_inc(chain, 1)
            dve.wait_ge(chain, T.next(chain))
            TT(KRT[R96, :], KRT[R96, :], COS[R96, 0, :], ALU.mult).then_inc(chain, 1)
            dve.wait_ge(chain, T.next(chain))
            TT(KRT[R96, :], KRT[R96, :], ANG[R96, 2, :], ALU.add).then_inc(free["v"][5], 1)
            T.add(free["v"][5])
            settled(5)
            dve.tensor_copy(KT[64:96, 0, :], KRT[64:96, :])
            dve.tensor_copy(KT[64:96, 1, :], KRT[64:96, :]).then_inc(chain, 1)
            dve.wait_ge(chain, T.next(chain))
            signal("krope_ready")
            gained(CKT, "ckv", 2)
            signal("kva_used")
            values(lambda c, t: (4, 5)[t])
            dve.wait_ge(sem("kva_ready"), T.next(sem("kva_ready")))
            scaled(KVA, QR).then_inc(sem("xs_ready"), 1)
            gained(CQT, "cq", 6, (0, 1, 2))

            def rotate():
                dve.wait_ge(full["v"][7], T.next(full["v"][7]))
                TT(ANG[R96, 0:2, :], view(ps[R96, 7, :], 2, S), SIN[R96, :, :], ALU.mult)
                TT(ANG[R96, 2:4, :], QRAW[R96, :, :], COS[R96, :, :], ALU.mult).then_inc(chain, 1)
                dve.wait_ge(chain, T.next(chain))
                TT(QT[R96, :, :], ANG[R96, 0:2, :], ANG[R96, 2:4, :], ALU.add).then_inc(free["v"][7], 1)
                T.add(free["v"][7])

            def mla_scores():
                for hh in range(2):
                    dve.wait_ge(full["v"][1 + hh], T.next(full["v"][1 + hh]))
                    STT(LG[:, hh, 0:P], ps[:, 1 + hh, 0:P], MLA_SCALE, CAUSAL[:, P:2 * P], ALU.mult, ALU.add)
                    STT(LG[:, hh, P:3 * P], ps[:, 1 + hh, P:3 * P], MLA_SCALE, CAUSAL, ALU.mult, ALU.add).then_inc(free["v"][1 + hh], 1)
                    T.add(free["v"][1 + hh])
                    settled(1 + hh)
                    neg_max(hh)

            rotate()
            with T.loop("mla", PAIRS - 1) as i:
                mla_scores()
                rotate()
                attend_tail(i)
            mla_scores()
            attend_tail(PAIRS - 1)
            first_gu()
            residual(lambda c, t: (6, 2)[c] + t)
            ffn(1)
            root_mean(H, D, squared=True)
            dve.wait_ge(sem("rowg_here"), T.next(sem("rowg_here"), 16))
            gained_rows(H).then_inc(chain, 1)
            dve.wait_ge(chain, T.next(chain))
            signal("rowg_used")
            norm("mix", squared=False)
            for t in range(NT):
                dve.wait_ge(full["v"][6 + t], T.next(full["v"][6 + t]))
                dve.tensor_copy(V[:, t, 0:512], ps[:, 6 + t, :]).then_inc(free["v"][6 + t], 1)
                T.add(free["v"][6 + t])

            def sb_scores():
                for hh in range(2):
                    dve.wait_ge(full["v"][1 + hh], T.next(full["v"][1 + hh]))
                    dve.tensor_copy(LG[:, hh, 0:384], ps[:, 1 + hh, 0:384]).then_inc(free["v"][1 + hh], 1)
                    T.add(free["v"][1 + hh])
                    settled(1 + hh)
                    absolute(PR[:, hh, 0:384], LG[:, hh, 0:384]).then_inc(sem("absz_ready"), 1)

            def sb_keep():
                for hh in range(2):
                    dve.wait_ge(sem("ln_ready"), T.next(sem("ln_ready")))
                    softplus(PT[:, hh, 0:384], LG[:, hh, 0:384], PR[:, hh, 0:384]).then_inc(chain, 1)
                    dve.wait_ge(chain, T.next(chain))
                    TT(LG[:, hh, 0:384], LG[:, hh, 0:384], const("sb_neg"), ALU.add)
                    TT(PT[:, hh, 0:384], PT[:, hh, 0:384], const("sb_keep"), ALU.mult).then_inc(sem("keep_ready"), 1)

            def sb_tail():
                for hh in range(2):
                    dve.wait_ge(full["v"][3 + hh], T.next(full["v"][3 + hh]))
                    TT(LG[:, hh, 0:384], LG[:, hh, 0:384], ps[:, 3 + hh, 0:384], ALU.add).then_inc(free["v"][3 + hh], 1)
                    T.add(free["v"][3 + hh])
                    settled(3 + hh)
                    signal("expo_ready")
                dve.wait_ge(full["v"][5], T.next(full["v"][5]))
                dve.tensor_copy(ON[:], view(ps[:, 5, 0:S], 2, P)).then_inc(free["v"][5], 1)
                T.add(free["v"][5])

            with T.loop("sb", 3) as i:
                sb_scores()
                sb_keep()
                sb_tail()
            sb_scores()
            sb_keep()
            sb_tail()
            T.add(sem("probs_ready"), 8)
            settled(5)
            dve.memset(PRE[:, :, 0:CONV - 1], 0.0).then_inc(chain, 1)
            dve.wait_ge(chain, T.next(chain))
            dve.memset(ST[:], 0.0).then_inc(sem("pad_ready"), 1)
            for b in range(6):
                dve.wait_ge(sem("pre_ready"), T.next(sem("pre_ready")))
                for j in range(CONV):
                    for c in (2 * b, 2 * b + 1):
                        tap, src = gcol("conv", j * 12 + c, 1), PRE[:, c, j:j + S]
                        m = TS(G[:, c, :], src, tap, None, ALU.mult) if j == 0 else STT(G[:, c, :], src, tap, G[:, c, :], ALU.mult, ALU.add)
                    m.then_inc(chain, 1)
                    dve.wait_ge(chain, T.next(chain))
            signal("conv_ready")
            dve.wait_ge(sem("gsm_here"), T.next(sem("gsm_here"), 48))
            dve.wait_ge(full["v"][0], T.next(full["v"][0]))
            dve.tensor_copy(BA[:], view(ps[:, 0, 0:16], NT, 8)).then_inc(free["v"][0], 1)
            T.add(free["v"][0])
            settled(0)
            TT(GZ, BA[:, :, 4:8], outer(GSM[:, 4:8], NT), ALU.add).then_inc(chain, 1)
            dve.wait_ge(chain, T.next(chain))
            absolute(GL, GZ).then_inc(sem("gates_ready"), 1)
            dve.wait_ge(sem("silu_ready"), T.next(sem("silu_ready")))
            TT(SQ[:], G[:, 0:8, :], G[:, 0:8, :], ALU.mult).then_inc(sem("sq_ready"), 1)
            dve.wait_ge(sem("ln_ready"), T.next(sem("ln_ready")))
            softplus(GZ, GZ, GL).then_inc(chain, 1)
            dve.wait_ge(chain, T.next(chain))
            STT(GG, GZ, -1.0, outer(AEXP, NT), ALU.mult, ALU.mult).then_inc(chain, 1)
            dve.wait_ge(chain, T.next(chain))
            signal("g_ready")
            for n_ in range(4):
                dve.wait_ge(full["v"][4 + n_], T.next(full["v"][4 + n_]))
                TS(SQ[:, 2 * n_:2 * n_ + 2, :], view(ps[:, 4 + n_, :], 2, S), EPS, None, ALU.add).then_inc(free["v"][4 + n_], 1)
                T.add(free["v"][4 + n_])
            settled(4, 5, 6, 7)
            dve.reciprocal(SQ[:], SQ[:]).then_inc(sem("rnorm_ready"), 1)
            dve.wait_ge(full["v"][1], T.next(full["v"][1]))
            dve.tensor_copy(RAW[:, 16:32], ps[:, 1, 16:32])
            dve.tensor_copy(RAW[:, 0:8], ps[:, 1, 0:8]).then_inc(chain, 1)
            dve.wait_ge(chain, T.next(chain))
            TT(RAW[:, 8:16], ps[:, 1, 8:16], RAW[:, 0:8], ALU.subtract).then_inc(free["v"][1], 1)
            T.add(free["v"][1])
            settled(1)
            signal("sums_ready")
            for t in range(NT):
                dve.wait_ge(full["v"][2 + t], T.next(full["v"][2 + t]))
                TT(view(DEC[:, t, :], GH, P), outer(const("dmask"), GH), view(ps[:, 2 + t, :], GH, P), ALU.subtract).then_inc(sem("dec_ready"), 1)
            dve.wait_ge(sem("sqrt_ready"), T.next(sem("sqrt_ready")))
            STT(G[:, 0:4, :], G[:, 0:4, :], float(P) ** -0.5, SQ[:, 0:4, :], ALU.mult, ALU.mult)
            TT(G[:, 4:8, :], G[:, 4:8, :], SQ[:, 4:8, :], ALU.mult).then_inc(chain, 1)
            dve.wait_ge(chain, T.next(chain))
            signal("unit_ready")
            dve.wait_ge(sem("er_ready"), T.next(sem("er_ready")))
            dve.wait_ge(sem("ex_ready"), T.next(sem("ex_ready")))
            for t in range(NT):
                TT(view(QD[:, t, :], GH, P), G[:, 0:4, t * P:(t + 1) * P], view(ER[:, t, :], GH, P), ALU.mult)
            TT(BE[:], BT[:], view(EX[:, 0:8], NT, GH), ALU.mult).then_inc(chain, 1)
            dve.wait_ge(chain, T.next(chain))
            for t in range(NT):
                dve.wait_ge(full["v"][t], T.next(full["v"][t]))
                TT(view(KBG[:, t, :], GH, P), view(ps[:, t, :], GH, P), inner(BE[:, t, :], P), ALU.mult)
                TT(view(KD[:, t, :], GH, P), view(ps[:, t, :], GH, P), inner(EX[:, 8 + 4 * t:12 + 4 * t], P), ALU.mult).then_inc(free["v"][t], 1)
                T.add(free["v"][t])
            for t in range(NT):
                dve.wait_ge(full["v"][2 + t], T.next(full["v"][2 + t]))
                TT(view(VB[:, t, :], GH, P), view(ps[:, 2 + t, :], GH, P), inner(BT[:, t, :], P), ALU.mult).then_inc(free["v"][2 + t], 1)
                T.add(free["v"][2 + t])
            settled(2, 3)
            for t in range(NT):
                dve.wait_ge(full["v"][4 + t], T.next(full["v"][4 + t]))
                TT(view(AA[:, t, :], GH, P), view(ps[:, 4 + t, :], GH, P), inner(BT[:, t, :], P), ALU.mult).then_inc(chain, 1)
                dve.wait_ge(chain, T.next(chain))
                TT(AA[:, t, :], AA[:, t, :], DEC[:, t, :], ALU.mult).then_inc(free["v"][4 + t], 1)
                T.add(free["v"][4 + t])
            for t in range(NT):
                dve.wait_ge(full["v"][6 + t], T.next(full["v"][6 + t]))
                TT(QK[:, t, :], ps[:, 6 + t, :], DEC[:, t, :], ALU.mult).then_inc(free["v"][6 + t], 1)
                T.add(free["v"][6 + t])

            def level(name, l):
                return outer(const(name)[:, l * P:(l + 1) * P], GH)

            settled(4, 5, 6, 7)
            dve.wait_ge(sem("at_ready"), T.next(sem("at_ready")))
            for t in range(NT):
                TT(view(TI_[:, t, :], GH, P), view(AA[:, t, :], GH, P), level("lev", 0), ALU.mult)
                TT(view(UI[:, t, :], GH, P), view(AT[:, t, :], GH, P), level("levT", 0), ALU.mult).then_inc(chain, 1)
                dve.wait_ge(chain, T.next(chain))
                TT(view(TI_[:, t, :], GH, P), outer(IDENT, GH), view(TI_[:, t, :], GH, P), ALU.subtract)
                TT(view(UI[:, t, :], GH, P), outer(IDENT, GH), view(UI[:, t, :], GH, P), ALU.subtract).then_inc(chain, 1)
                dve.wait_ge(chain, T.next(chain))
            for lev in range(1, 6):
                for t in range(NT):
                    TT(view(LT[:, t, :], GH, P), view(AT[:, t, :], GH, P), level("levT", lev), ALU.mult).then_inc(sem("lt_ready"), 1)
                for t in range(NT):
                    dve.wait_ge(full["v"][2 + t], T.next(full["v"][2 + t]))
                    TT(TI_[:, t, :], TI_[:, t, :], ps[:, 2 + t, :], ALU.subtract).then_inc(free["v"][2 + t], 1)
                    T.add(free["v"][2 + t])
                    dve.wait_ge(full["v"][4 + t], T.next(full["v"][4 + t]))
                    TT(UI[:, t, :], UI[:, t, :], ps[:, 4 + t, :], ALU.subtract).then_inc(free["v"][4 + t], 1)
                    T.add(free["v"][4 + t])
                settled(2, 3, 4, 5)
            signal("kb_ready")
            for t in range(NT):
                dve.wait_ge(full["v"][t], T.next(full["v"][t]))
                dve.tensor_copy(UU[:, t, :], ps[:, t, :]).then_inc(free["v"][t], 1)
                T.add(free["v"][t])
            settled(0, 1)
            signal("state_ready")
            for c in range(4):
                t, r = c // 2, slice(64 * (c % 2), 64 * (c % 2) + 64)
                dve.wait_ge(full["v"][4], T.next(full["v"][4]))
                TT(VN[r, t, :], UU[r, t, :], ps[r, 4, :], ALU.subtract).then_inc(free["v"][4], 1)
                T.add(free["v"][4])
                dve.wait_ge(full["v"][5], T.next(full["v"][5]))
                dve.tensor_copy(OI[r, t, :], ps[r, 5, :]).then_inc(free["v"][5], 1)
                T.add(free["v"][5])
                TT(view(ST, GH, P), view(ST, GH, P), inner(EX[:, 16 + 4 * c:20 + 4 * c], P), ALU.mult).then_inc(chain, 1)
                dve.wait_ge(chain, T.next(chain))
                dve.wait_ge(full["v"][6], T.next(full["v"][6]))
                TT(ST, ST, ps[:, 6, :], ALU.add).then_inc(free["v"][6], 1)
                T.add(free["v"][6])
                settled(6)
                if c % 2:
                    dve.wait_ge(full["v"][7], T.next(full["v"][7]))
                    TT(OI[:, t, :], OI[:, t, :], ps[:, 7, :], ALU.add).then_inc(free["v"][7], 1)
                    T.add(free["v"][7])
                if c == 0:
                    dve.wait_ge(sem("gt_ready"), T.next(sem("gt_ready")))
                dve.wait_ge(full["v"][c], T.next(full["v"][c]))
                half = slice(c // 2 * 512, c // 2 * 512 + 512)
                TT(MG[:, c % 2, half], ps[:, c, :], GT[0][:, c % 2, half], ALU.mult).then_inc(free["v"][c], 1)
                T.add(free["v"][c])
            settled(7)
            TT(VN[:], OI[:], OI[:], ALU.mult).then_inc(chain, 1)
            dve.wait_ge(chain, T.next(chain))
            dve.tensor_reduce(SS[:, 0:8], VN[:].rearrange("p t (h d) -> p (t h) d", h=GH), AX, ALU.add).then_inc(chain, 1)
            dve.wait_ge(chain, T.next(chain))
            rstd(P, 8)
            for t in range(NT):
                m = TT(view(OI[:, t, :], GH, P), view(OI[:, t, :], GH, P), inner(RS[:, 4 * t:4 * t + 4], P), ALU.mult)
            m.then_inc(chain, 1)
            dve.wait_ge(chain, T.next(chain))
            TT(OI[:], OI[:], V[:, :, 512:], ALU.mult).then_inc(chain, 1)
            dve.wait_ge(chain, T.next(chain))
            signal("og_ready")
            for g in range(2):
                dve.wait_ge(full["v"][g], T.next(full["v"][g]))
                TS(OT[:, 4 + 2 * g:6 + 2 * g, :], view(ps[:, g, :], 2, S), GDNG, None, ALU.mult).then_inc(free["v"][g], 1)
                T.add(free["v"][g])
            dve.wait_ge(sem("gt_ready"), T.next(sem("gt_ready")))
            for c in range(2):
                for t in range(NT):
                    b = 4 + 2 * c + t
                    half = XS[:, t, c * 512:(c + 1) * 512]
                    dve.wait_ge(full["v"][b], T.next(full["v"][b]))
                    TT(half, ps[:, b, :], half, ALU.mult).then_inc(free["v"][b], 1)
                    T.add(free["v"][b])
            settled(*range(8))
            TT(MG[:], MG[:], XS[:], ALU.add).then_inc(chain, 1)
            dve.wait_ge(chain, T.next(chain))
            signal("merged_ready")
            for g in range(4):
                dve.wait_ge(full["v"][g], T.next(full["v"][g]))
                dve.tensor_copy(XT2[:, 2 * g:2 * g + 2, :], view(ps[:, g, :], 2, S)).then_inc(free["v"][g], 1)
                T.add(free["v"][g])
            dve.wait_ge(sem("mem_here"), T.next(sem("mem_here"), 16))
            scaled(MEM, D).then_inc(sem("xs_ready"), 1)
            residual()
            gained(XT2, "mem", KC, (4, 5, 6, 7))
            settled(4, 5, 6, 7)
            scaled(H, D, squared=True).then_inc(sem("xs_ready"), 1)
            values(lambda c, t: 4 + 2 * c + t)
            gained(XT, "cross", KC)

            def cross_scores():
                dve.wait_ge(full["v"][1], T.next(full["v"][1]))
                dve.tensor_copy(LG[:, 0, :], ps[:, 1, :]).then_inc(free["v"][1], 1)
                T.add(free["v"][1])
                settled(1)
                dve.tensor_reduce(SM[:, 0:2], view(LG[:, 0, :], 2, S), AX, ALU.max, negate=True).then_inc(sem("max_ready"), 1)

            def cross_tail():
                dve.wait_ge(sem("probs_ready"), T.next(sem("probs_ready")))
                dve.reciprocal(SM[:, 16:18], SM[:, 8:10]).then_inc(chain, 1)
                dve.wait_ge(chain, T.next(chain))
                dve.wait_ge(full["v"][4], T.next(full["v"][4]))
                for t in range(NT):
                    m = TS(ONX[:, t, :], ps[:, 4, t * XD:(t + 1) * XD], SM[:, 16 + t:17 + t], None, ALU.mult)
                m.then_inc(free["v"][4], 1)
                T.add(free["v"][4])

            with T.loop("cross", 3) as i:
                cross_scores()
                cross_tail()
            cross_scores()
            cross_tail()
            residual(lambda c, t: (6, 2)[c] + t)
            norm("peer")
            dve.wait_ge(sem("rowg_here"), T.next(sem("rowg_here"), 16))
            gained_rows(V).then_inc(chain, 1)
            dve.wait_ge(chain, T.next(chain))
            signal("rowg_used")
            four = [(t, q) for t in range(NT) for q in range(2)]
            def keys():
                dve.wait_ge(full["v"][6], T.next(full["v"][6]))
                dve.tensor_copy(SKT[:], view(ps[:, 6, 0:2 * P], 2, P)).then_inc(free["v"][6], 1)
                T.add(free["v"][6])

            def route(h):
                keys()
                dve.wait_ge(full["v"][7], T.next(full["v"][7]))
                dve.tensor_copy(SC[:], view(ps[:, 7, :], NT, 2, P)).then_inc(free["v"][7], 1)
                T.add(free["v"][7])
                settled(7)

                def bear():
                    spare.append(34 + len(spare) % 24)
                    dve.tensor_copy(SM[:, spare[-1]:spare[-1] + 1], SM[:, 33:34])

                def top16(sets, values_, replaced, vals, idx):
                    bear()
                    for s_ in sets:
                        m = dve.max(vals(s_)[:, 0:8], values_(s_))
                    m.then_inc(chain, 1)
                    dve.wait_ge(chain, T.next(chain))
                    bear()
                    for s_ in sets:
                        dve.max_index(idx(s_)[:, 0:8], vals(s_)[:, 0:8], values_(s_))
                        m = dve.match_replace(replaced(s_), vals(s_)[:, 0:8], values_(s_), -3.0e38)
                    m.then_inc(chain, 1)
                    dve.wait_ge(chain, T.next(chain))
                    bear()
                    for s_ in sets:
                        m = dve.max(vals(s_)[:, 8:16], replaced(s_))
                    m.then_inc(chain, 1)
                    dve.wait_ge(chain, T.next(chain))
                    bear()
                    for s_ in sets:
                        m = dve.max_index(idx(s_)[:, 8:16], vals(s_)[:, 8:16], replaced(s_))
                    m.then_inc(chain, 1)
                    dve.wait_ge(chain, T.next(chain))

                top16(four, lambda s_: SC[:, s_[0], s_[1], :], lambda s_: SCR[:, s_[0], s_[1], :],
                      lambda s_: TV[:, s_[0], s_[1], :], lambda s_: TIX[:, s_[0], s_[1], :])
                dve.tensor_copy(TIF[:], TIX[:])
                for t in range(NT):
                    m = TT(view(CAND[:, t, :], 16, 16), inner(TV[:, t, 0, :], 16), outer(TV[:, t, 1, :], 16), ALU.add)
                m.then_inc(chain, 1)
                dve.wait_ge(chain, T.next(chain))
                top16(range(NT), lambda t: CAND[:, t, :], lambda t: CANDR[:, t, :], lambda t: BV[:, t, :], lambda t: BP[:, t, :])
                dve.tensor_single_scalar(PA[:], BP[:], 4, ALU.logical_shift_right)
                dve.tensor_single_scalar(PB[:], BP[:], 15, ALU.bitwise_and).then_inc(chain, 1)
                dve.wait_ge(chain, T.next(chain))
                dve.tensor_copy(PAF[:], PA[:])
                dve.tensor_copy(PBF[:], PB[:]).then_inc(chain, 1)
                dve.wait_ge(chain, T.next(chain))
                for q, where in ((0, PAF), (1, PBF)):
                    for t in range(NT):
                        m = TT(view(OH[:, t, :], 16, 16), inner(where[:, t, :], 16), outer(const("iota16"), 16), ALU.is_equal)
                    m.then_inc(chain, 1)
                    dve.wait_ge(chain, T.next(chain))
                    for t in range(NT):
                        m = TT(view(OH[:, t, :], 16, 16), view(OH[:, t, :], 16, 16), outer(TIF[:, t, q, :], 16), ALU.mult)
                    m.then_inc(chain, 1)
                    dve.wait_ge(chain, T.next(chain))
                    dve.tensor_reduce(where[:].rearrange("p t k -> p (t k)"), OH[:].rearrange("p t (k b) -> p (t k) b", b=16), AX, ALU.add).then_inc(chain, 1)
                    dve.wait_ge(chain, T.next(chain))
                STT(PAF[:], PAF[:], float(P), PBF[:], ALU.mult, ALU.add).then_inc(chain, 1)
                dve.wait_ge(chain, T.next(chain))
                dve.tensor_copy(EXU[:, :, ds(h * 16, 16)], PAF[:]).then_inc(sem("expert_ready"), 1)
                TT(BSX[:], BV[:], BV[:, :, 0:1].to_broadcast([P, NT, 16]), ALU.subtract).then_inc(sem("best_ready"), 1)

            def dots():
                for t in range(NT):
                    for j in range(RING):
                        dve.wait_ge(gathered[j], T.next(gathered[j], 16))
                        STT(ring(j), ring(j), 1.0, V[:, t, :], ALU.mult, ALU.mult, accum_out=DOT[:, t, j:j + 1]).then_inc(ring_used[j], 1)

            def weigh(h):
                dve.wait_ge(sem("gate_exp"), T.next(sem("gate_exp")))
                dve.tensor_reduce(GS[:, 0:NT], GX[:], AX, ALU.add).then_inc(chain, 1)
                dve.wait_ge(chain, T.next(chain))
                dve.reciprocal(GS[:, 0:NT], GS[:, 0:NT]).then_inc(chain, 1)
                dve.wait_ge(chain, T.next(chain))
                TT(GX[:], GX[:], inner(GS[:, 0:NT], TOPK), ALU.mult).then_inc(chain, 1)
                dve.wait_ge(chain, T.next(chain))
                dve.wait_ge(sem("gelu_ready"), T.next(sem("gelu_ready")))
                TT(AV[:, :, ds(h * TOPK, TOPK)], AX_[:], GX[:], ALU.mult).then_inc(sem("av_ready"), 1)

            def skip_v():
                for j in range(RING):
                    T.add(gathered[j], 16 * NT)

            route(0)
            dots()
            weigh(0)
            route(1)
            with T.loop("peer", PH - 2) as i:
                dots()
                weigh(i + 1)
                skip_v()
                route(i + 2)
            dots()
            weigh(PH - 1)
            dve.wait_ge(sem("av_ready"), T.next(sem("av_ready"), PH))

            def mix_shared(h):
                for t in range(NT):
                    for j in range(RING):
                        if j in SHARED:
                            dve.wait_ge(gathered[j], T.next(gathered[j], 16))
                            if last:
                                dve.wait_ge(ring_used[last[-1]], T.next(ring_used[last[-1]]))
                            last.append(j)
                            weight = AV[:, t, h * TOPK + j:h * TOPK + j + 1]
                            STT(H[:, t, :], ring(j), weight, H[:, t, :], ALU.mult, ALU.add).then_inc(ring_used[j], 1)
                        else:
                            T.add(gathered[j], 16)

            last = []
            for j in SHARED:
                T.add(ring_used[j], 1 + NT * (2 * PH - 2))
            mix_shared(PH - 2)
            mix_shared(PH - 1)
            dve.wait_ge(ring_used[last[-1]], T.next(ring_used[last[-1]]))
            residual(lambda c, t: 2 * t + c)
            root_mean(H, D, squared=True)
            dve.wait_ge(sem("rowg_here"), T.next(sem("rowg_here"), 16))
            gained_rows(XS).then_inc(sem("result"), 1)


PER_ITER = {
    "sp:fox": dict(slot_used0=1, slot_used1=1),
    "sp:ffn0": dict(slot_used0=1, slot_used1=1, slot_used2=1, slot_used3=1),
    "sp:mla": dict(slot_used0=1, slot_used1=1),
    "sp:ffn1": dict(slot_used0=1, slot_used1=1, slot_used2=1, slot_used3=1),
    "sp:sb": dict(slot_used0=1, slot_used1=1),
    "sp:cross": dict(slot_used0=1, slot_used1=1),
    "sp:route": dict(slot_used0=1, slot_used1=1),
    "pe:fox": dict(free_v1=1, free_v2=1, slot_here0=16, slot_here1=16, free_a0=1, probs_ready=2, free_a3=1, free_a4=1,
        free_a2=1, free_v5=1),
    "pe:ffn0": dict(gu_split0=1, free_v4=1, gu_split1=1, free_v5=1, dn_split0=1, dn_split1=1),
    "pe:mla": dict(free_v1=1, free_v2=1, slot_here0=16, free_a0=1, slot_here1=16, free_a6=1, free_v7=1, probs_ready=2,
        free_a3=1, free_a4=1, free_a2=1, free_v5=1),
    "pe:ffn1": dict(gu_split0=1, free_v4=1, gu_split1=1, free_v5=1, dn_split0=1, dn_split1=1),
    "pe:sb": dict(free_v1=1, free_v2=1, slot_here0=16, slot_here1=16, free_a0=1, keep_ready=2, free_v3=1, free_v4=1,
        free_a6=1, probs_ready=2, free_v5=1),
    "pe:cross": dict(free_v1=1, slot_here0=16, free_a0=1, slot_here1=16, free_a6=1, probs_ready=1, free_a3=1, free_a5=1,
        free_v4=1),
    "pe:peer": dict(slot_here0=32, free_a4=1, free_a5=1, slot_here1=16, free_v6=1, free_v7=1, gathered0=64, gathered1=64,
        gathered2=64, gathered3=64, gathered4=64, gathered5=64, gathered6=64, gathered7=64, gathered8=64,
        gathered9=64, gathered10=64, gathered11=64, gathered12=64, gathered13=64, gathered14=64, gathered15=64,
        diag_ready=32),
    "act:fox": dict(max_ready=2, full_a0=1, full_a3=1, full_a4=1, full_a2=1),
    "act:ffn0": dict(full_a4=1, raw_here0=32, full_a5=1, raw_here1=32, raw_here2=16, dn_used0=1, raw_here3=16, dn_used1=1),
    "act:mla": dict(max_ready=2, full_a0=1, full_a6=1, full_a3=1, full_a4=1, full_a2=1),
    "act:ffn1": dict(full_a4=1, raw_here0=32, full_a5=1, raw_here1=32, raw_here2=16, dn_used0=1, raw_here3=16, dn_used1=1),
    "act:sb": dict(absz_ready=2, act_chain=2, full_a0=1, expo_ready=2, full_a6=1),
    "act:cross": dict(max_ready=1, full_a0=1, full_a6=1, full_a3=1, full_a5=1),
    "act:peer": dict(full_a4=1, full_a5=1, ring_used0=4, ring_used1=4, ring_used2=4, ring_used3=4, ring_used4=4, ring_used5=4,
        ring_used6=4, ring_used7=4, ring_used8=4, ring_used9=4, ring_used10=4, ring_used11=4, ring_used12=4,
        ring_used13=4, ring_used14=4, ring_used15=4, av_ready=1, best_ready=1),
    "pool:peer": dict(expert_ready=1, ring_used0=4, ring_used1=4, ring_used2=4, ring_used3=4, pool_chain=16, ring_used4=4,
        ring_used5=4, ring_used6=4, ring_used7=4, ring_used8=4, ring_used9=4, ring_used10=4, ring_used11=4,
        ring_used12=4, ring_used13=4, ring_used14=4, ring_used15=4),
    "dve:fox": dict(full_v1=1, free_v1=1, full_v2=1, free_v2=1, probs_ready=2, dve_chain=1, full_v5=1, free_v5=1),
    "dve:ffn0": dict(silu_ready=2, dve_chain=4, free_v4=1, high_ready=4, free_v5=1),
    "dve:mla": dict(full_v1=1, free_v1=1, full_v2=1, free_v2=1, full_v7=1, dve_chain=2, free_v7=1, probs_ready=2, full_v5=1,
        free_v5=1),
    "dve:ffn1": dict(silu_ready=2, dve_chain=4, free_v4=1, high_ready=4, free_v5=1),
    "dve:sb": dict(full_v1=1, free_v1=1, full_v2=1, free_v2=1, ln_ready=2, dve_chain=2, full_v3=1, free_v3=1, full_v4=1,
        free_v4=1, full_v5=1, free_v5=1),
    "dve:cross": dict(full_v1=1, free_v1=1, probs_ready=1, dve_chain=1, full_v4=1, free_v4=1),
    "dve:peer": dict(gathered0=64, gathered1=64, gathered2=64, gathered3=64, gathered4=64, gathered5=64, gathered6=64,
        gathered7=64, gathered8=64, gathered9=64, gathered10=64, gathered11=64, gathered12=64, gathered13=64,
        gathered14=64, gathered15=64, gate_exp=1, dve_chain=21, gelu_ready=1, full_v6=1, free_v6=1, full_v7=1,
        free_v7=1),
}

_INS = ["x", "positions", "attn_norm", "ffn_norm", "w_gate", "w_up", "w_down", "fox_w_in", "fox_b_f", "fox_w_o", "kv_norm", "w_kv_a",
        "ckv_norm", "w_uk", "w_uv", "mla_w_dq", "cq_norm", "mla_w_uq", "mla_w_o", "final_norm", "mem_2", "g_mix_2", "w_in_2",
        "gdn_conv_2", "gdn_a_log_2", "gdn_dt_bias_2", "gdn_norm_g_2", "w_sb_up_2", "w_gdn_up_2", "w_mix_out_2", "g_cross_2", "g_mem_2",
        "w_cq_2", "w_ckv_2", "w_co_2", "g_peer_2", "w_pq_2", "peer_subkeys_2", "peer_u_2", "peer_v_2", "g_final_2"]


def kernel(**inputs):
    import concourse.bacc as bacc
    from concourse.bass_utils import run_bass_kernel_spmd

    nc = bacc.Bacc("TRN2", target_bir_lowering=False, num_devices=1)
    arrays, aps = {}, {}
    for name in _INS:
        arrays[f"in_{name}"] = np.ascontiguousarray(inputs[name])
    arrays["in_consts"] = constant_table()
    for name, v in arrays.items():
        aps[name[3:]] = nc.dram_tensor(name, v.shape, mybir.dt.from_np(v.dtype), kind="ExternalInput").ap()
    out = nc.dram_tensor("out_0", (1, S, D), F32, kind="ExternalOutput").ap()
    program(nc, aps, out, PER_ITER)
    r = run_bass_kernel_spmd(nc, [arrays], core_ids=[0])
    return r.results[0]["out_0"]
```
